# Optimizing a Trainium2 kernel written in Bass

```python
import math
import jax
import jax.numpy as jnp
from jax import lax
import numpy as np
import jax, jax.numpy as jnp

D_MODEL = 1024
BATCH = 1
SEQ = 256
DEPTH = 2

HEAD_DIM = 64
HGRN_WIDTH = D_MODEL // 4
HGRN_HEADS = HGRN_WIDTH // HEAD_DIM
HGRN_KEY_DIM = HEAD_DIM
HGRN_VAL_DIM = HEAD_DIM
HGRN_KEY_WIDTH = HGRN_HEADS * HGRN_KEY_DIM
HGRN_CHUNK = 64
ATTN_WIDTH = 3 * D_MODEL // 8
ATTN_HEADS = ATTN_WIDTH // HEAD_DIM
DILATED_PAIRS = ((128, 1), (512, 4), (2048, 16))
ATTN_BLOCK = 128
NUM_BUCKETS = 32
MAX_DISTANCE = 2048
SSM_WIDTH = D_MODEL - HGRN_WIDTH - ATTN_WIDTH
SSM_HEADS = SSM_WIDTH // HEAD_DIM
SSM_GROUPS = 2
SSM_STATE = 128
SSM_CONV = 4
SSM_CHUNK = 64
SSM_CONV_CH = SSM_WIDTH + 2 * SSM_GROUPS * SSM_STATE
MIX_WIDTH = HGRN_WIDTH + ATTN_WIDTH + SSM_WIDTH
IN_SIZES = (HGRN_KEY_WIDTH, HGRN_KEY_WIDTH, HGRN_WIDTH, HGRN_WIDTH, ATTN_WIDTH, ATTN_WIDTH, ATTN_WIDTH, SSM_WIDTH, SSM_CONV_CH, SSM_HEADS)
IN_COLS = 2 * HGRN_KEY_WIDTH + 2 * HGRN_WIDTH + 3 * ATTN_WIDTH + SSM_WIDTH + SSM_CONV_CH + SSM_HEADS
PEER_HEADS = 8
PEER_NKEYS = 128
PEER_EXPERTS = PEER_NKEYS * PEER_NKEYS
PEER_DKEY = 128
PEER_HALF = PEER_DKEY // 2
PEER_TOPK = 16
PEER_TOKEN_BLOCK = 128
NORM_EPS = 1e-6


def rms_norm(x, w):
    xf = x.astype(jnp.float32)
    xf = xf * lax.rsqrt(jnp.mean(xf * xf, axis=-1, keepdims=True) + NORM_EPS)
    return (xf * w.astype(jnp.float32)).astype(x.dtype)

def t5_bucket(dist):
    max_exact = NUM_BUCKETS // 2
    d = np.maximum(dist, 1).astype(np.float32)
    large = max_exact + (np.log(d / max_exact) / np.log(MAX_DISTANCE / max_exact) * (NUM_BUCKETS - max_exact)).astype(np.int32)
    large = np.minimum(large, NUM_BUCKETS - 1)
    return np.where(dist < max_exact, dist, large).astype(np.int32)

def hgrn2_mixer(q, f, i, g, lower_bound, norm_w):
    bsz, seq, _ = q.shape
    H, K, V, C = HGRN_HEADS, HGRN_KEY_DIM, HGRN_VAL_DIM, HGRN_CHUNK
    lb = lower_bound.astype(jnp.float32)
    forget = lb + (1.0 - lb) * jax.nn.sigmoid(f.astype(jnp.float32))
    log_f = jnp.log(forget)
    key = 1.0 - forget
    qs = q.astype(jnp.float32) * (K ** -0.5)

    def chunks(t, d):
        return t.reshape(bsz, seq // C, C, H, d).swapaxes(0, 1)

    causal = jnp.asarray(np.tril(np.ones((C, C), dtype=bool)))[None, :, :, None, None]

    def step(state, inp):
        qc, kc, vc, lc = inp
        b = jnp.cumsum(lc, axis=1)
        o = jnp.einsum('bthk,bhkv->bthv', qc * jnp.exp(b), state)
        decay = jnp.exp(jnp.where(causal, b[:, :, None] - b[:, None, :], -jnp.inf))
        a = jnp.einsum('bthk,bshk,btshk->btsh', qc, kc, decay)
        o = o + jnp.einsum('btsh,bshv->bthv', a, vc)
        b_end = b[:, -1]
        state = state * jnp.exp(b_end)[..., None] + jnp.einsum('bshk,bshv->bhkv', kc * jnp.exp(b_end[:, None] - b), vc)
        return state, o

    state0 = jnp.zeros((bsz, H, K, V), jnp.float32)
    _, o = lax.scan(step, state0, (chunks(qs, K), chunks(key, K), chunks(i.astype(jnp.float32), V), chunks(log_f, K)))
    o = o.swapaxes(0, 1).reshape(bsz, seq, H, V)
    o = rms_norm(o, norm_w) * jax.nn.silu(g.astype(jnp.float32).reshape(bsz, seq, H, V))
    return o.reshape(bsz, seq, H * V)

def dilated_branch(q, k, v, rel_bias, window, dil):
    bsz, seq, H, Dh = q.shape
    blk = ATTN_BLOCK
    n_back = window // dil
    L = seq // dil
    nb = -(-L // blk)
    Lp = nb * blk

    def residue(t):
        return t.reshape(bsz, L, dil, H, Dh).transpose(0, 2, 3, 1, 4)

    qb = jnp.pad(residue(q), ((0, 0), (0, 0), (0, 0), (0, Lp - L), (0, 0))).reshape(bsz, dil, H, nb, blk, Dh)

    def key_windows(t):
        tp = jnp.pad(residue(t), ((0, 0), (0, 0), (0, 0), (blk, Lp - L), (0, 0)))
        tb = tp.reshape(bsz, dil, H, nb + 1, blk, Dh)
        return jnp.concatenate([tb[:, :, :, :-1], tb[:, :, :, 1:]], axis=4)

    kw, vw = key_windows(k), key_windows(v)
    qi = np.arange(blk)[:, None]
    kj = np.arange(2 * blk)[None, :]
    delta = qi - kj + blk
    band = (delta >= 0) & (delta <= n_back)
    key_pos = (np.arange(nb)[:, None, None] - 1) * blk + kj[None]
    mask = jnp.asarray(band[None] & (key_pos >= 0))
    bucket = t5_bucket(np.maximum(delta, 0) * dil)
    bias = rel_bias.astype(jnp.float32)[bucket].transpose(2, 0, 1)
    s = jnp.einsum('bghnid,bghnjd->bghnij', qb, kw).astype(jnp.float32) + bias[None, None, :, None]
    s = jnp.where(mask[None, None, None], s, -jnp.inf)
    lse = jax.nn.logsumexp(s, axis=-1)
    p = jnp.exp(s - lse[..., None])
    o = jnp.einsum('bghnij,bghnjd->bghnid', p, vw.astype(jnp.float32))
    o = o.reshape(bsz, dil, H, Lp, Dh)[:, :, :, :L].transpose(0, 3, 1, 2, 4).reshape(bsz, seq, H, Dh)
    lse = lse.reshape(bsz, dil, H, Lp)[..., :L].transpose(0, 3, 1, 2).reshape(bsz, seq, H)
    return o, lse

def dilated_attention_mixer(q, k, v, q_norm_w, k_norm_w, rel_bias):
    bsz, seq, _ = q.shape
    H, Dh = ATTN_HEADS, HEAD_DIM
    q = rms_norm(q.reshape(bsz, seq, H, Dh), q_norm_w) * (Dh ** -0.5)
    k = rms_norm(k.reshape(bsz, seq, H, Dh), k_norm_w)
    v = v.reshape(bsz, seq, H, Dh)
    outs, lses = [], []
    for window, dil in DILATED_PAIRS:
        o, lse = dilated_branch(q, k, v, rel_bias, window, dil)
        outs.append(o)
        lses.append(lse)
    w = jax.nn.softmax(jnp.stack(lses, axis=0), axis=0)
    o = jnp.sum(w[..., None] * jnp.stack(outs, axis=0), axis=0)
    return o.reshape(bsz, seq, H * Dh)

def mamba2_mixer(z, xbc, dt, conv_w, conv_b, dt_bias, a_log, d_skip, norm_w):
    bsz, seq, _ = z.shape
    H, P, G, N, Q = SSM_HEADS, HEAD_DIM, SSM_GROUPS, SSM_STATE, SSM_CHUNK
    R = H // G
    xbc = lax.conv_general_dilated(xbc, conv_w[:, None, :], window_strides=(1,), padding=((SSM_CONV - 1, 0),),
                                   dimension_numbers=('NWC', 'WIO', 'NWC'), feature_group_count=SSM_CONV_CH) + conv_b
    xbc = jax.nn.silu(xbc.astype(jnp.float32))
    xs, bm, cm = jnp.split(xbc, [SSM_WIDTH, SSM_WIDTH + G * N], axis=-1)
    xs = xs.reshape(bsz, seq, H, P)
    bm = bm.reshape(bsz, seq, G, N)
    cm = cm.reshape(bsz, seq, G, N)
    dt = jax.nn.softplus(dt.astype(jnp.float32) + dt_bias.astype(jnp.float32))
    A = -jnp.exp(a_log.astype(jnp.float32))

    def chunks(t):
        return t.reshape((bsz, seq // Q, Q) + t.shape[2:]).swapaxes(0, 1)

    causal = jnp.asarray(np.tril(np.ones((Q, Q), dtype=bool)))[None, :, :, None]

    def step(state, inp):
        xc, dtc, bc, cc = inp
        bh = jnp.repeat(bc, R, axis=2)
        ch = jnp.repeat(cc, R, axis=2)
        cum = jnp.cumsum(dtc * A, axis=1)
        decay = jnp.exp(jnp.where(causal, cum[:, :, None, :] - cum[:, None, :, :], -jnp.inf))
        scores = jnp.einsum('bthn,bshn->btsh', ch, bh) * decay
        y = jnp.einsum('btsh,bshp->bthp', scores, xc * dtc[..., None])
        y = y + jnp.einsum('bthn,bhpn->bthp', ch, state) * jnp.exp(cum)[..., None]
        to_end = jnp.exp(cum[:, -1:] - cum) * dtc
        state = state * jnp.exp(cum[:, -1])[:, :, None, None] + jnp.einsum('bsh,bshn,bshp->bhpn', to_end, bh, xc)
        return state, y

    state0 = jnp.zeros((bsz, H, P, N), jnp.float32)
    _, y = lax.scan(step, state0, (chunks(xs), chunks(dt), chunks(bm), chunks(cm)))
    y = y.swapaxes(0, 1).reshape(bsz, seq, H, P)
    y = y + d_skip.astype(jnp.float32)[:, None] * xs
    y = y.reshape(bsz, seq, SSM_WIDTH) * jax.nn.silu(z.astype(jnp.float32))
    y = rms_norm(y.reshape(bsz, seq, G, SSM_WIDTH // G), norm_w.reshape(G, SSM_WIDTH // G))
    return y.reshape(bsz, seq, SSM_WIDTH)

def peer_ffn(x, w_query, sub_keys, down, up):
    bsz, seq, D = x.shape
    T = bsz * seq
    H, K, TB = PEER_HEADS, PEER_TOPK, PEER_TOKEN_BLOCK
    xt = x.reshape(T, D)
    q = (xt @ w_query).reshape(T, H, 2, PEER_HALF)
    s = jnp.einsum('thcd,cnd->thcn', q, sub_keys).astype(jnp.float32)
    sv, si = lax.top_k(s, K)
    cand_s = (sv[:, :, 0, :, None] + sv[:, :, 1, None, :]).reshape(T, H, K * K)
    cand_i = (si[:, :, 0, :, None] * PEER_NKEYS + si[:, :, 1, None, :]).reshape(T, H, K * K)
    top_s, pos = lax.top_k(cand_s, K)
    idx = jnp.take_along_axis(cand_i, pos, axis=-1)
    gate = jax.nn.softmax(top_s, axis=-1)

    def expert_block(args):
        xb, ib, gb = args
        a = jnp.einsum('thkd,td->thk', down[ib], xb).astype(jnp.float32)
        c = (gb * jax.nn.gelu(a)).astype(up.dtype)
        return jnp.einsum('thk,thkd->td', c, up[ib]).astype(x.dtype)

    nblk = T // TB
    out = lax.map(expert_block, (xt.reshape(nblk, TB, D), idx.reshape(nblk, TB, H, K), gate.reshape(nblk, TB, H, K)))
    return out.reshape(bsz, seq, D)

def hybrid_layer(x, attn_norm_w, w_in, lower_bound, hgrn_norm_w, q_norm_w, k_norm_w, rel_bias,
                 ssm_conv_w, ssm_conv_b, ssm_dt_bias, ssm_a_log, ssm_d, ssm_norm_w, w_out,
                 ffn_norm_w, peer_w_query, peer_sub_keys, peer_down, peer_up):
    u = rms_norm(x, attn_norm_w) @ w_in
    points = [int(p) for p in np.cumsum(IN_SIZES)[:-1]]
    hq, hf, hi, hg, aq, ak, av, sz, sxbc, sdt = jnp.split(u, points, axis=-1)
    mix = jnp.concatenate([
        hgrn2_mixer(hq, hf, hi, hg, lower_bound, hgrn_norm_w).astype(x.dtype),
        dilated_attention_mixer(aq, ak, av, q_norm_w, k_norm_w, rel_bias).astype(x.dtype),
        mamba2_mixer(sz, sxbc, sdt, ssm_conv_w, ssm_conv_b, ssm_dt_bias, ssm_a_log, ssm_d, ssm_norm_w).astype(x.dtype),
    ], axis=-1)
    x = x + (mix @ w_out).astype(x.dtype)
    x = x + peer_ffn(rms_norm(x, ffn_norm_w), peer_w_query, peer_sub_keys, peer_down, peer_up)
    return x

def first_inputs(seed: int = 0) -> dict:
    key = jax.random.key(seed)
    ks = jax.random.split(key, 20)

    def nrm(k, shape, scale):
        return jax.random.normal(k, shape, jnp.float32) * scale

    dt0 = jnp.exp(jax.random.uniform(ks[10], (DEPTH, SSM_HEADS), jnp.float32, math.log(1e-3), math.log(1e-1)))
    return {
        'x': nrm(ks[0], (BATCH, SEQ, D_MODEL), 1.0),
        'attn_norm_w': 1.0 + nrm(ks[1], (DEPTH, D_MODEL), 0.02),
        'w_in': nrm(ks[2], (DEPTH, D_MODEL, IN_COLS), D_MODEL ** -0.5),
        'hgrn_lower_bounds': nrm(ks[3], (DEPTH, HGRN_KEY_WIDTH), 0.5),
        'hgrn_norm_w': 1.0 + nrm(ks[4], (DEPTH, HGRN_VAL_DIM), 0.02),
        'q_norm_w': 1.0 + nrm(ks[5], (DEPTH, HEAD_DIM), 0.02),
        'k_norm_w': 1.0 + nrm(ks[6], (DEPTH, HEAD_DIM), 0.02),
        'rel_bias': nrm(ks[7], (NUM_BUCKETS, ATTN_HEADS), 0.1),
        'ssm_conv_w': nrm(ks[8], (DEPTH, SSM_CONV, SSM_CONV_CH), SSM_CONV ** -0.5),
        'ssm_conv_b': nrm(ks[9], (DEPTH, SSM_CONV_CH), 0.02),
        'ssm_dt_bias': dt0 + jnp.log(-jnp.expm1(-dt0)),
        'ssm_a_log': jnp.log(jax.random.uniform(ks[11], (DEPTH, SSM_HEADS), jnp.float32, 1.0, 16.0)),
        'ssm_d': 1.0 + nrm(ks[12], (DEPTH, SSM_HEADS), 0.02),
        'ssm_norm_w': 1.0 + nrm(ks[13], (DEPTH, SSM_WIDTH), 0.02),
        'w_out': nrm(ks[14], (DEPTH, MIX_WIDTH, D_MODEL), MIX_WIDTH ** -0.5),
        'ffn_norm_w': 1.0 + nrm(ks[15], (DEPTH, D_MODEL), 0.02),
        'peer_w_query': nrm(ks[16], (DEPTH, D_MODEL, PEER_HEADS * PEER_DKEY), D_MODEL ** -0.5),
        'peer_sub_keys': nrm(ks[17], (DEPTH, 2, PEER_NKEYS, PEER_HALF), PEER_HALF ** -0.5),
        'peer_down': nrm(ks[18], (DEPTH, PEER_EXPERTS, D_MODEL), D_MODEL ** -0.5),
        'peer_up': nrm(ks[19], (DEPTH, PEER_EXPERTS, D_MODEL), D_MODEL ** -0.5),
    }

def first_block(x, attn_norm_w, w_in, hgrn_lower_bounds, hgrn_norm_w, q_norm_w, k_norm_w, rel_bias,
              ssm_conv_w, ssm_conv_b, ssm_dt_bias, ssm_a_log, ssm_d, ssm_norm_w, w_out,
              ffn_norm_w, peer_w_query, peer_sub_keys, peer_down, peer_up):
    lb = jnp.cumsum(jax.nn.softmax(hgrn_lower_bounds.astype(jnp.float32), axis=0), axis=0)
    lb = lb - lb[0]
    for l in range(DEPTH):
        x = hybrid_layer(x, attn_norm_w[l], w_in[l], lb[l], hgrn_norm_w[l], q_norm_w[l], k_norm_w[l], rel_bias,
                         ssm_conv_w[l], ssm_conv_b[l], ssm_dt_bias[l], ssm_a_log[l], ssm_d[l], ssm_norm_w[l], w_out[l],
                         ffn_norm_w[l], peer_w_query[l], peer_sub_keys[l], peer_down[l], peer_up[l])
    return x


MEM_LEN = 256
CONV_WIDTH = 256
CONV_K = 3
RET_HEADS = 4
RET_QK_DIM = 64
RET_V_DIM = 128
RET_CHUNK = 128
RET_QK = RET_HEADS * RET_QK_DIM
RET_V = RET_HEADS * RET_V_DIM
ROPE_BASE = 10000.0
SG_GROUPS = 4
SG_GROUP_DIM = 64
SG_WIDTH = SG_GROUPS * SG_GROUP_DIM
SG_CHUNK = 128
N_BRANCH = 3
XA_HEADS = 4
XA_HEAD_DIM = D_MODEL // XA_HEADS
D_FF = -(-8 * D_MODEL // (3 * 256)) * 256
EPS = 1e-6

IN_WIDTHS = (CONV_WIDTH, CONV_WIDTH, CONV_WIDTH,
             RET_QK, RET_QK, RET_V, RET_V,
             2 * SG_WIDTH,
             N_BRANCH * D_MODEL)
IN_COLS_2 = int(sum(IN_WIDTHS))
IN_SPLITS = [int(s) for s in np.cumsum(IN_WIDTHS)[:-1]]


def rmsnorm(x, g):
    xf = x.astype(jnp.float32)
    y = xf * lax.rsqrt(jnp.mean(xf * xf, axis=-1, keepdims=True) + EPS)
    return (y * g.astype(jnp.float32)).astype(x.dtype)

def layernorm(x, g):
    xf = x.astype(jnp.float32)
    mu = jnp.mean(xf, axis=-1, keepdims=True)
    var = jnp.mean(jnp.square(xf - mu), axis=-1, keepdims=True)
    return ((xf - mu) * lax.rsqrt(var + EPS) * g.astype(jnp.float32)).astype(x.dtype)

def short_conv_mixer(a_x, a_c, a_b, conv_w):
    z = a_c * a_x
    S = z.shape[1]
    zp = jnp.pad(z, ((0, 0), (CONV_K - 1, 0), (0, 0)))
    y = sum(conv_w[k] * zp[:, k:k + S] for k in range(CONV_K))
    return a_b * y

def rotary(x):
    S, Dh = x.shape[1], x.shape[-1]
    half = Dh // 2
    inv = ROPE_BASE ** (-jnp.arange(half, dtype=jnp.float32) / half)
    ang = jnp.arange(S, dtype=jnp.float32)[:, None] * inv[None, :]
    cos = jnp.cos(ang)[None, :, None, :]
    sin = jnp.sin(ang)[None, :, None, :]
    xf = x.astype(jnp.float32)
    x1, x2 = xf[..., :half], xf[..., half:]
    return jnp.concatenate([x1 * cos - x2 * sin, x1 * sin + x2 * cos], axis=-1)

def retention(q, k, v, gn_gain):
    B, S, H, dk = q.shape
    dv = v.shape[-1]
    C = RET_CHUNK
    N = S // C
    out_dtype = v.dtype
    gamma = 1.0 - jnp.exp2(-5.0 - jnp.arange(H, dtype=jnp.float32))
    log_g = jnp.log(gamma)
    q = q.reshape(B, N, C, H, dk)
    k = k.reshape(B, N, C, H, dk) * (dk ** -0.5)
    v = v.astype(jnp.float32).reshape(B, N, C, H, dv)
    idx = jnp.arange(C, dtype=jnp.float32)
    diff = idx[:, None] - idx[None, :]
    decay = jnp.where(diff >= 0, jnp.exp(log_g[:, None, None] * jnp.maximum(diff, 0.0)), 0.0)
    scores = jnp.einsum('bnchd,bnmhd->bnhcm', q, k) * decay[None, None]
    inner = jnp.einsum('bnhcm,bnmhe->bnche', scores, v)
    zeta = jnp.exp(log_g[:, None] * (C - 1 - idx)[None, :])
    kv = jnp.einsum('bnmhd,bnmhe->nbhde', k, v * zeta.T[None, None, :, :, None])
    chunk_decay = jnp.exp(log_g * C)[None, :, None, None]

    def step(R, kv_n):
        return chunk_decay * R + kv_n, R

    _, R_prev = lax.scan(step, jnp.zeros((B, H, dk, dv), jnp.float32), kv)
    xi = jnp.exp(log_g[:, None] * (idx + 1.0)[None, :])
    cross = jnp.einsum('bnchd,nbhde->bnche', q, R_prev) * xi.T[None, None, :, :, None]
    o = (inner + cross).reshape(B, S, H, dv)
    mu = jnp.mean(o, axis=-1, keepdims=True)
    var = jnp.mean(jnp.square(o - mu), axis=-1, keepdims=True)
    o = ((o - mu) * lax.rsqrt(var + EPS)).reshape(B, S, H * dv) * gn_gain.astype(jnp.float32)
    return o.astype(out_dtype)

def spatial_gating(z, ln_g, w_s, b_s):
    B, S, _ = z.shape
    C = SG_CHUNK
    N = S // C
    u, v = jnp.split(z, 2, axis=-1)
    v = layernorm(v, ln_g).reshape(B, N, C, SG_GROUPS, SG_GROUP_DIM)
    mask = jnp.tril(jnp.ones((C, C), dtype=w_s.dtype))
    vm = jnp.einsum('gcm,bnmgd->bncgd', w_s * mask[None], v) + b_s.T[None, None, :, :, None]
    return u * vm.reshape(B, S, SG_WIDTH)

def cross_attention(h, mm, wq, wk, wv, wo):
    B, S, _ = h.shape
    M = mm.shape[1]
    q = (h @ wq).reshape(B, S, XA_HEADS, XA_HEAD_DIM)
    k = (mm @ wk).reshape(B, M, XA_HEADS, XA_HEAD_DIM)
    v = (mm @ wv).reshape(B, M, XA_HEADS, XA_HEAD_DIM)
    s = jnp.einsum('bshd,bmhd->bhsm', q, k).astype(jnp.float32) * (XA_HEAD_DIM ** -0.5)
    p = jax.nn.softmax(s, axis=-1).astype(v.dtype)
    o = jnp.einsum('bhsm,bmhd->bshd', p, v).reshape(B, S, D_MODEL)
    return o @ wo

def second_inputs(seed: int = 0) -> dict:
    key = jax.random.key(seed)
    ks = jax.random.split(key, 32)
    L = DEPTH
    f32 = jnp.float32

    def w(k, shape, fan_in):
        return jax.random.normal(k, shape, f32) * (fan_in ** -0.5)

    def gain(k, shape):
        return 1.0 + 0.02 * jax.random.normal(k, shape, f32)

    return {
        "x": jax.random.normal(ks[0], (BATCH, SEQ, D_MODEL), f32),
        "mem": jax.random.normal(ks[1], (BATCH, MEM_LEN, D_MODEL), f32),
        "norm_mix": gain(ks[2], (L, D_MODEL)),
        "w_in": w(ks[3], (L, D_MODEL, IN_COLS_2), D_MODEL),
        "conv_w": 0.5 * jax.random.normal(ks[4], (L, CONV_K, CONV_WIDTH), f32),
        "w_a_out": w(ks[5], (L, CONV_WIDTH, D_MODEL), CONV_WIDTH),
        "ret_gn": gain(ks[6], (L, RET_V)),
        "w_b_out": w(ks[7], (L, RET_V, D_MODEL), RET_V),
        "sg_ln": gain(ks[8], (L, SG_WIDTH)),
        "sg_w": w(ks[9], (L, SG_GROUPS, SG_CHUNK, SG_CHUNK), SG_CHUNK),
        "sg_b": 1.0 + 0.1 * jax.random.normal(ks[10], (L, SG_GROUPS, SG_CHUNK), f32),
        "w_c_out": w(ks[11], (L, SG_WIDTH, D_MODEL), SG_WIDTH),
        "w_o": w(ks[12], (L, D_MODEL, D_MODEL), D_MODEL),
        "norm_xa": gain(ks[13], (L, D_MODEL)),
        "norm_mem": gain(ks[14], (L, D_MODEL)),
        "xa_q": w(ks[15], (L, D_MODEL, D_MODEL), D_MODEL),
        "xa_k": w(ks[16], (L, D_MODEL, D_MODEL), D_MODEL),
        "xa_v": w(ks[17], (L, D_MODEL, D_MODEL), D_MODEL),
        "xa_o": w(ks[18], (L, D_MODEL, D_MODEL), D_MODEL),
        "norm_ffn": gain(ks[19], (L, D_MODEL)),
        "w1": w(ks[20], (L, D_MODEL, D_FF), D_MODEL),
        "w3": w(ks[21], (L, D_MODEL, D_FF), D_MODEL),
        "w2": w(ks[22], (L, D_FF, D_MODEL), D_FF),
        "final_norm": gain(ks[23], (D_MODEL,)),
    }

def second_block(x, mem, norm_mix, w_in, conv_w, w_a_out, ret_gn, w_b_out, sg_ln, sg_w, sg_b,
              w_c_out, w_o, norm_xa, norm_mem, xa_q, xa_k, xa_v, xa_o, norm_ffn, w1, w3, w2,
              final_norm):
    B, S, _ = x.shape
    for l in range(DEPTH):
        h = rmsnorm(x, norm_mix[l])
        p = h @ w_in[l]
        a_x, a_c, a_b, q, k, v, g, z, gates = jnp.split(p, IN_SPLITS, axis=-1)
        y_a = short_conv_mixer(a_x, a_c, a_b, conv_w[l]) @ w_a_out[l]
        qr = rotary(q.reshape(B, S, RET_HEADS, RET_QK_DIM))
        kr = rotary(k.reshape(B, S, RET_HEADS, RET_QK_DIM))
        r = retention(qr, kr, v.reshape(B, S, RET_HEADS, RET_V_DIM), ret_gn[l])
        y_b = (jax.nn.silu(g) * r) @ w_b_out[l]
        y_c = spatial_gating(jax.nn.gelu(z), sg_ln[l], sg_w[l], sg_b[l]) @ w_c_out[l]
        g_a, g_b, g_c = jnp.split(jax.nn.sigmoid(gates), N_BRANCH, axis=-1)
        merged = g_a * y_a + g_b * y_b + g_c * y_c
        x = x + merged @ w_o[l]
        h = rmsnorm(x, norm_xa[l])
        mm = rmsnorm(mem, norm_mem[l])
        x = x + cross_attention(h, mm, xa_q[l], xa_k[l], xa_v[l], xa_o[l])
        h = rmsnorm(x, norm_ffn[l])
        x = x + (jax.nn.silu(h @ w1[l]) * (h @ w3[l])) @ w2[l]
    return rmsnorm(x, final_norm)


def setup_inputs(seed=0):
    out = dict(first_inputs(seed))
    for name, value in second_inputs(seed + 1).items():
        if name != "x":
            out[name + "_2"] = value
    return out


def reference(
    x, attn_norm_w, w_in, hgrn_lower_bounds, hgrn_norm_w, q_norm_w, k_norm_w, rel_bias,
    ssm_conv_w, ssm_conv_b, ssm_dt_bias, ssm_a_log, ssm_d, ssm_norm_w, w_out, ffn_norm_w,
    peer_w_query, peer_sub_keys, peer_down, peer_up, mem_2, norm_mix_2, w_in_2, conv_w_2,
    w_a_out_2, ret_gn_2, w_b_out_2, sg_ln_2, sg_w_2, sg_b_2, w_c_out_2, w_o_2, norm_xa_2,
    norm_mem_2, xa_q_2, xa_k_2, xa_v_2, xa_o_2, norm_ffn_2, w1_2, w3_2, w2_2, final_norm_2,
):
    x = first_block(
        x, attn_norm_w, w_in, hgrn_lower_bounds, hgrn_norm_w, q_norm_w, k_norm_w, rel_bias,
        ssm_conv_w, ssm_conv_b, ssm_dt_bias, ssm_a_log, ssm_d, ssm_norm_w, w_out, ffn_norm_w,
        peer_w_query, peer_sub_keys, peer_down, peer_up,
    )
    return second_block(
        x, mem_2, norm_mix_2, w_in_2, conv_w_2, w_a_out_2, ret_gn_2, w_b_out_2, sg_ln_2, sg_w_2,
        sg_b_2, w_c_out_2, w_o_2, norm_xa_2, norm_mem_2, xa_q_2, xa_k_2, xa_v_2, xa_o_2,
        norm_ffn_2, w1_2, w3_2, w2_2, final_norm_2,
    )


_drawn_inputs = setup_inputs


def setup_inputs(seed=0):
    import zlib

    import numpy as np

    out = dict(_drawn_inputs(seed))
    spreads = {}
    factors = {'hgrn_norm_w': 5.056,
     'q_norm_w': 8.0,
     'k_norm_w': 8.0,
     'rel_bias': 2.783,
     'ssm_d': 4.402,
     'ffn_norm_w': 8.0,
     'ret_gn_2': 8.0,
     'sg_ln_2': 8.0,
     'norm_xa_2': 8.0,
     'norm_mem_2': 8.0,
     'norm_ffn_2': 3.745,
     'final_norm_2': 2.852}
    for name, (base, spread) in spreads.items():
        noise = np.random.default_rng([zlib.crc32(name.encode()), seed]).standard_normal(out[name].shape)
        drawn = base * np.exp(spread * noise) if base else spread * noise
        out[name] = jnp.asarray(drawn.astype(out[name].dtype))
    for name, factor in factors.items():
        out[name] = (out[name] * factor).astype(out[name].dtype)
    return out
```

```python
from collections import defaultdict
from contextlib import ExitStack, contextmanager

import numpy as np

import concourse.bass as bass
from concourse import mybir

ALU = mybir.AluOpType
ACT = mybir.ActivationFunctionType
AX = mybir.AxisListType
F32 = mybir.dt.float32
U32 = mybir.dt.uint32

P = 128
T = 256
D = 1024
TT = T // P
KD = D // P
DEPTH = 2
EPS = 1e-6
NEG = -1e30
BIG = 3e38

HEAD = 64
HG_HEADS, AT_HEADS, SS_HEADS = 4, 6, 6
HG_W, AT_W, SS_W = HG_HEADS * HEAD, AT_HEADS * HEAD, SS_HEADS * HEAD
GROUPS = 2
CONV_CH = SS_W + 2 * GROUPS * 128
CONV_TILES = CONV_CH // P
IN1 = 4 * HG_W + 3 * AT_W + SS_W + CONV_CH + SS_HEADS
BUCKETS, MAX_DISTANCE = 32, 2048
REL = T + P - 1
NKEYS, TOPK, PEER_HEADS = 128, 16, 8
HC = PEER_HEADS * 2
VGROUP = 4
IN2 = 3 * 256 + 2 * 256 + 2 * 512 + 512 + 3 * D
RET_HEADS, RET_V = 4, 128
D_FF = 2816
KF = D_FF // P

HYBRID_BLOCKS = [
    ("w_in", 0, KD, 0, 512), ("w_in", 0, KD, 512, 256), ("w_in", 0, KD, 768, 512), ("w_in", 0, KD, 1280, 512),
    ("w_in", 0, KD, 1792, 512), ("w_in", 0, KD, 2304, 256), ("w_in", 0, KD, 2560, 512), ("w_in", 0, KD, 3072, 390),
    ("w_out", 0, KD, 0, 512), ("w_out", 0, KD, 512, 512),
    ("peer_w_query", 0, KD, 0, 512), ("peer_w_query", 0, KD, 512, 512),
]
SECOND_BLOCKS = (
    [("xa_k_2", 0, KD, 0, 512), ("xa_k_2", 0, KD, 512, 512), ("xa_v_2", 0, KD, 0, 512), ("xa_v_2", 0, KD, 512, 512)]
    + [("w_in_2", 0, KD, 0, 512), ("w_in_2", 0, KD, 512, 256)]
    + [("w_in_2", 0, KD, 768 + 512 * n, 512) for n in range(10)]
    + [("w_a_out_2", 0, 2, 0, D), ("w_b_out_2", 0, 4, 0, D), ("w_c_out_2", 0, 2, 0, D)]
    + [("w_o_2", 0, KD, 0, 512), ("w_o_2", 0, KD, 512, 512)]
    + [("xa_q_2", 0, KD, 0, 512), ("xa_q_2", 0, KD, 512, 512), ("xa_o_2", 0, KD, 0, 512), ("xa_o_2", 0, KD, 512, 512)]
    + [("w1w3", 0, KD, 256 * n, 256) for n in range(D_FF // 256)]
    + [("w2_2", 4 * n, min(4, KF - 4 * n), 0, D) for n in range(-(-KF // 4))]
)
COLUMNS = {"w_in": IN1, "w_out": D, "peer_w_query": D, "w_in_2": IN2, "w_a_out_2": D, "w_b_out_2": D, "w_c_out_2": D,
           "w_o_2": D, "xa_q_2": D, "xa_k_2": D, "xa_v_2": D, "xa_o_2": D, "w1_2": D_FF, "w3_2": D_FF, "w2_2": D}
ROWS = {"w_a_out_2": 256, "w_b_out_2": 512, "w_c_out_2": 256, "w2_2": D_FF}

HYBRID_PARAMS = {}
for _name, _n in [("attn_norm", KD), ("ffn_norm", KD), ("mix_norm", KD), ("q_norm", 1), ("k_norm", 1),
                  ("conv_w", 4 * CONV_TILES), ("conv_b", CONV_TILES), ("dt_bias", 1), ("a_log", 1), ("d_skip", SS_HEADS)]:
    HYBRID_PARAMS[_name] = (sum(n for _, n in HYBRID_PARAMS.values()), _n)
N_HYBRID = sum(n for _, n in HYBRID_PARAMS.values())
SECOND_PARAMS = {}
for _name, _n in [("norm_mix", KD), ("norm_xa", KD), ("norm_mem", KD), ("norm_ffn", KD), ("ret_gn", 4),
                  ("conv_w", 6), ("sg_b", 4), ("sg_ln", 256), ("sg_w", 512)]:
    SECOND_PARAMS[_name] = (sum(n for _, n in SECOND_PARAMS.values()), _n)
N_SECOND = sum(n for _, n in SECOND_PARAMS.values())
N_COMMON = 3 * P + 16 + 2
N_HYBRID_CONST = 2 * (T + P) + REL
N_SECOND_CONST = 4 * (T + P) + 2 * TT * 32 + P
N_PHASE_CONST = max(N_HYBRID_CONST, N_SECOND_CONST)


class Steps:

    def __init__(self, before=None):
        self.known = before
        self.marks, self.per, self.turns, self.semaphores = {}, {}, {}, {}


class Program:

    def __init__(self, engine, own_name, steps):
        self.e, self.own_name, self.steps = engine, own_name, steps
        self.path, self.counts = [], defaultdict(int)

    def count(self, name=None, stream=None):
        counted = stream or self.own_name
        self.counts[counted] += 1
        if name:
            assert name not in self.steps.marks, name
            self.steps.marks[name] = (counted, [(loop, base[counted]) for loop, _, base in self.path],
                                      self.counts[counted])
        return self.steps.semaphores[counted], 16 if stream else 1

    @contextmanager
    def loop(self, name, turns):
        base = self.counts
        self.steps.turns[name] = turns
        with self.e.Fori(0, turns) as i:
            self.path.append((name, i, base))
            self.counts = defaultdict(int)
            yield i
        for counted, n in self.counts.items():
            self.steps.per[name, counted] = n
            base[counted] += turns * n
        self.path.pop()
        self.counts = base

    def value(self, counted, loops, value, back=0):
        known = self.steps.known
        semaphore = self.steps.semaphores[counted]
        if known is None:
            return semaphore, 1
        mine = {name: i for name, i, _ in self.path}
        shared = [loop for loop, _ in loops if loop in mine]
        moving = []
        for loop, base in loops:
            per = known.per[loop, counted]
            value += base
            if loop in mine:
                moving.append((mine[loop], per))
            else:
                value += (known.turns[loop] - 1) * per
            if back and loop == shared[-1]:
                value -= back * per
        assert value > 0, (counted, loops, value)
        unit = 16 if counted.startswith("dma") else 1
        total = value * unit
        for i, per in moving:
            total = i * (per * unit) + total
        return semaphore, total

    def at(self, name, back=0):
        if self.steps.known is None:
            return self.steps.semaphores["dma_start"], 1
        return self.value(*self.steps.known.marks[name], back)

    def mine(self, lag=0):
        loops = [(loop, base[self.own_name]) for loop, _, base in self.path]
        return self.value(self.own_name, loops, self.counts[self.own_name] - lag)


def constants():
    p = np.arange(P)[:, None]
    common = np.zeros((P, N_COMMON), np.float32)
    common[:, 0:P] = np.eye(P)
    common[:, P:2 * P] = np.eye(P)[::-1]
    common[:, 2 * P:3 * P] = np.arange(P)[None]
    common[:, 3 * P:3 * P + 16] = np.arange(16)[None]
    common[:, 3 * P + 16] = np.arange(P) < 64
    common[:, 3 * P + 17] = np.arange(P) >= 64

    def times(delta):
        n = (delta <= 128).astype(int) + (delta % 4 == 0) + (delta % 16 == 0)
        n = np.where(delta >= 0, n, 0)
        return np.where(n > 0, np.log(np.maximum(n, 1)), NEG).astype(np.float32)

    hybrid = np.zeros((P, N_HYBRID_CONST), np.float32)
    s = np.arange(T)[None]
    hybrid[:, 0:T] = times(P + p - s)
    hybrid[:, T:T + P] = times(p - s[:, :P])
    hybrid[:, T + P:2 * T + P] = np.where(s >= p, 0, NEG)
    hybrid[:, 2 * T + P:2 * (T + P)] = np.where(s[:, :P] >= p, 0, NEG)
    dist = np.maximum(T - 1 - np.arange(REL), 0)
    exact = BUCKETS // 2
    d = np.maximum(dist, 1).astype(np.float32)
    large = exact + (np.log(d / exact) / np.log(MAX_DISTANCE / exact) * (BUCKETS - exact)).astype(np.int32)
    bucket = np.where(dist < exact, dist, np.minimum(large, BUCKETS - 1))
    hybrid[0:BUCKETS, 2 * (T + P):] = np.arange(BUCKETS)[:, None] == bucket[None]

    second = np.zeros((P, N_SECOND_CONST), np.float32)
    gamma = 1.0 - np.exp2(-5.0 - np.arange(RET_HEADS))
    for h in range(RET_HEADS):
        at = h * (T + P)
        full = np.where(s >= p, np.exp(np.log(gamma[h]) * np.maximum(s - p, 0)), 0) * 64 ** -0.5
        second[:, at:at + T] = full
        second[:, at + T:at + T + P] = full[:, :P]
    at = 4 * (T + P)
    inv = np.float32(10000.0) ** (-np.arange(32, dtype=np.float32) / np.float32(32))
    angle = (np.arange(T, dtype=np.float32)[:, None] * inv[None].astype(np.float32)).reshape(TT, P, 32)
    second[:, at:at + 64] = np.cos(angle).transpose(1, 0, 2).reshape(P, 64)
    second[:, at + 64:at + 128] = np.sin(angle).transpose(1, 0, 2).reshape(P, 64)
    second[:, at + 128:] = s[:, :P] >= p
    return {"common": common, "hybrid_const": hybrid, "second_const": second}


def build(nc, dram, out, steps):
    ctx = ExitStack()
    with ctx:
        def sb(name, shape, dt=F32):
            return ctx.enter_context(nc.sbuf_tensor(name, shape, dt))

        for name in ("vector", "scalar", "tensor", "pool", "dma_w0", "dma_w1", "dma_down0", "dma_down1", "dma_up0",
                     "dma_up1", "dma_start", "dma_const", "dma_params", "dma_bias_out", "dma_bias_in", "dma_hi_out",
                     "dma_hi_in0", "dma_hi_in1", "dma_out"):
            steps.semaphores[name] = ctx.enter_context(nc.semaphore(name))

        X = sb("x_res", [P, TT, D])
        HT = sb("h_t", [P, KD, T])
        RING = sb("ring", [P, 2, 4096])
        ARENA = sb("arena", [P, 32768])
        COMMON = sb("common_sb", [P, N_COMMON])
        PHASE = sb("phase_sb", [P, N_PHASE_CONST])
        HPAR = sb("hybrid_params", [P, N_HYBRID])
        LB = sb("lower", [P, 16])
        STAT = sb("stat", [P, 128])
        HK = sb("hk_t", [P, 3, T])
        ONE = sb("one_hot", [P, 2, 2, 4, P])
        KEYS = sb("keys", [P, P])
        PS = ctx.enter_context(nc.psum_tensor("ps", [P, 8, 512], F32))
        IDENT, FLIP = COMMON[:, 0:P], COMMON[:, P:2 * P]
        IOTA, IOTA16 = COMMON[:, 2 * P:3 * P], COMMON[:, 3 * P:3 * P + 16]
        HALVES = COMMON[:, 3 * P + 16:3 * P + 18]
        bias_rows = nc.dram_tensor("bias_rows", [AT_HEADS, REL], F32, kind="Internal").ap()
        hi_rows = nc.dram_tensor("hi_rows", [HG_W, T], F32, kind="Internal").ap()

        def carve(start, *sizes):
            pieces = []
            for n in sizes:
                pieces.append(ARENA[:, start:start + n])
                start += n
            assert start <= 32768, start
            return pieces, start

        def split(ap, pattern, **sizes):
            return ap.rearrange(pattern, **sizes)

        (SCR_,), after_scr = carve(0, TT * D)
        SCR = split(SCR_, "p (t d) -> p t d", t=TT)
        (HQ, FS, HI, KEY, FR_, U, XB, XC), scan_at = carve(
            after_scr, 2 * T, 2 * T, 2 * T, 2 * T, 2 * VGROUP * T, TT * 1792, CONV_TILES * (T + 3), CONV_TILES * T)
        HQ, FS, HI, KEY = (split(a, "p (c t) -> p c t", c=2) for a in (HQ, FS, HI, KEY))
        FR = split(FR_, "p (c v t) -> p c v t", c=2, v=VGROUP)
        QKN = split(FR_[:, 0:TT * 768], "p (t n) -> p t n", t=TT)
        U = split(U, "p (t n) -> p t n", t=TT)
        XB, XC = (split(a, "p (c t) -> p c t", c=CONV_TILES) for a in (XB, XC))
        scan_buffers, mix_at = carve(scan_at, *[2 * VGROUP * T] * 4)
        VB, KV, ST, QS = (split(a, "p (b v t) -> p b v t", b=2, v=VGROUP) for a in scan_buffers)
        (SCORE, PT, XDT, XSK, SZ), end = carve(scan_at, AT_HEADS * (T + P), AT_HEADS * 3 * P, *[TT * SS_W] * 3)
        assert end <= mix_at
        PT = split(PT, "p (h k t) -> p h k t", h=AT_HEADS, k=3)
        XDT, XSK, SZ = (split(a, "p (t n) -> p t n", t=TT) for a in (XDT, XSK, SZ))
        (MIX, BIAS, DT, DC, CD, HANK, QKT), _ = carve(mix_at, TT * D, AT_HEADS * (T + P), 6 * T, T, TT * 64,
                                                      AT_HEADS * T, 6 * T)
        MIX = split(MIX, "p (t d) -> p t d", t=TT)
        DT = split(DT, "p (k t) -> p k t", k=6)
        CD = split(CD, "p (t n) -> p t n", t=TT)
        HANK = split(HANK, "p (h i) -> p h i", h=AT_HEADS)
        QKT = split(QKT, "p (c t) -> p c t", c=6)
        SCORE1, BIAS1 = (split(a[:, 0:AT_HEADS * T], "p (h s) -> p h s", h=AT_HEADS) for a in (SCORE, BIAS))
        SCORE0, BIAS0 = (split(a[:, AT_HEADS * T:], "p (h s) -> p h s", h=AT_HEADS) for a in (SCORE, BIAS))
        DEC = split(SCORE, "p (h s) -> p h s", h=SS_HEADS)
        (PQ, SC, SC2, CAND, CAND2, EQ, TOPV, TOPI, TOPF, BESTV, BESTI, KI, KF_, HKR, OFF), _ = carve(
            after_scr, PEER_HEADS * T, TT * HC * P, HC * P, *[PEER_HEADS * 256] * 3, *[HC * TOPK] * 3, P, P,
            2 * P, 2 * P, 3 * P, P)
        PQ = split(PQ, "p (h t) -> p h t", h=PEER_HEADS)
        SC = split(SC, "p (t c n) -> p t c n", t=TT, c=HC)
        SC2 = split(SC2, "p (c n) -> p c n", c=HC)
        CAND, CAND2 = (split(a, "p (h n) -> p h n", h=PEER_HEADS) for a in (CAND, CAND2))
        TOPV, TOPF = (split(a, "p (c k) -> p c k", c=HC) for a in (TOPV, TOPF))
        TOPI = split(TOPI.bitcast(U32), "p (c k) -> p c k", c=HC)
        BESTV = split(BESTV, "p (h k) -> p h k", h=PEER_HEADS)
        BESTI = BESTI.bitcast(U32)
        KI = split(KI.bitcast(U32), "p (c n) -> p c n", c=2)
        KF_ = split(KF_, "p (c n) -> p c n", c=2)
        HKR = split(HKR, "p (c n) -> p c n", c=3)
        G = split(ARENA[:, :], "p (t n) -> p t n", t=T)
        GELU = ONE[:, 0, :, :, :].rearrange("p b j n -> p b (j n)")
        COEF = ONE[:, 1, :, :, :].rearrange("p b j n -> p b (j n)")
        (SPAR, MEMX, MT, MK, MV, ABC, Z3, YA, QKVG, ZG, GT, MER, QKR, QKT2, DM, R, RT), _ = carve(
            after_scr, N_SECOND + N_SECOND % 2, TT * D, KD * T, KD * T, TT * D, 4 * T, 2 * (T + 2), 2 * T, TT * 1536,
            TT * 512, TT * 3 * D, TT * D, TT * 512, 4 * T, 4 * (T + P), TT * 512, 4 * T)
        flat = ONE.ap().rearrange("p a b j n -> p (a b j n)")
        WSM, VN, YC, YCT = (flat[:, n * 512:(n + 1) * 512] for n in range(4))
        MEMX, MV, MER = (split(a, "p (t n) -> p t n", t=TT) for a in (MEMX, MV, MER))
        QX_, SX_, PTX_, FF_, SILU = QKVG[:, 0:KD * T], None, None, GT[:, 0:KF * T], QKVG[:, 2 * D:2 * D + 1024]
        SX_, PTX_ = GT[:, 0:TT * 4 * T], GT[:, TT * 4 * T:2 * TT * 4 * T]
        FINAL = MT[:, 0:D]
        MT, MK = (split(a, "p (k t) -> p k t", k=KD) for a in (MT, MK))
        ABC = split(ABC, "p (c t) -> p c t", c=4)
        Z3 = split(Z3, "p (c t) -> p c t", c=2)
        YA, YCT = (split(a, "p (c t) -> p c t", c=2) for a in (YA, YCT))
        QKVG, ZG, GT, QKR, R, VN, YC = (split(a, "p (t n) -> p t n", t=TT) for a in (QKVG, ZG, GT, QKR, R, VN, YC))
        QKT2, RT = (split(a, "p (c t) -> p c t", c=4) for a in (QKT2, RT))
        DM = split(DM, "p (h s) -> p h s", h=RET_HEADS)
        WSM = split(WSM, "p (g n) -> p g n", g=4)
        QX = split(QX_, "p (k t) -> p k t", k=KD)
        SX = split(SX_, "p (t h m) -> p t h m", t=TT, h=4)
        PTX = split(PTX_, "p (h k t) -> p h k t", h=4, k=TT)
        FF = split(FF_, "p (k t) -> p k t", k=KF)
        SILU = split(SILU, "p (b n) -> p b n", b=2)

        def spar(name, a=0, b=None):
            o, n = SECOND_PARAMS[name]
            return SPAR[:, o + a:o + (n if b is None else b)]

        def hpar(name, a=0, b=None):
            o, n = HYBRID_PARAMS[name]
            return HPAR[:, o + a:o + (n if b is None else b)]

        def ring(j, k, w):
            return RING[:, j % 2, 0:k * w].rearrange("p (k w) -> p k w", k=k)

        block = ctx.enter_context(nc.Block())

        def weight_blocks(sp, blocks, tag, l):
            for j, (name, k0, k, c0, w) in enumerate(blocks):
                if j >= 2:
                    sp.e.wait_ge(*sp.at(f"{tag}{j - 2}_mm"))
                for half in range(2):
                    stream = f"dma_w{j % 2}"
                    if name == "w1w3":
                        src, kk, first, n = ("w1_2", "w3_2")[half], KD, 0, w
                        cols = COLUMNS[src]
                        view = ring(j, 2 * KD, w)[:, half * KD:(half + 1) * KD, :]
                    else:
                        src, kk = name, k // 2
                        first = half * kk
                        cols = COLUMNS[src]
                        view = ring(j, k, w)[:, first:first + kk, :]
                    rows = ROWS.get(src, D)
                    ap = bass.AP(tensor=dram[src].tensor, offset=l * (rows * cols) + (k0 + first) * P * cols + c0,
                                 ap=[[cols, P], [P * cols, kk], [1, w]])
                    sp.e.dma_start(view, ap).then_inc(*sp.count(f"{tag}{j}_in" if half else None, stream))

        def peer_block(sp, which, b, slot, l, name=None):
            n = 2 * D
            if which == "down":
                ap = bass.AP(tensor=dram["peer_down"].tensor, offset=l * (NKEYS * NKEYS * D) + b * (2 * P * D),
                             ap=[[D, P], [P * D, 2], [1, D]])
                view = RING[:, slot, 0:n].rearrange("p (j n) -> p j n", j=2)
            else:
                ap = bass.AP(tensor=dram["peer_up"].tensor, offset=l * (NKEYS * NKEYS * D) + b * (2 * D),
                             ap=[[NKEYS * D, P], [1, n]])
                view = RING[:, slot, n:2 * n]
            sp.e.dma_start(view, ap).then_inc(*sp.count(name, f"dma_{which}{slot}"))

        def norm_scalar(a, tag, src, ready):
            for name in ready:
                a.e.wait_ge(*a.at(name))
            for t in range(TT):
                a.e.activation(SCR[:, t, :], src[:, t, :], ACT.Square, accum_out=STAT[:, 48 + t:49 + t]) \
                    .then_inc(*a.count(f"{tag}_sq{t}"))
            a.e.wait_ge(*a.at(f"{tag}_ms"))
            a.e.activation(STAT[:, 52:54], STAT[:, 50:52], ACT.Sqrt).then_inc(*a.count(f"{tag}_sd"))

        def norm_vector(v, tag, src):
            v.e.wait_ge(*v.at(f"{tag}_sq1"))
            v.e.tensor_scalar(STAT[:, 50:52], STAT[:, 48:50], 1.0 / D, EPS, ALU.mult, ALU.add) \
                .then_inc(*v.count(f"{tag}_ms"))
            v.e.wait_ge(*v.at(f"{tag}_sd"))
            v.e.reciprocal(STAT[:, 54:56], STAT[:, 52:54]).then_inc(*v.count())
            v.e.wait_ge(*v.mine())
            for t in range(TT):
                v.e.tensor_scalar(SCR[:, t, :], src[:, t, :], STAT[:, 54 + t:55 + t], None, ALU.mult) \
                    .then_inc(*v.count(f"{tag}_xn{t}"))

        def turn_tensor(pe, tag, src, nk, ready, free=()):
            for name in free:
                pe.e.wait_ge(*pe.at(name))
            for t in range(TT):
                pe.e.wait_ge(*pe.at(ready[t]))
                for k0 in range(0, nk, 4):
                    kn = min(4, nk - k0)
                    for k in range(k0, k0 + kn):
                        m = pe.e.transpose(PS[:, 4 + 2 * t + k0 // 4, (k - k0) * P:(k - k0 + 1) * P],
                                           src[:, t, k * P:(k + 1) * P], IDENT)
                    m.then_inc(*pe.count(f"{tag}_t{t}{k0 // 4}"))

        def turn_vector(v, tag, dst, nk, weight):
            for t in range(TT):
                for k0 in range(0, nk, 4):
                    kn = min(4, nk - k0)
                    v.e.wait_ge(*v.at(f"{tag}_t{t}{k0 // 4}"))
                    src = PS[:, 4 + 2 * t + k0 // 4, 0:kn * P].rearrange("p (k n) -> p k n", k=kn)
                    to = dst[:, k0:k0 + kn, t * P:(t + 1) * P]
                    name = f"{tag}_done" if t == TT - 1 and k0 + 4 >= nk else None
                    if weight is None:
                        v.e.tensor_copy(to, src).then_inc(*v.count(name))
                    else:
                        w = weight[:, k0:k0 + kn].unsqueeze(2).broadcast_to([P, kn, P])
                        v.e.tensor_tensor(to, src, w, ALU.mult).then_inc(*v.count(name))

        def product(pe, tag, blocks, j, kind, src, bank, free=(), first=True, last=True):
            _, _, k, _, w = blocks[j]
            pe.e.wait_ge(*pe.at(f"{tag}{j}_in"))
            for name in free:
                pe.e.wait_ge(*pe.at(name))
            W = ring(j, k, w)
            if kind == "tokens":
                for t in range(TT):
                    for c0 in range(0, w, 512):
                        cw = min(512, w - c0)
                        b = bank + (t if w <= 512 else 2 * t + c0 // 512)
                        for kc in range(k):
                            m = pe.e.matmul(PS[:, b, 0:cw], src[:, kc, t * P:(t + 1) * P], W[:, kc, c0:c0 + cw],
                                            start=first and kc == 0, stop=last and kc == k - 1)
            else:
                for c in range(-(-w // P)):
                    cw = min(P, w - c * P)
                    for kc in range(k):
                        m = pe.e.matmul(PS[0:cw, bank + c // 2, (c % 2) * T:(c % 2 + 1) * T],
                                        W[:, kc, c * P:c * P + cw], src[:, kc, :], start=kc == 0, stop=kc == k - 1)
            m.then_inc(*pe.count(f"{tag}{j}_mm"))

        def hybrid_pool(p):
            with p.loop("hybrid", DEPTH) as l:
                p.e.wait_ge(*p.at("hybrid_start"))
                p.e.wait_ge(*p.mine())
                p.e.tensor_tensor(LB[:, 15:16], COMMON[:, 0:1], COMMON[:, 0:1], ALU.add).then_inc(*p.count())
                p.e.dma_start(HPAR[:, :], bass.AP(tensor=dram["hybrid_par"].tensor, offset=l * (P * N_HYBRID),
                                                  ap=[[N_HYBRID, P], [1, N_HYBRID]])) \
                    .then_inc(*p.count(None, "dma_params"))
                p.e.dma_start(KEYS[:, :], bass.AP(tensor=dram["sub_keys"].tensor, offset=l * (P * P),
                                                  ap=[[P, P], [1, P]])).then_inc(*p.count("params_in", "dma_params"))
                p.e.wait_ge(*p.at("bias_out"))
                p.e.dma_start(HANK, bass.AP(tensor=bias_rows.tensor, offset=0,
                                            ap=[[1, P], [REL, AT_HEADS], [1, T]])) \
                    .then_inc(*p.count("hank_in", "dma_bias_in"))
                p.e.memset(DC, 0.0).then_inc(*p.count())
                p.e.memset(DT[:, 5, :], 1.0).then_inc(*p.count("dt_clear"))
                p.e.wait_ge(*p.at("h1_ev"))
                p.e.wait_ge(*p.mine())
                p.e.tensor_tensor(LB[:, 15:16], COMMON[:, 0:1], COMMON[:, 0:1], ALU.add).then_inc(*p.count())
                p.e.dma_start(hi_rows.rearrange("(c p) t -> p c t", p=P), HI) \
                    .then_inc(*p.count("hi_out", "dma_hi_out"))
                for pair in range(2):
                    with p.loop(f"scan{pair}", HEAD // (2 * VGROUP)):
                        for b in range(2):
                            p.e.wait_ge(*p.at(f"hi_in{pair}{b}"))
                            p.e.wait_ge(*p.at(f"state{pair}{b}", back=1))
                            p.e.wait_ge(*p.at("gates"))
                            p.e.tensor_tensor(KV[:, b, :, :], VB[:, b, :, :],
                                              KEY[:, pair, :].unsqueeze(1).broadcast_to([P, VGROUP, T]), ALU.mult) \
                                .then_inc(*p.count(f"kv{pair}{b}"))

        def hybrid_scalar(a, l):
            norm_scalar(a, "n1", X, ["hybrid_start"])
            a.e.wait_ge(*a.at("h0_mm"))
            a.e.activation(HQ.rearrange("p c t -> p (c t)"), PS[:, 0, :], ACT.Copy, scale=HEAD ** -0.5) \
                .then_inc(*a.count())
            a.e.activation(FS.rearrange("p c t -> p (c t)"), PS[:, 1, :], ACT.Sigmoid).then_inc(*a.count("h0_ev"))
            a.e.wait_ge(*a.at("h1_mm"))
            a.e.activation(HI.rearrange("p c t -> p (c t)"), PS[:, 2, :], ACT.Copy).then_inc(*a.count("h1_ev"))
            for j in range(2, 6):
                _, _, _, c0, w = HYBRID_BLOCKS[j]
                a.e.wait_ge(*a.at(f"h{j}_mm"))
                for t in range(TT):
                    a.e.activation(U[:, t, c0 - 768:c0 - 768 + w], PS[:, 2 * (j % 2) + t, 0:w], ACT.Copy) \
                        .then_inc(*a.count(f"h{j}_ev" if t else None))
            for j in range(6, 8):
                a.e.wait_ge(*a.at(f"h{j}_mm"))
                for b in range(2):
                    c = 4 * (j - 6) + 2 * b
                    n = min(2, CONV_TILES - c)
                    a.e.activation(XB[:, c:c + n, 3:T + 3],
                                   PS[:, 2 * (j % 2) + b, 0:n * T].rearrange("p (c t) -> p c t", c=n), ACT.Copy) \
                        .then_inc(*a.count("h6_ev" if j == 6 and b else None))
            a.e.wait_ge(*a.at("dt_clear"))
            a.e.activation(DT[0:SS_HEADS, 0, :], PS[0:SS_HEADS, 3, T:2 * T], ACT.Copy).then_inc(*a.count("h7_ev"))
            a.e.wait_ge(*a.at("hi_out"))
            for pair in range(2):
                with a.loop(f"scan{pair}", HEAD // (2 * VGROUP)) as i:
                    for b in range(2):
                        a.e.wait_ge(*a.at(f"kv{pair}{b}", back=1))
                        for h in range(2):
                            row = (2 * pair + h) * HEAD
                            src = bass.AP(tensor=hi_rows.tensor, offset=i * (2 * VGROUP * T) + (row + b * VGROUP) * T,
                                          ap=[[0, HEAD], [T, VGROUP], [1, T]])
                            a.e.dma_start(VB[h * HEAD:(h + 1) * HEAD, b, :, :], src) \
                                .then_inc(*a.count(f"hi_in{pair}{b}" if h else None, f"dma_hi_in{b}"))
            a.e.wait_ge(*a.at("gates"))
            a.e.activation(FS.rearrange("p c t -> p (c t)").rearrange("p (t n) -> p t n", t=TT),
                           U[:, :, 0:HG_W], ACT.Silu).then_inc(*a.count("g_silu"))
            a.e.wait_ge(*a.at("hg_ms"))
            a.e.activation(STAT[:, 24:32], STAT[:, 16:24], ACT.Sqrt).then_inc(*a.count("hg_sd"))
            a.e.wait_ge(*a.at("qk_ms"))
            a.e.activation(STAT[:, 88:112], STAT[:, 64:88], ACT.Sqrt).then_inc(*a.count("qk_sd"))
            a.e.wait_ge(*a.at("at_max"))
            for h in range(AT_HEADS):
                for t, s in ((0, SCORE0), (1, SCORE1)):
                    c = t * AT_HEADS + h
                    a.e.activation(s[:, h, :], s[:, h, :], ACT.Exp, bias=STAT[:, c:c + 1],
                                   accum_out=STAT[:, 12 + c:13 + c]) \
                        .then_inc(*a.count("at_exp" if h == 5 and t == 1 else None))
            for n in range(5):
                a.e.wait_ge(*a.at(f"pt{n}"))
                w = min(4, 18 - 4 * n) * P
                a.e.activation(PT.rearrange("p h k t -> p (h k t)")[:, n * 512:n * 512 + w], PS[:, n, 0:w],
                               ACT.Copy).then_inc(*a.count(f"pt{n}_ev"))
            a.e.wait_ge(*a.at("dt_neg"))
            a.e.activation(DT[0:SS_HEADS, 3, :], DT[0:SS_HEADS, 2, :], ACT.Exp).then_inc(*a.count())
            a.e.wait_ge(*a.mine())
            a.e.activation(DT[0:SS_HEADS, 3, :], DT[0:SS_HEADS, 3, :], ACT.Ln, bias=1.0).then_inc(*a.count())
            a.e.activation(STAT[0:SS_HEADS, 56:57], hpar("a_log")[0:SS_HEADS], ACT.Exp).then_inc(*a.count("dt_log"))
            a.e.wait_ge(*a.at("conv"))
            for c in range(CONV_TILES):
                a.e.activation(XC[:, c, :], XC[:, c, :], ACT.Silu, bias=hpar("conv_b", c, c + 1)) \
                    .then_inc(*a.count(f"xc{c}"))
            a.e.activation(SZ, U[:, :, 1408:1792], ACT.Silu).then_inc(*a.count("z_silu"))
            a.e.wait_ge(*a.at("dec"))
            a.e.activation(SCORE, SCORE, ACT.Exp).then_inc(*a.count("dec_exp"))
            a.e.wait_ge(*a.at("ss_ms"))
            a.e.activation(STAT[:, 24:28], STAT[:, 16:20], ACT.Sqrt).then_inc(*a.count("ss_sd"))
            norm_scalar(a, "n2", X, ["h9_ev"])
            for j in (10, 11):
                a.e.wait_ge(*a.at(f"h{j}_mm"))
                for b in range(2):
                    h = 4 * (j - 10) + 2 * b
                    a.e.activation(PQ[:, h:h + 2, :].rearrange("p h t -> p (h t)"), PS[:, 2 * (j % 2) + b, :],
                                   ACT.Copy).then_inc(*a.count(f"h{j}_ev" if b else None))
            for t in range(TT):
                a.e.wait_ge(*a.at(f"key_mm{t}"))
                for b in range(4):
                    to = SC[:, t, :, :].rearrange("p (h c) n -> p h c n", c=2)[:, 4 * (b % 2):4 * (b % 2) + 4, b // 2, :]
                    a.e.activation(to, PS[:, 4 * t + b, :].rearrange("p (h n) -> p h n", h=4), ACT.Copy) \
                        .then_inc(*a.count(f"key_ev{t}" if b == 3 else None))
            for t in range(TT):
                a.e.wait_ge(*a.at(f"best_off{t}"))
                a.e.activation(BESTV.rearrange("p h k -> p (h k)"), OFF, ACT.Exp).then_inc(*a.count(f"best_exp{t}"))
            with a.loop("gate", T // 8) as i:
                for b in range(2):
                    a.e.wait_ge(*a.at(f"gate_mm{b}"))
                    a.e.activation(ARENA[:, bass.ds(i * 1024 + b * 512, 512)], PS[:, 6 + b, :], ACT.Copy) \
                        .then_inc(*a.count(f"gate_ev{b}"))
            a.e.wait_ge(*a.at("act_in_first"))
            a.e.activation(GELU[:, 0, :], PS[:, 4, :], ACT.Gelu_apprx_tanh).then_inc(*a.count("gelu_first"))
            with a.loop("peer", NKEYS // 4 - 1):
                a.e.wait_ge(*a.at("act_in1"))
                a.e.wait_ge(*a.at("coef1", back=1))
                a.e.activation(GELU[:, 1, :], PS[:, 5, :], ACT.Gelu_apprx_tanh).then_inc(*a.count("gelu1"))
                a.e.wait_ge(*a.at("act_in0"))
                a.e.wait_ge(*a.at("coef0", back=1))
                a.e.activation(GELU[:, 0, :], PS[:, 4, :], ACT.Gelu_apprx_tanh).then_inc(*a.count("gelu0"))
            a.e.wait_ge(*a.at("act_in_last"))
            a.e.wait_ge(*a.at("coef1"))
            a.e.activation(GELU[:, 1, :], PS[:, 5, :], ACT.Gelu_apprx_tanh).then_inc(*a.count("gelu_last"))

        def hybrid_tensor(pe, l):
            turn_tensor(pe, "n1", SCR, KD, ["n1_xn0", "n1_xn1"], ["hybrid_start"])
            pe.e.wait_ge(*pe.at("n1_done"))
            for j in range(8):
                kind = "tokens" if 2 <= j < 6 else "channels"
                product(pe, "h", HYBRID_BLOCKS, j, kind, HT, 2 * (j % 2), [f"h{j - 2}_ev"] if j >= 2 else [])
            pe.e.wait_ge(*pe.at("hank_in"))
            for h in range(AT_HEADS):
                m = pe.e.matmul(PS[:, 4 + h // 2, (h % 2) * T:(h % 2 + 1) * T], FLIP, HANK[:, h, :], start=True,
                                stop=True)
            m.then_inc(*pe.count("flip"))
            OB = PS[:, 7, :].rearrange("p (t h v) -> p t h v", t=TT, h=HG_HEADS)
            for pair in range(2):
                with pe.loop(f"scan{pair}", HEAD // (2 * VGROUP)) as i:
                    for b in range(2):
                        pe.e.wait_ge(*pe.at(f"qs{pair}{b}"))
                        for v in range(VGROUP):
                            for t in range(TT):
                                m = pe.e.matmul(OB[:, t, 2 * pair:2 * pair + 2,
                                                   bass.ds(i * (2 * VGROUP) + (b * VGROUP + v), 1)],
                                                QS[:, b, v, t * P:(t + 1) * P], HALVES, start=True, stop=True)
                        m.then_inc(*pe.count(f"hg{pair}{b}"))
            pe.e.wait_ge(*pe.at("qkn"))
            pe.e.wait_ge(*pe.at("bias_ev"))
            for c in range(6):
                for t in range(TT):
                    m = pe.e.transpose(PS[:, 4 + c // 2, (c % 2) * T + t * P:(c % 2) * T + (t + 1) * P],
                                       QKN[:, t, c * P:(c + 1) * P], IDENT)
            m.then_inc(*pe.count("qk_t"))
            pe.e.wait_ge(*pe.at("qkt"))
            pe.e.wait_ge(*pe.at("h6_ev"))
            pe.e.wait_ge(*pe.at("h7_ev"))
            for h in range(AT_HEADS):
                r = 64 * (h % 2)
                q, k = QKT[r:r + 64, h // 2, :], QKT[r:r + 64, 3 + h // 2, :]
                pe.e.matmul(PS[:, 2 * (h % 2) + h // 4, (h // 2 % 2) * T:(h // 2 % 2 + 1) * T], q[:, P:T], k,
                            start=True, stop=True)
                m = pe.e.matmul(PS[:, 4 + h % 2, (h // 2) * P:(h // 2 + 1) * P], q[:, 0:P], k[:, 0:P], start=True,
                                stop=True)
            m.then_inc(*pe.count("at_scores"))
            pe.e.wait_ge(*pe.at("at_exp"))
            for n in range(18):
                h, k = divmod(n, 3)
                src = SCORE0[:, h, :] if k == 0 else SCORE1[:, h, (k - 1) * P:k * P]
                m = pe.e.transpose(PS[:, n // 4, (n % 4) * P:(n % 4 + 1) * P], src, IDENT)
                if n % 4 == 3 or n == 17:
                    m.then_inc(*pe.count(f"pt{n // 4}"))
            pe.e.wait_ge(*pe.at("pt4_ev"))
            for h in range(AT_HEADS):
                v = [U[:, t, 1024 + HEAD * h:1024 + HEAD * (h + 1)] for t in range(TT)]
                o = slice(h * HEAD, (h + 1) * HEAD)
                pe.e.matmul(PS[:, 5, o], PT[:, h, 0, :], v[0], start=True, stop=True)
                pe.e.matmul(PS[:, 6, o], PT[:, h, 1, :], v[0], start=True, stop=False)
                m = pe.e.matmul(PS[:, 6, o], PT[:, h, 2, :], v[1], start=False, stop=True)
            m.then_inc(*pe.count("at_out"))
            pe.e.wait_ge(*pe.at("dc"))
            pe.e.wait_ge(*pe.at("hg_read"))
            for t in range(TT):
                m = pe.e.transpose(PS[:, 7, t * P:(t + 1) * P], DC[:, t * P:(t + 1) * P], IDENT)
            m.then_inc(*pe.count("cd_t"))
            for h in range(SS_HEADS):
                m = pe.e.matmul(PS[:, h // 2, (h % 2) * T:(h % 2 + 1) * T],
                                IDENT[0:SS_HEADS, h:h + 1].broadcast_to([SS_HEADS, P]), DT[0:SS_HEADS, 4, :],
                                start=True, stop=True)
            m.then_inc(*pe.count("cum_rows"))
            pe.e.wait_ge(*pe.at("xc6"))
            for g in range(GROUPS):
                pe.e.matmul(PS[:, 3 + g, 0:T], XC[:, 3 + g, 0:P], XC[:, 5 + g, :], start=True, stop=True)
                m = pe.e.matmul(PS[:, 3 + g, T:T + P], XC[:, 3 + g, P:T], XC[:, 5 + g, P:T], start=True, stop=True)
            m.then_inc(*pe.count("bc"))
            pe.e.wait_ge(*pe.at("at_mix"))
            for t in range(TT):
                for c in range(3):
                    m = pe.e.transpose(PS[:, 5 + t, c * P:(c + 1) * P], XC[:, c, t * P:(t + 1) * P], IDENT)
            m.then_inc(*pe.count("xs_t"))
            pe.e.wait_ge(*pe.at("dec_bc"))
            pe.e.wait_ge(*pe.at("xdt"))
            for h in range(SS_HEADS):
                o = slice(h * HEAD, (h + 1) * HEAD)
                pe.e.matmul(PS[:, 0, o], DEC[:, h, 0:P], XDT[:, 0, o], start=True, stop=True)
                pe.e.matmul(PS[:, 1, o], DEC[:, h, P:T], XDT[:, 0, o], start=True, stop=False)
                m = pe.e.matmul(PS[:, 1, o], DEC[:, h, T:T + P], XDT[:, 1, o], start=False, stop=True)
            m.then_inc(*pe.count("ss_out"))
            turn_tensor(pe, "mx", MIX, KD, ["mix", "mix"])
            pe.e.wait_ge(*pe.at("mx_done"))
            for j in (8, 9):
                product(pe, "h", HYBRID_BLOCKS, j, "tokens", HT, 2 * (j % 2), ["ss_read"])
            turn_tensor(pe, "n2", SCR, KD, ["n2_xn0", "n2_xn1"])
            pe.e.wait_ge(*pe.at("n2_done"))
            for j in (10, 11):
                product(pe, "h", HYBRID_BLOCKS, j, "channels", HT, 2 * (j % 2), [f"h{j - 2}_ev"])
            pe.e.wait_ge(*pe.at("h11_ev"))
            pe.e.wait_ge(*pe.at("params_in"))
            for t in range(TT):
                for h in range(PEER_HEADS):
                    for c in range(2):
                        r = 64 * c
                        m = pe.e.matmul(PS[:, 4 * t + 2 * c + h // 4, (h % 4) * P:(h % 4 + 1) * P],
                                        PQ[r:r + 64, h, t * P:(t + 1) * P], KEYS[r:r + 64, :], start=True, stop=True)
                m.then_inc(*pe.count(f"key_mm{t}"))
            for t in range(TT):
                pe.e.wait_ge(*pe.at(f"hkr{t}"))
                pe.e.wait_ge(*pe.at("key_ev1"))
                for c in range(3):
                    m = pe.e.transpose(PS[:, t, c * P:(c + 1) * P], HKR[:, c, :], IDENT)
                m.then_inc(*pe.count(f"hk_t{t}"))
            with pe.loop("gate", T // 8):
                for b in range(2):
                    pe.e.wait_ge(*pe.at(f"hot{b}"))
                    pe.e.wait_ge(*pe.at(f"gate_ev{b}", back=1))
                    for j in range(4):
                        m = pe.e.matmul(PS[:, 6 + b, j * P:(j + 1) * P], ONE[:, 0, b, j, :], ONE[:, 1, b, j, :],
                                        start=True, stop=True)
                    m.then_inc(*pe.count(f"gate_mm{b}"))

            def act_in(b, name):
                for j in range(2):
                    for kc in range(KD):
                        m = pe.e.matmul(PS[:, 4 + b, j * T:(j + 1) * T],
                                        RING[:, b, j * D + kc * P:j * D + (kc + 1) * P], HT[:, kc, :],
                                        start=kc == 0, stop=kc == KD - 1)
                m.then_inc(*pe.count(name))

            def out_of(b, name, last=False):
                for j in range(2):
                    for t in range(TT):
                        for half in range(2):
                            m = pe.e.matmul(PS[:, 2 * t + half, :], COEF[:, b, j * T + t * P:j * T + (t + 1) * P],
                                            RING[:, b, 2 * D + j * D + half * 512:2 * D + j * D + (half + 1) * 512],
                                            start=False, stop=last and j == 1, skip_group_check=True)
                m.then_inc(*pe.count(name))

            pe.e.wait_ge(*pe.at("zero"))
            pe.e.wait_ge(*pe.at("hk_read"))
            for b in range(4):
                m = pe.e.matmul(PS[:, b, :], KEYS[:, :], PHASE[:, 0:512], start=True, stop=False,
                                skip_group_check=True)
            pe.e.wait_ge(*pe.at("down_first0"))
            act_in(0, "act_in_first")
            with pe.loop("peer", NKEYS // 4 - 1) as i:
                pe.e.wait_ge(*pe.at("down1", back=1))
                pe.e.wait_ge(*pe.at("gelu1", back=1))
                act_in(1, "act_in1")
                pe.e.wait_ge(*pe.at("up0", back=1))
                pe.e.wait_ge(*pe.at("coef0", back=1))
                out_of(0, "out0")
                pe.e.wait_ge(*pe.at("down0"))
                pe.e.wait_ge(*pe.at("gelu0", back=1))
                act_in(0, "act_in0")
                pe.e.wait_ge(*pe.at("up1", back=1))
                pe.e.wait_ge(*pe.at("coef1"))
                out_of(1, "out1")
            pe.e.wait_ge(*pe.at("down1"))
            pe.e.wait_ge(*pe.at("gelu1"))
            act_in(1, "act_in_last")
            pe.e.wait_ge(*pe.at("up0"))
            pe.e.wait_ge(*pe.at("coef0"))
            out_of(0, "out_last0")
            pe.e.wait_ge(*pe.at("up1"))
            pe.e.wait_ge(*pe.at("coef_last"))
            out_of(1, "out_last1", last=True)

        def hybrid_vector(v, l):
            def bc(ap, n):
                return ap.unsqueeze(2).broadcast_to([P, ap.shape[1], n])

            def rstd(tag, n, width, src, dst):
                v.e.wait_ge(*v.mine())
                v.e.tensor_scalar(STAT[:, src:src + n], STAT[:, src:src + n], 1.0 / width, EPS, ALU.mult,
                                  ALU.add).then_inc(*v.count(f"{tag}_ms"))
                v.e.wait_ge(*v.at(f"{tag}_sd"))
                v.e.reciprocal(STAT[:, dst:dst + n], STAT[:, dst:dst + n]).then_inc(*v.count())
                v.e.wait_ge(*v.mine())

            v.e.wait_ge(*v.mine())
            v.e.memset(XB[:, :, 0:3], 0.0).then_inc(*v.count("hybrid_start"))
            norm_vector(v, "n1", X)
            v.e.wait_ge(*v.at("params_in"))
            turn_vector(v, "n1", HT, KD, hpar("attn_norm"))
            v.e.tensor_copy(STAT[:, 0:2], LB[:, bass.ds(l * 2 + 10, 2)]).then_inc(*v.count())
            v.e.wait_ge(*v.mine())
            v.e.tensor_scalar(STAT[:, 2:4], STAT[:, 0:2], -1.0, 1.0, ALU.mult, ALU.add).then_inc(*v.count())
            v.e.wait_ge(*v.mine())
            v.e.wait_ge(*v.at("h0_ev"))
            for c in range(2):
                v.e.tensor_scalar(FS[:, c, :], FS[:, c, :], STAT[:, 2 + c:3 + c], STAT[:, c:c + 1], ALU.mult,
                                  ALU.add).then_inc(*v.count())
            v.e.wait_ge(*v.mine())
            v.e.tensor_scalar(KEY, FS, -1.0, 1.0, ALU.mult, ALU.add).then_inc(*v.count())
            for c in range(2):
                v.e.tensor_copy(FR[:, c, :, :], FS[:, c, :].unsqueeze(1).broadcast_to([P, VGROUP, T])) \
                    .then_inc(*v.count())
            v.e.wait_ge(*v.mine())
            v.e.memset(FR[:, :, :, 0:1], 0.0).then_inc(*v.count("gates"))
            v.e.wait_ge(*v.mine())
            v.e.tensor_copy(LB[:, 14:15], COMMON[:, 0:1]).then_inc(*v.count())
            for pair in range(2):
                with v.loop(f"scan{pair}", HEAD // (2 * VGROUP)):
                    for b in range(2):
                        v.e.wait_ge(*v.at(f"kv{pair}{b}"))
                        v.e.tensor_tensor_scan(
                            ST[:, b, :, :].rearrange("p v t -> p (v t)"),
                            FR[:, pair, :, :].rearrange("p v t -> p (v t)"),
                            KV[:, b, :, :].rearrange("p v t -> p (v t)"), 0.0, ALU.mult, ALU.add) \
                            .then_inc(*v.count(f"state{pair}{b}"))
                        v.e.wait_ge(*v.mine())
                        v.e.wait_ge(*v.at(f"hg{pair}{b}", back=1))
                        v.e.tensor_tensor(QS[:, b, :, :], ST[:, b, :, :],
                                          HQ[:, pair, :].unsqueeze(1).broadcast_to([P, VGROUP, T]), ALU.mult) \
                            .then_inc(*v.count(f"qs{pair}{b}"))
            v.e.wait_ge(*v.at("flip"))
            for b in range(3):
                v.e.tensor_tensor(BIAS1[:, 2 * b:2 * b + 2, :],
                                  PS[:, 4 + b, :].rearrange("p (h s) -> p h s", h=2),
                                  PHASE[:, 0:T].unsqueeze(1).broadcast_to([P, 2, T]), ALU.add).then_inc(*v.count())
                v.e.tensor_tensor(BIAS0[:, 2 * b:2 * b + 2, :],
                                  PS[:, 4 + b, :].rearrange("p (h s) -> p h s", h=2)[:, :, P:T],
                                  PHASE[:, T:T + P].unsqueeze(1).broadcast_to([P, 2, P]), ALU.add) \
                    .then_inc(*v.count("bias_ev" if b == 2 else None))
            v.e.wait_ge(*v.at("hg11"))
            o, sq = SCORE[:, 0:512], SCORE[:, 512:1024]
            v.e.tensor_copy(o, PS[:, 7, :]).then_inc(*v.count("hg_read"))
            v.e.wait_ge(*v.mine())
            v.e.tensor_tensor(sq, o, o, ALU.mult).then_inc(*v.count())
            v.e.wait_ge(*v.mine())
            v.e.tensor_reduce(STAT[:, 16:24], sq.rearrange("p (n v) -> p n v", v=HEAD), AX.X, ALU.add) \
                .then_inc(*v.count())
            rstd("hg", 8, HEAD, 16, 24)
            v.e.tensor_tensor(o.rearrange("p (n v) -> p n v", v=HEAD), o.rearrange("p (n v) -> p n v", v=HEAD),
                              bc(STAT[:, 24:32], HEAD), ALU.mult).then_inc(*v.count())
            v.e.wait_ge(*v.mine())
            v.e.wait_ge(*v.at("g_silu"))
            v.e.tensor_tensor(MIX[:, :, 0:HG_W], o.rearrange("p (t n) -> p t n", t=TT),
                              FS.rearrange("p c t -> p (c t)").rearrange("p (t n) -> p t n", t=TT), ALU.mult) \
                .then_inc(*v.count())
            v.e.wait_ge(*v.mine())
            sq = SCORE[:, 0:1536].rearrange("p (t n) -> p t n", t=TT)
            v.e.tensor_tensor(sq, U[:, :, 256:1024], U[:, :, 256:1024], ALU.mult).then_inc(*v.count())
            v.e.wait_ge(*v.mine())
            v.e.tensor_reduce(STAT[:, 64:88], SCORE[:, 0:1536].rearrange("p (n d) -> p n d", d=HEAD), AX.X,
                              ALU.add).then_inc(*v.count())
            rstd("qk", 24, HEAD, 64, 88)
            for t in range(TT):
                v.e.tensor_tensor(QKN[:, t, :].rearrange("p (n d) -> p n d", d=HEAD),
                                  U[:, t, 256:1024].rearrange("p (n d) -> p n d", d=HEAD),
                                  bc(STAT[:, 88 + 12 * t:100 + 12 * t], HEAD), ALU.mult) \
                    .then_inc(*v.count("qkn" if t else None))
            v.e.wait_ge(*v.at("qk_t"))
            for c0, c1, w in ((0, 2, "q_norm"), (2, 3, "q_norm"), (3, 4, "k_norm"), (4, 6, "k_norm")):
                v.e.tensor_scalar(QKT[:, c0:c1, :].rearrange("p c t -> p (c t)"),
                                  PS[:, 4 + c0 // 2, (c0 % 2) * T:(c0 % 2) * T + (c1 - c0) * T],
                                  hpar(w), HEAD ** -0.5 if w == "q_norm" else 1.0, ALU.mult, ALU.mult) \
                    .then_inc(*v.count("qkt" if c1 == 6 else None))
            v.e.wait_ge(*v.at("at_scores"))
            v.e.wait_ge(*v.mine())
            for odd in range(2):
                v.e.tensor_tensor(SCORE1[:, odd:4:2, :],
                                  PS[:, 2 * odd, :].rearrange("p (h s) -> p h s", h=2),
                                  BIAS1[:, odd:4:2, :], ALU.add).then_inc(*v.count())
                v.e.tensor_tensor(SCORE1[:, 4 + odd, :], PS[:, 2 * odd + 1, 0:T], BIAS1[:, 4 + odd, :],
                                  ALU.add).then_inc(*v.count())
                v.e.tensor_tensor(SCORE0[:, odd:6:2, :],
                                  PS[:, 4 + odd, 0:3 * P].rearrange("p (h s) -> p h s", h=3),
                                  BIAS0[:, odd:6:2, :], ALU.add).then_inc(*v.count())
            v.e.wait_ge(*v.mine())
            v.e.tensor_reduce(STAT[:, 0:6], SCORE0, AX.X, ALU.max, negate=True).then_inc(*v.count())
            v.e.tensor_reduce(STAT[:, 6:12], SCORE1, AX.X, ALU.max, negate=True).then_inc(*v.count("at_max"))
            v.e.wait_ge(*v.at("h7_ev"))
            z, neg, soft, cum = (DT[0:SS_HEADS, k, :] for k in (1, 2, 3, 4))
            v.e.tensor_scalar(z, DT[0:SS_HEADS, 0, :], hpar("dt_bias")[0:SS_HEADS], None, ALU.add) \
                .then_inc(*v.count())
            v.e.wait_ge(*v.mine())
            v.e.scalar_tensor_tensor(neg, z, -1.0, z, ALU.mult, ALU.min).then_inc(*v.count("dt_neg"))
            for k in range(4):
                for c in range(CONV_TILES):
                    w = hpar("conv_w", k * CONV_TILES + c, k * CONV_TILES + c + 1)
                    if k == 0:
                        i = v.e.tensor_scalar(XC[:, c, :], XB[:, c, 0:T], w, None, ALU.mult)
                    else:
                        v.e.wait_ge(*v.mine(CONV_TILES - 1))
                        i = v.e.scalar_tensor_tensor(XC[:, c, :], XB[:, c, k:k + T], w, XC[:, c, :], ALU.mult, ALU.add)
                    i.then_inc(*v.count("conv" if k == 3 and c == CONV_TILES - 1 else None))
            v.e.wait_ge(*v.at("at_exp"))
            v.e.reciprocal(STAT[:, 32:44], STAT[:, 12:24]).then_inc(*v.count())
            v.e.wait_ge(*v.mine())
            v.e.wait_ge(*v.at("at_out"))
            for t in range(TT):
                v.e.tensor_tensor(MIX[:, t, HG_W:HG_W + AT_W].rearrange("p (h d) -> p h d", d=HEAD),
                                  PS[:, 5 + t, 0:AT_W].rearrange("p (h d) -> p h d", d=HEAD),
                                  bc(STAT[:, 32 + 6 * t:38 + 6 * t], HEAD), ALU.mult) \
                    .then_inc(*v.count("at_mix" if t else None))
            v.e.wait_ge(*v.at("dt_log"))
            v.e.scalar_tensor_tensor(neg, z, 0.0, soft, ALU.max, ALU.add).then_inc(*v.count())
            v.e.wait_ge(*v.mine())
            v.e.tensor_scalar(soft, neg, STAT[0:SS_HEADS, 56:57], -1.0, ALU.mult, ALU.mult).then_inc(*v.count())
            v.e.wait_ge(*v.mine())
            v.e.tensor_tensor_scan(cum, DT[0:SS_HEADS, 5, :], soft, 0.0, ALU.mult, ALU.add).then_inc(*v.count())
            v.e.wait_ge(*v.mine())
            v.e.tensor_copy(DC[0:SS_HEADS, :], cum).then_inc(*v.count())
            v.e.tensor_copy(DC[32:32 + SS_HEADS, :], neg).then_inc(*v.count("dc"))
            v.e.wait_ge(*v.at("cd_t"))
            v.e.tensor_copy(CD, PS[:, 7, 0:T].rearrange("p (t n) -> p t n", t=TT)[:, :, 0:64]).then_inc(*v.count())
            v.e.wait_ge(*v.mine())
            v.e.wait_ge(*v.at("cum_rows"))
            mask = PHASE[:, T + P:2 * (T + P)]
            for h in range(SS_HEADS):
                row = PS[:, h // 2, (h % 2) * T:(h % 2 + 1) * T]
                v.e.scalar_tensor_tensor(DEC[:, h, 0:T], row, CD[:, 0, h:h + 1], mask[:, 0:T], ALU.subtract,
                                         ALU.add).then_inc(*v.count())
                v.e.scalar_tensor_tensor(DEC[:, h, T:T + P], row[:, P:T], CD[:, 1, h:h + 1], mask[:, T:T + P],
                                         ALU.subtract, ALU.add) \
                    .then_inc(*v.count("dec" if h == SS_HEADS - 1 else None))
            v.e.wait_ge(*v.at("xs_t"))
            for t in range(TT):
                x = PS[:, 5 + t, 0:SS_W].rearrange("p (h d) -> p h d", d=HEAD)
                v.e.tensor_tensor(XDT[:, t, :].rearrange("p (h d) -> p h d", d=HEAD), x,
                                  bc(CD[:, t, 32:32 + SS_HEADS], HEAD), ALU.mult).then_inc(*v.count())
                v.e.tensor_tensor(XSK[:, t, :].rearrange("p (h d) -> p h d", d=HEAD), x,
                                  bc(hpar("d_skip"), HEAD), ALU.mult).then_inc(*v.count("xdt" if t else None))
            v.e.wait_ge(*v.at("dec_exp"))
            v.e.wait_ge(*v.at("bc"))
            for g in range(GROUPS):
                d = DEC[:, 3 * g:3 * g + 3, :]
                v.e.tensor_tensor(d, d, PS[:, 3 + g, 0:T + P].unsqueeze(1).broadcast_to([P, 3, T + P]),
                                  ALU.mult).then_inc(*v.count("dec_bc" if g else None))
            v.e.wait_ge(*v.at("ss_out"))
            for t in range(TT):
                v.e.tensor_tensor(XSK[:, t, :], PS[:, t, 0:SS_W], XSK[:, t, :], ALU.add) \
                    .then_inc(*v.count("ss_read" if t else None))
            v.e.wait_ge(*v.mine())
            v.e.wait_ge(*v.at("z_silu"))
            v.e.tensor_tensor(XSK, XSK, SZ, ALU.mult).then_inc(*v.count())
            v.e.wait_ge(*v.mine())
            v.e.tensor_tensor(XDT, XSK, XSK, ALU.mult).then_inc(*v.count())
            v.e.wait_ge(*v.mine())
            v.e.tensor_reduce(STAT[:, 16:20], XDT.rearrange("p t (g n) -> p (t g) n", g=GROUPS), AX.X, ALU.add) \
                .then_inc(*v.count())
            rstd("ss", 4, SS_W // GROUPS, 16, 24)
            for t in range(TT):
                v.e.tensor_tensor(MIX[:, t, HG_W + AT_W:D].rearrange("p (g n) -> p g n", g=GROUPS),
                                  XSK[:, t, :].rearrange("p (g n) -> p g n", g=GROUPS),
                                  bc(STAT[:, 24 + 2 * t:26 + 2 * t], SS_W // GROUPS), ALU.mult) \
                    .then_inc(*v.count("mix" if t else None))
            turn_vector(v, "mx", HT, KD, hpar("mix_norm"))
            add_to_x(v, "h", HYBRID_BLOCKS, (8, 9))
            v.e.wait_ge(*v.mine())
            norm_vector(v, "n2", X)
            turn_vector(v, "n2", HT, KD, hpar("ffn_norm"))
            for t in range(TT):
                top_keys(v, t)
            v.e.wait_ge(*v.at("key_mm1"))
            v.e.memset(KEYS[:, :], 0.0).then_inc(*v.count("zero"))
            with v.loop("gate", T // 8) as i:
                for b in range(2):
                    v.e.wait_ge(*v.at(f"gate_mm{b}", back=1))
                    for j in range(4):
                        at = i * 8 + (4 * b + j)
                        v.e.tensor_scalar(ONE[:, 0, b, j, :], IOTA, HK[:, 0, bass.ds(at, 1)], None,
                                          ALU.is_equal).then_inc(*v.count())
                        v.e.tensor_scalar(ONE[:, 1, b, j, :], IOTA, HK[:, 1, bass.ds(at, 1)],
                                          HK[:, 2, bass.ds(at, 1)], ALU.is_equal, ALU.mult) \
                            .then_inc(*v.count(f"hot{b}" if j == 3 else None))

            def coef(b, n2, name):
                v.e.tensor_tensor(COEF[:, b, :].rearrange("p (j t) -> p j t", j=2),
                                  GELU[:, b, :].rearrange("p (j t) -> p j t", j=2),
                                  G[:, :, bass.ds(n2, 2)].rearrange("p t j -> p j t"), ALU.mult) \
                    .then_inc(*v.count(name))

            v.e.wait_ge(*v.at("gelu_first"))
            coef(0, 0, "coef_first")
            with v.loop("peer", NKEYS // 4 - 1) as i:
                v.e.wait_ge(*v.at("gelu1"))
                v.e.wait_ge(*v.at("out1", back=1))
                coef(1, i * 4 + 2, "coef1")
                v.e.wait_ge(*v.at("gelu0"))
                v.e.wait_ge(*v.at("out0"))
                coef(0, i * 4 + 4, "coef0")
            v.e.wait_ge(*v.at("gelu_last"))
            v.e.wait_ge(*v.at("out1"))
            coef(1, NKEYS - 2, "coef_last")
            v.e.wait_ge(*v.at("out_last1"))
            for t in range(TT):
                for half in range(2):
                    x = X[:, t, half * 512:(half + 1) * 512]
                    v.e.tensor_tensor(x, PS[:, 2 * t + half, :], x, ALU.add) \
                        .then_inc(*v.count("hybrid_end" if t == 1 and half else None))

        def add_to_x(v, tag, blocks, js):
            for j in js:
                c0 = blocks[j][3]
                v.e.wait_ge(*v.at(f"{tag}{j}_mm"))
                for t in range(TT):
                    x = X[:, t, c0:c0 + 512]
                    v.e.tensor_tensor(x, PS[:, 2 * (j % 2) + t, :], x, ALU.add) \
                        .then_inc(*v.count(f"{tag}{j}_ev" if t else None))

        def top_keys(v, t):
            S = SC[:, t, :, :]
            v.e.wait_ge(*v.at(f"key_ev{t}"))

            def best(scores, spare, values, index, n):
                v.e.wait_ge(*v.mine())
                v.e.tensor_copy(LB[:, 14:15], COMMON[:, 0:1]).then_inc(*v.count())
                for c in range(n):
                    v.e.max(values(c)[:, 0:8], scores(c)).then_inc(*v.count())
                v.e.wait_ge(*v.mine())
                v.e.tensor_copy(LB[:, 14:15], COMMON[:, 0:1]).then_inc(*v.count())
                for c in range(n):
                    v.e.max_index(index(c)[:, 0:8], values(c)[:, 0:8], scores(c)).then_inc(*v.count())
                for c in range(n):
                    v.e.match_replace(spare(c), values(c)[:, 0:8], scores(c), -BIG).then_inc(*v.count())
                v.e.wait_ge(*v.mine())
                v.e.tensor_copy(LB[:, 14:15], COMMON[:, 0:1]).then_inc(*v.count())
                for c in range(n):
                    v.e.max(values(c)[:, 8:16], spare(c)).then_inc(*v.count())
                v.e.wait_ge(*v.mine())
                v.e.tensor_copy(LB[:, 14:15], COMMON[:, 0:1]).then_inc(*v.count())
                for c in range(n):
                    v.e.max_index(index(c)[:, 8:16], values(c)[:, 8:16], spare(c)).then_inc(*v.count())
                v.e.wait_ge(*v.mine())

            best(lambda c: S[:, c, :], lambda c: SC2[:, c, :], lambda c: TOPV[:, c, :], lambda c: TOPI[:, c, :], HC)
            v.e.tensor_copy(TOPF, TOPI).then_inc(*v.count())
            pair = TOPV.rearrange("p (h c) k -> p h c k", c=2)
            v.e.tensor_tensor(CAND.rearrange("p h (a b) -> p h a b", a=TOPK),
                              pair[:, :, 0, :].unsqueeze(3).broadcast_to([P, PEER_HEADS, TOPK, TOPK]),
                              pair[:, :, 1, :].unsqueeze(2).broadcast_to([P, PEER_HEADS, TOPK, TOPK]), ALU.add) \
                .then_inc(*v.count())
            BI = BESTI.rearrange("p (h k) -> p h k", h=PEER_HEADS)
            if t:
                v.e.wait_ge(*v.at(f"hk_t{t - 1}"))
            best(lambda c: CAND[:, c, :], lambda c: CAND2[:, c, :], lambda c: BESTV[:, c, :], lambda c: BI[:, c, :],
                 PEER_HEADS)
            v.e.tensor_scalar(KI[:, 0, :], BESTI, 4, None, ALU.logical_shift_right).then_inc(*v.count())
            v.e.tensor_scalar(KI[:, 1, :], BESTI, 15, None, ALU.bitwise_and).then_inc(*v.count())
            v.e.tensor_tensor(OFF.rearrange("p (h k) -> p h k", h=PEER_HEADS), BESTV,
                              BESTV[:, :, 0:1].broadcast_to([P, PEER_HEADS, TOPK]), ALU.subtract) \
                .then_inc(*v.count(f"best_off{t}"))
            v.e.wait_ge(*v.mine())
            v.e.tensor_copy(KF_, KI).then_inc(*v.count())
            topf = TOPF.rearrange("p (h c) k -> p h c k", c=2)
            E4 = EQ.rearrange("p (h k i) -> p h k i", h=PEER_HEADS, k=TOPK)
            E3 = EQ.rearrange("p (n i) -> p n i", i=TOPK)
            for c in range(2):
                v.e.wait_ge(*v.mine())
                v.e.tensor_tensor(E3, bc16(KF_[:, c, :]), IOTA16.unsqueeze(1).broadcast_to([P, P, TOPK]),
                                  ALU.is_equal).then_inc(*v.count())
                v.e.wait_ge(*v.mine())
                v.e.tensor_tensor(E4, E4, topf[:, :, c, :].unsqueeze(2).broadcast_to(
                    [P, PEER_HEADS, TOPK, TOPK]), ALU.mult).then_inc(*v.count())
                v.e.wait_ge(*v.mine())
                v.e.tensor_reduce(HKR[:, c, :], E3, AX.X, ALU.add).then_inc(*v.count())
            v.e.wait_ge(*v.at(f"best_exp{t}"))
            v.e.tensor_reduce(STAT[:, 0:8], BESTV, AX.X, ALU.add).then_inc(*v.count())
            v.e.wait_ge(*v.mine())
            v.e.reciprocal(STAT[:, 8:16], STAT[:, 0:8]).then_inc(*v.count())
            v.e.wait_ge(*v.mine())
            v.e.tensor_tensor(HKR[:, 2, :].rearrange("p (h k) -> p h k", h=PEER_HEADS), BESTV,
                              STAT[:, 8:16].unsqueeze(2).broadcast_to([P, PEER_HEADS, TOPK]), ALU.mult) \
                .then_inc(*v.count(f"hkr{t}"))
            v.e.wait_ge(*v.at(f"hk_t{t}"))
            v.e.tensor_copy(HK[:, :, t * P:(t + 1) * P], PS[:, t, 0:3 * P].rearrange("p (c n) -> p c n", c=3)) \
                .then_inc(*v.count("hk_read" if t else None))

        def bc16(ap):
            return ap.unsqueeze(2).broadcast_to([P, ap.shape[1], TOPK])
        def second_loads(sp):
            sp.e.dma_start(MEMX, dram["mem_2"].rearrange("b (t p) d -> p (b t) d", p=P)) \
                .then_inc(*sp.count("mem_in", "dma_start"))
            with sp.loop("second", DEPTH) as l:
                sp.e.wait_ge(*sp.at("second_start"))
                weight_blocks(sp, SECOND_BLOCKS, "s", l)

        def second_pool(p):
            with p.loop("second", DEPTH) as l:
                p.e.wait_ge(*p.at("second_start"))
                p.e.wait_ge(*p.mine())
                p.e.tensor_tensor(LB[:, 15:16], COMMON[:, 0:1], COMMON[:, 0:1], ALU.add).then_inc(*p.count())
                p.e.dma_start(SPAR[:, 0:N_SECOND],
                              bass.AP(tensor=dram["second_par"].tensor, offset=l * (P * N_SECOND),
                                      ap=[[N_SECOND, P], [1, N_SECOND]])) \
                    .then_inc(*p.count("second_params_in", "dma_params"))
            p.e.wait_ge(*p.at("second_end"))
            p.e.dma_start(FINAL, bass.AP(tensor=dram["final_norm_2"].tensor, offset=0, ap=[[0, P], [1, D]])) \
                .then_inc(*p.count("final_in", "dma_params"))

        def second_scalar(a, l):
            norm_scalar(a, "nm", MEMX, ["second_start", "mem_in"])
            for j in (0, 1):
                a.e.wait_ge(*a.at(f"s{j}_mm"))
                for b in range(2):
                    k = 4 * j + 2 * b
                    a.e.activation(MK[:, k:k + 2, :].rearrange("p k t -> p (k t)"),
                                   PS[:, 2 * (j % 2) + b, :], ACT.Copy).then_inc(*a.count(f"s{j}_ev" if b else None))
            for j in (2, 3):
                a.e.wait_ge(*a.at(f"s{j}_mm"))
                for t in range(TT):
                    a.e.activation(MV[:, t, (j - 2) * 512:(j - 1) * 512], PS[:, 2 * (j % 2) + t, :], ACT.Copy) \
                        .then_inc(*a.count(f"s{j}_ev" if t else None))
            norm_scalar(a, "nx", X, ["nm_done"])
            a.e.wait_ge(*a.at("s4_mm"))
            a.e.activation(ABC[:, 0:2, :].rearrange("p c t -> p (c t)"), PS[:, 0, :], ACT.Copy) \
                .then_inc(*a.count("ax_ev"))
            a.e.wait_ge(*a.at("s5_mm"))
            a.e.activation(ABC[:, 2:4, :].rearrange("p c t -> p (c t)"), PS[:, 2, :], ACT.Copy) \
                .then_inc(*a.count("s5_ev"))
            for j in range(6, 16):
                to, c0, func = ((QKVG, 0, ACT.Copy) if j == 6 else (QKVG, 512, ACT.Copy) if j == 7 else
                                (QKVG, 1024, ACT.Silu) if j == 8 else (ZG, 0, ACT.Gelu_apprx_tanh) if j == 9 else
                                (GT, (j - 10) * 512, ACT.Sigmoid))
                a.e.wait_ge(*a.at(f"s{j}_mm"))
                for t in range(TT):
                    a.e.activation(to[:, t, c0:c0 + 512], PS[:, 2 * (j % 2) + t, :], func) \
                        .then_inc(*a.count(f"s{j}_ev" if t else None))
            a.e.wait_ge(*a.at("ln_var"))
            a.e.activation(STAT[:, 100:102], STAT[:, 98:100], ACT.Sqrt).then_inc(*a.count("ln_sd"))
            a.e.wait_ge(*a.at("gn_var"))
            a.e.activation(STAT[:, 80:88], STAT[:, 72:80], ACT.Sqrt).then_inc(*a.count("gn_sd"))
            norm_scalar(a, "nq", X, ["s20_ev"])
            for j in (21, 22):
                a.e.wait_ge(*a.at(f"s{j}_mm"))
                for b in range(2):
                    k = 4 * (j - 21) + 2 * b
                    a.e.activation(QX[:, k:k + 2, :].rearrange("p k t -> p (k t)"),
                                   PS[:, 2 * (j % 2) + b, :], ACT.Copy).then_inc(*a.count(f"s{j}_ev" if b else None))
            a.e.wait_ge(*a.at("xa_max"))
            for t in range(TT):
                for h in range(4):
                    c = 4 * t + h
                    a.e.activation(SX[:, t, h, :], PS[:, 4 + 2 * t + h // 2, (h % 2) * T:(h % 2 + 1) * T],
                                   ACT.Exp, bias=STAT[:, 8 + c:9 + c], scale=1.0 / 16,
                                   accum_out=STAT[:, 16 + c:17 + c]).then_inc(*a.count("xa_exp" if c == 7 else None))
            for h in range(4):
                a.e.wait_ge(*a.at(f"ptx{h}"))
                a.e.activation(PTX[:, h, :, :].rearrange("p k t -> p (k t)"), PS[:, h, :], ACT.Copy) \
                    .then_inc(*a.count(f"ptx{h}_ev"))
            norm_scalar(a, "nf", X, ["s24_ev"])
            for n in range(D_FF // 256):
                j = 25 + n
                a.e.wait_ge(*a.at(f"s{j}_mm"))
                if n >= 2:
                    a.e.wait_ge(*a.at(f"s{j - 2}_ev"))
                a.e.activation(SILU[:, j % 2, :], PS[:, 2 * (j % 2), :], ACT.Silu).then_inc(*a.count(f"ff_silu{n}"))

        def second_tensor(pe, l):
            turn_tensor(pe, "nm", SCR, KD, ["nm_xn0", "nm_xn1"])
            pe.e.wait_ge(*pe.at("nm_done"))
            B = SECOND_BLOCKS
            for j in range(4):
                product(pe, "s", B, j, "channels" if j < 2 else "tokens", MT, 2 * (j % 2),
                        [f"s{j - 2}_ev"] if j >= 2 else [])
            turn_tensor(pe, "nx", SCR, KD, ["nx_xn0", "nx_xn1"])
            pe.e.wait_ge(*pe.at("nx_done"))
            for j in range(4, 16):
                product(pe, "s", B, j, "channels" if j < 6 else "tokens", HT, 2 * (j % 2), [f"s{j - 2}_ev"])
            turn_tensor(pe, "rq", QKR, 4, ["rot", "rot"])
            pe.e.wait_ge(*pe.at("rq_done"))
            for h in range(RET_HEADS):
                r = 64 * (h % 2)
                q, k = QKT2[r:r + 64, h // 2, :], QKT2[r:r + 64, 2 + h // 2, :]
                pe.e.matmul(PS[:, 4 + h, 0:T], k[:, 0:P], q, start=True, stop=True)
                m = pe.e.matmul(PS[:, 4 + h, T:T + P], k[:, P:T], q[:, P:T], start=True, stop=True)
            m.then_inc(*pe.count("ret_scores"))
            pe.e.wait_ge(*pe.at("ret_dec"))
            for h in range(RET_HEADS):
                o = slice(h * RET_V, (h + 1) * RET_V)
                v = [QKVG[:, t, 512 + h * RET_V:512 + (h + 1) * RET_V] for t in range(TT)]
                pe.e.matmul(PS[:, 4, o], DM[:, h, 0:P], v[0], start=True, stop=True)
                pe.e.matmul(PS[:, 5, o], DM[:, h, P:T], v[0], start=True, stop=False)
                m = pe.e.matmul(PS[:, 5, o], DM[:, h, T:T + P], v[1], start=False, stop=True)
            m.then_inc(*pe.count("ret_out"))
            pe.e.wait_ge(*pe.at("sg_norm"))
            for t in range(TT):
                for g in range(4):
                    m = pe.e.matmul(PS[:, 6, t * 256 + g * 64:t * 256 + (g + 1) * 64], WSM[:, g, :],
                                    VN[:, t, g * 64:(g + 1) * 64], start=True, stop=True)
            m.then_inc(*pe.count("sg_mm"))
            turn_tensor(pe, "rr", R, 4, ["ret_norm", "ret_norm"], ["sg_out"])
            turn_tensor(pe, "yc", YC, 2, ["sg_out", "sg_out"], ["rr_done"])
            product(pe, "s", B, 16, "tokens", YA, 0, ["conv_out", "s14_ev", "s15_ev"])
            product(pe, "s", B, 17, "tokens", RT, 4, ["yc_done"])
            product(pe, "s", B, 18, "tokens", YCT, 0, ["s16_ev"])
            turn_tensor(pe, "mg", MER, KD, ["merged", "merged"])
            pe.e.wait_ge(*pe.at("mg_done"))
            for j in (19, 20):
                product(pe, "s", B, j, "tokens", HT, 2 * (j % 2), [f"s{18}_ev"])
            turn_tensor(pe, "nq", SCR, KD, ["nq_xn0", "nq_xn1"])
            pe.e.wait_ge(*pe.at("nq_done"))
            for j in (21, 22):
                product(pe, "s", B, j, "channels", HT, 2 * (j % 2), [f"s{j - 2}_ev"])
            pe.e.wait_ge(*pe.at("s21_ev"))
            pe.e.wait_ge(*pe.at("s22_ev"))
            for t in range(TT):
                for h in range(4):
                    for c in range(2):
                        m = pe.e.matmul(PS[:, 4 + 2 * t + h // 2, (h % 2) * T:(h % 2 + 1) * T],
                                        QX[:, 2 * h + c, t * P:(t + 1) * P], MK[:, 2 * h + c, :], start=c == 0,
                                        stop=c == 1)
            m.then_inc(*pe.count("xa_scores"))
            pe.e.wait_ge(*pe.at("xa_probs"))
            for h in range(4):
                for k in range(TT):
                    for t in range(TT):
                        m = pe.e.transpose(PS[:, h, k * T + t * P:k * T + (t + 1) * P],
                                           SX[:, t, h, k * P:(k + 1) * P], IDENT)
                m.then_inc(*pe.count(f"ptx{h}"))
            for h in range(4):
                pe.e.wait_ge(*pe.at(f"ptx{h}_ev"))
                for c in range(2):
                    for k in range(TT):
                        m = pe.e.matmul(PS[:, 4 + h, c * T:(c + 1) * T],
                                        MV[:, k, h * 256 + c * P:h * 256 + (c + 1) * P], PTX[:, h, k, :],
                                        start=k == 0, stop=k == TT - 1)
                m.then_inc(*pe.count(f"xa_out{h}"))
            pe.e.wait_ge(*pe.at("xa_done"))
            for j in (23, 24):
                product(pe, "s", B, j, "tokens", HT, 2 * (j % 2))
            turn_tensor(pe, "nf", SCR, KD, ["nf_xn0", "nf_xn1"])
            pe.e.wait_ge(*pe.at("nf_done"))
            for n in range(D_FF // 256):
                j = 25 + n
                pe.e.wait_ge(*pe.at(f"s{j}_in"))
                pe.e.wait_ge(*pe.at(f"s{j - 2}_ev"))
                W = RING[:, j % 2, :].rearrange("p (k w) -> p k w", w=256)
                for half in range(2):
                    for c in range(2):
                        for kc in range(KD):
                            m = pe.e.matmul(PS[:, 2 * (j % 2) + half, c * T:(c + 1) * T],
                                            W[:, half * KD + kc, c * P:(c + 1) * P], HT[:, kc, :], start=kc == 0,
                                            stop=kc == KD - 1)
                m.then_inc(*pe.count(f"s{j}_mm"))
            for n in range(-(-KF // 4)):
                j = 36 + n
                product(pe, "s", B, j, "tokens", FF[:, 4 * n:, :], 4, ["s35_ev"], n == 0, 4 * n + 4 >= KF)

        def second_vector(v, l):
            cos = PHASE[:, 4 * (T + P):4 * (T + P) + 64].rearrange("p (t n) -> p t n", t=TT)
            sin = PHASE[:, 4 * (T + P) + 64:4 * (T + P) + 128].rearrange("p (t n) -> p t n", t=TT)
            tri = PHASE[:, 4 * (T + P) + 128:4 * (T + P) + 128 + P]
            v.e.wait_ge(*v.mine())
            v.e.memset(Z3[:, :, 0:2], 0.0).then_inc(*v.count("second_start"))
            norm_vector(v, "nm", MEMX)
            v.e.wait_ge(*v.at("second_params_in"))
            turn_vector(v, "nm", MT, KD, spar("norm_mem"))
            norm_vector(v, "nx", X)
            turn_vector(v, "nx", HT, KD, spar("norm_mix"))
            v.e.wait_ge(*v.at("ax_ev"))
            v.e.wait_ge(*v.at("s4_mm"))
            v.e.tensor_tensor(Z3[:, :, 2:T + 2], PS[:, 1, :].rearrange("p (c t) -> p c t", c=2),
                              ABC[:, 0:2, :], ALU.mult).then_inc(*v.count("s4_ev"))
            v.e.wait_ge(*v.mine())
            for k in range(3):
                for c in range(2):
                    w = spar("conv_w", 2 * k + c, 2 * k + c + 1)
                    if k == 0:
                        v.e.tensor_scalar(YA[:, c, :], Z3[:, c, 0:T], w, None, ALU.mult).then_inc(*v.count())
                    else:
                        v.e.wait_ge(*v.mine(1))
                        v.e.scalar_tensor_tensor(YA[:, c, :], Z3[:, c, k:k + T], w, YA[:, c, :], ALU.mult,
                                                 ALU.add).then_inc(*v.count())
            v.e.wait_ge(*v.mine())
            v.e.wait_ge(*v.at("s5_ev"))
            v.e.tensor_tensor(YA, YA, ABC[:, 2:4, :], ALU.mult).then_inc(*v.count("conv_out"))
            v.e.tensor_tensor(WSM, spar("sg_w").rearrange("p (g n) -> p g n", g=4),
                              tri.unsqueeze(1).broadcast_to([P, 4, P]), ALU.mult).then_inc(*v.count())
            v.e.wait_ge(*v.at("s6_ev"))
            parts = MER.rearrange("p t (m g n) -> p (t m) g n", m=4, n=32)
            C, S = ([w[:, t, :].unsqueeze(1).broadcast_to([P, 8, 32]) for t in range(TT)] for w in (cos, sin))
            for t in range(TT):
                x = QKVG[:, t, 0:512].rearrange("p (g c n) -> p g c n", g=8, c=2)
                for n, (c, w) in enumerate(((0, C), (1, S), (0, S), (1, C))):
                    v.e.tensor_tensor(parts[:, 4 * t + n, :, :], x[:, :, c, :], w[t], ALU.mult).then_inc(*v.count())
            v.e.wait_ge(*v.mine())
            for t in range(TT):
                to = QKR[:, t, :].rearrange("p (g c n) -> p g c n", g=8, c=2)
                for c, op in ((0, ALU.subtract), (1, ALU.add)):
                    v.e.tensor_tensor(to[:, :, c, :], parts[:, 4 * t + 2 * c, :, :],
                                      parts[:, 4 * t + 2 * c + 1, :, :], op) \
                        .then_inc(*v.count("rot" if t and c else None))
            turn_vector(v, "rq", QKT2, 4, None)
            v.e.wait_ge(*v.at("ret_scores"))
            for h in range(RET_HEADS):
                v.e.tensor_tensor(DM[:, h, :], PS[:, 4 + h, 0:T + P],
                                  PHASE[:, h * (T + P):(h + 1) * (T + P)], ALU.mult) \
                    .then_inc(*v.count("ret_dec" if h == 3 else None))

            def center(tag, src, dst, n, at):
                for i in range(n):
                    v.e.bn_stats(MER[:, 0, 512 + 8 * i:518 + 8 * i], src(i)).then_inc(*v.count())
                v.e.wait_ge(*v.mine())
                v.e.tensor_copy(LB[:, 14:15], COMMON[:, 0:1]).then_inc(*v.count())
                for i in range(n):
                    v.e.bn_aggr(MER[:, 0, 640 + 2 * i:642 + 2 * i], MER[:, 0, 512 + 8 * i:518 + 8 * i]) \
                        .then_inc(*v.count())
                v.e.wait_ge(*v.mine())
                v.e.tensor_scalar(STAT[:, at:at + n],
                                  MER[:, 0, 640:640 + 2 * n].rearrange("p (i c) -> p i c", c=2)[:, :, 1],
                                  EPS, None, ALU.add).then_inc(*v.count(f"{tag}_var"))
                v.e.wait_ge(*v.at(f"{tag}_sd"))
                sd = at + (n if n > 2 else 2)
                v.e.reciprocal(STAT[:, sd:sd + n], STAT[:, sd:sd + n]).then_inc(*v.count())
                v.e.wait_ge(*v.mine())
                for i in range(n):
                    v.e.tensor_scalar(dst(i), src(i), MER[:, 0, 640 + 2 * i:641 + 2 * i],
                                      STAT[:, sd + i:sd + i + 1], ALU.subtract, ALU.mult).then_inc(*v.count())
                v.e.wait_ge(*v.mine())

            v.e.wait_ge(*v.at("s9_ev"))
            center("ln", lambda t: ZG[:, t, 256:512], lambda t: VN[:, t, :], TT, 98)
            v.e.tensor_tensor(VN, VN, spar("sg_ln").unsqueeze(1).broadcast_to([P, TT, 256]), ALU.mult) \
                .then_inc(*v.count("sg_norm"))
            v.e.wait_ge(*v.at("ret_out"))
            v.e.wait_ge(*v.mine())
            center("gn", lambda i: PS[:, 4 + i // 4, (i % 4) * P:(i % 4 + 1) * P],
                   lambda i: R[:, i // 4, (i % 4) * P:(i % 4 + 1) * P], 8, 72)
            v.e.wait_ge(*v.at("s8_ev"))
            v.e.tensor_tensor(R, R, QKVG[:, :, 1024:1536], ALU.mult).then_inc(*v.count("ret_norm"))
            v.e.wait_ge(*v.at("sg_mm"))
            for g in range(4):
                o = slice(g * 64, (g + 1) * 64)
                v.e.scalar_tensor_tensor(YC[:, :, o], PS[:, 6, :].rearrange("p (t n) -> p t n", t=TT)[:, :, o],
                                         spar("sg_b", g, g + 1), ZG[:, :, o], ALU.add, ALU.mult) \
                    .then_inc(*v.count("sg_out" if g == 3 else None))
            turn_vector(v, "rr", RT, 4, spar("ret_gn"))
            turn_vector(v, "yc", YCT, 2, None)
            v.e.wait_ge(*v.at("s15_ev"))
            for n, (j, bank) in enumerate(((16, 0), (17, 4), (18, 0))):
                v.e.wait_ge(*v.at(f"s{j}_mm"))
                v.e.wait_ge(*v.mine())
                for t in range(TT):
                    for half in range(2):
                        o = slice(half * 512, (half + 1) * 512)
                        to = (MER if n == 0 else SCR)[:, t, o]
                        v.e.tensor_tensor(to, PS[:, bank + 2 * t + half, :],
                                          GT[:, t, n * D + half * 512:n * D + (half + 1) * 512], ALU.mult) \
                            .then_inc(*v.count(f"s{j}_ev" if t and half else None))
                if n:
                    v.e.wait_ge(*v.mine())
                    v.e.tensor_tensor(MER, MER, SCR, ALU.add).then_inc(*v.count("merged" if n == 2 else None))
            turn_vector(v, "mg", HT, KD, None)
            add_to_x(v, "s", SECOND_BLOCKS, (19, 20))
            v.e.wait_ge(*v.mine())
            norm_vector(v, "nq", X)
            turn_vector(v, "nq", HT, KD, spar("norm_xa"))
            v.e.wait_ge(*v.at("xa_scores"))
            for b in range(4):
                v.e.tensor_reduce(STAT[:, 2 * b:2 * b + 2], PS[:, 4 + b, :].rearrange("p (h m) -> p h m", h=2),
                                  AX.X, ALU.max, negate=True).then_inc(*v.count())
            v.e.wait_ge(*v.mine())
            v.e.tensor_scalar(STAT[:, 8:16], STAT[:, 0:8], 1.0 / 16, None, ALU.mult).then_inc(*v.count("xa_max"))
            v.e.wait_ge(*v.at("xa_exp"))
            v.e.reciprocal(STAT[:, 24:32], STAT[:, 16:24]).then_inc(*v.count())
            v.e.wait_ge(*v.mine())
            flat = SX.rearrange("p t h m -> p (t h) m")
            v.e.tensor_tensor(flat, flat, STAT[:, 24:32].unsqueeze(2).broadcast_to([P, 8, T]), ALU.mult) \
                .then_inc(*v.count("xa_probs"))
            for h in range(4):
                v.e.wait_ge(*v.at(f"xa_out{h}"))
                v.e.tensor_copy(HT[:, 2 * h:2 * h + 2, :].rearrange("p k t -> p (k t)"), PS[:, 4 + h, :]) \
                    .then_inc(*v.count("xa_done" if h == 3 else None))
            add_to_x(v, "s", SECOND_BLOCKS, (23, 24))
            v.e.wait_ge(*v.mine())
            norm_vector(v, "nf", X)
            turn_vector(v, "nf", HT, KD, spar("norm_ffn"))
            for n in range(D_FF // 256):
                j = 25 + n
                v.e.wait_ge(*v.at(f"ff_silu{n}"))
                v.e.tensor_tensor(FF[:, 2 * n:2 * n + 2, :].rearrange("p k t -> p (k t)"),
                                  PS[:, 2 * (j % 2) + 1, :], SILU[:, j % 2, :], ALU.mult) \
                    .then_inc(*v.count(f"s{j}_ev"))
            v.e.wait_ge(*v.at("s41_mm"))
            for t in range(TT):
                for half in range(2):
                    x = X[:, t, half * 512:(half + 1) * 512]
                    v.e.tensor_tensor(x, PS[:, 4 + 2 * t + half, :], x, ALU.add) \
                        .then_inc(*v.count("second_end" if t and half else None))

        @block.sync
        def _(eng):
            sp = Program(eng, "sync", steps)
            eng.dma_start(X[:, :, :], dram["x"].rearrange("b (t p) d -> p (b t) d", p=P)) \
                .then_inc(*sp.count(None, "dma_start"))
            eng.dma_start(COMMON[:, :], dram["common"]).then_inc(*sp.count(None, "dma_start"))
            eng.dma_start(PHASE[:, 0:N_HYBRID_CONST], dram["hybrid_const"]).then_inc(*sp.count(None, "dma_start"))
            eng.dma_start(STAT[0:BUCKETS, 0:AT_HEADS], dram["rel_bias"]).then_inc(*sp.count(None, "dma_start"))
            eng.dma_start(LB[:, 0:4], dram["lower_bounds"]).then_inc(*sp.count("start_in", "dma_start"))
            with sp.loop("hybrid", DEPTH) as l:
                sp.e.wait_ge(*sp.at("hybrid_start"))
                weight_blocks(sp, HYBRID_BLOCKS, "h", l)
                n = len(HYBRID_BLOCKS)
                for b in range(2):
                    sp.e.wait_ge(*sp.at(f"h{n - 2 + b}_mm"))
                    peer_block(sp, "down", b, b, l, f"down_first{b}")
                    peer_block(sp, "up", b, b, l, f"up_first{b}")
                with sp.loop("peer", NKEYS // 4 - 1) as i:
                    sp.e.wait_ge(*sp.at("out1", back=1))
                    peer_block(sp, "down", 2 * i + 2, 0, l, "down0")
                    sp.e.wait_ge(*sp.at("act_in1"))
                    peer_block(sp, "down", 2 * i + 3, 1, l, "down1")
                    sp.e.wait_ge(*sp.at("out0"))
                    peer_block(sp, "up", 2 * i + 2, 0, l, "up0")
                    sp.e.wait_ge(*sp.at("out1"))
                    peer_block(sp, "up", 2 * i + 3, 1, l, "up1")
            sp.e.wait_ge(*sp.at("hybrid_end"))
            eng.dma_start(PHASE[:, 0:N_SECOND_CONST], dram["second_const"]) \
                .then_inc(*sp.count("second_const_in", "dma_const"))
            second_loads(sp)
            sp.e.wait_ge(*sp.at("result"))
            eng.dma_start(out.rearrange("b (t p) d -> p (b t) d", p=P), SCR) \
                .then_inc(*sp.count("out_done", "dma_out"))
            sp.e.wait_ge(*sp.at("out_done"))

        @block.gpsimd
        def _(eng):
            p = Program(eng, "pool", steps)
            p.e.wait_ge(*p.at("start_in"))
            p.e.tensor_tensor(LB[:, 15:16], COMMON[:, 0:1], COMMON[:, 0:1], ALU.add).then_inc(*p.count())
            p.e.wait_ge(*p.at("bias_sb"))
            eng.dma_start(bias_rows, SCR[0:AT_HEADS, 0, 0:REL]).then_inc(*p.count("bias_out", "dma_bias_out"))
            hybrid_pool(p)
            second_pool(p)

        @block.scalar
        def _(eng):
            a = Program(eng, "scalar", steps)
            a.e.wait_ge(*a.at("lower_off"))
            eng.activation(LB[:, 6:10], LB[:, 6:10], ACT.Exp).then_inc(*a.count("lower_exp"))
            a.e.wait_ge(*a.at("bias_mm"))
            eng.activation(SCR[0:AT_HEADS, 0, 0:REL], PS[0:AT_HEADS, 6, 0:REL], ACT.Copy) \
                .then_inc(*a.count("bias_sb"))
            a.e.wait_ge(*a.at("bias_out"))
            with a.loop("hybrid", DEPTH) as l:
                hybrid_scalar(a, l)
            a.e.wait_ge(*a.at("hybrid_end"))
            with a.loop("second", DEPTH) as l:
                second_scalar(a, l)
            norm_scalar(a, "end", X, ["second_end"])

        @block.tensor
        def _(eng):
            pe = Program(eng, "tensor", steps)
            pe.e.wait_ge(*pe.at("start_in"))
            eng.matmul(PS[0:AT_HEADS, 6, 0:REL], STAT[0:BUCKETS, 0:AT_HEADS],
                       PHASE[0:BUCKETS, 2 * (T + P):2 * (T + P) + REL], start=True, stop=True) \
                .then_inc(*pe.count("bias_mm"))
            with pe.loop("hybrid", DEPTH) as l:
                hybrid_tensor(pe, l)
            pe.e.wait_ge(*pe.at("second_const_in"))
            with pe.loop("second", DEPTH) as l:
                second_tensor(pe, l)

        @block.vector
        def _(eng):
            v = Program(eng, "vector", steps)
            v.e.wait_ge(*v.at("start_in"))
            raw = LB[:, 0:4].rearrange("p (l c) -> p l c", l=DEPTH)
            off = LB[:, 6:10].rearrange("p (l c) -> p l c", l=DEPTH)
            eng.tensor_tensor(LB[:, 4:6], LB[:, 0:2], LB[:, 2:4], ALU.max).then_inc(*v.count())
            v.e.wait_ge(*v.mine())
            eng.tensor_tensor(off, raw, LB[:, 4:6].unsqueeze(1).broadcast_to([P, DEPTH, 2]), ALU.subtract) \
                .then_inc(*v.count("lower_off"))
            v.e.wait_ge(*v.at("lower_exp"))
            eng.tensor_tensor(LB[:, 4:6], LB[:, 6:8], LB[:, 8:10], ALU.add).then_inc(*v.count())
            v.e.wait_ge(*v.mine())
            eng.reciprocal(LB[:, 4:6], LB[:, 4:6]).then_inc(*v.count())
            v.e.wait_ge(*v.mine())
            eng.tensor_tensor(off, off, LB[:, 4:6].unsqueeze(1).broadcast_to([P, DEPTH, 2]), ALU.mult) \
                .then_inc(*v.count())
            v.e.wait_ge(*v.mine())
            eng.tensor_tensor(LB[:, 10:12], LB[:, 6:8], LB[:, 6:8], ALU.subtract).then_inc(*v.count())
            eng.tensor_tensor(LB[:, 12:14], LB[:, 6:8], LB[:, 8:10], ALU.add).then_inc(*v.count())
            v.e.wait_ge(*v.mine())
            eng.tensor_tensor(LB[:, 12:14], LB[:, 12:14], LB[:, 6:8], ALU.subtract).then_inc(*v.count())
            v.e.wait_ge(*v.at("bias_mm"))
            with v.loop("hybrid", DEPTH) as l:
                hybrid_vector(v, l)
            v.e.wait_ge(*v.at("second_const_in"))
            v.e.wait_ge(*v.at("mem_in"))
            with v.loop("second", DEPTH) as l:
                second_vector(v, l)
            norm_vector(v, "end", X)
            v.e.wait_ge(*v.mine())
            v.e.wait_ge(*v.at("final_in"))
            eng.tensor_tensor(SCR, SCR, FINAL.unsqueeze(1).broadcast_to([P, TT, D]), ALU.mult) \
                .then_inc(*v.count("result"))


def columns(rows):
    return np.ascontiguousarray(rows.reshape(DEPTH, -1, P).transpose(0, 2, 1))


def layouts(i):
    i = {k: np.asarray(v) for k, v in i.items()}
    a = {k: i[k] for k in ("x", "w_in", "w_out", "peer_w_query", "peer_up", "rel_bias", "mem_2", "w_in_2", "w_a_out_2",
                           "w_b_out_2", "w_c_out_2", "w_o_2", "xa_q_2", "xa_k_2", "xa_v_2", "xa_o_2", "w1_2", "w3_2",
                           "w2_2", "final_norm_2")}
    a["peer_down"] = i["peer_down"].reshape(DEPTH, NKEYS, NKEYS, KD, P).transpose(0, 2, 4, 3, 1)
    a["sub_keys"] = i["peer_sub_keys"].transpose(0, 1, 3, 2).reshape(DEPTH, P, NKEYS)
    a["lower_bounds"] = i["hgrn_lower_bounds"].reshape(DEPTH * 2, P).T

    def rows(name, n):
        out = np.zeros((DEPTH, P, 1), np.float32)
        out[:, 0:n, 0] = i[name]
        return out

    parts = {
        "attn_norm": columns(i["attn_norm_w"]), "ffn_norm": columns(i["ffn_norm_w"]),
        "mix_norm": columns(np.concatenate([np.tile(i["hgrn_norm_w"], (1, HG_HEADS)),
                                            np.ones((DEPTH, AT_W), np.float32), i["ssm_norm_w"]], axis=1)),
        "q_norm": columns(np.tile(i["q_norm_w"], (1, 2))), "k_norm": columns(np.tile(i["k_norm_w"], (1, 2))),
        "conv_w": columns(i["ssm_conv_w"].reshape(DEPTH, -1)), "conv_b": columns(i["ssm_conv_b"]),
        "dt_bias": rows("ssm_dt_bias", SS_HEADS), "a_log": rows("ssm_a_log", SS_HEADS),
        "d_skip": np.repeat(i["ssm_d"][:, None, :], P, axis=1),
    }
    a["hybrid_par"] = np.concatenate([parts[k] for k in HYBRID_PARAMS], axis=2)
    parts = {
        "norm_mix": columns(i["norm_mix_2"]), "norm_xa": columns(i["norm_xa_2"]), "norm_mem": columns(i["norm_mem_2"]),
        "norm_ffn": columns(i["norm_ffn_2"]), "ret_gn": columns(i["ret_gn_2"]),
        "conv_w": columns(i["conv_w_2"].reshape(DEPTH, -1)), "sg_b": i["sg_b_2"].transpose(0, 2, 1),
        "sg_ln": np.repeat(i["sg_ln_2"][:, None, :], P, axis=1),
        "sg_w": i["sg_w_2"].transpose(0, 3, 1, 2).reshape(DEPTH, P, 512),
    }
    a["second_par"] = np.concatenate([parts[k] for k in SECOND_PARAMS], axis=2)
    a.update(constants())
    return {k: np.ascontiguousarray(v) for k, v in a.items()}


def kernel(**inputs):
    import concourse.bacc as bacc
    from concourse.bass_utils import run_bass_kernel_spmd as run

    arrays = layouts(inputs)

    def program(steps):
        nc = bacc.Bacc("TRN2", target_bir_lowering=False, num_devices=1)
        dram = {k: nc.dram_tensor(f"in_{k}", v.shape, F32, kind="ExternalInput").ap() for k, v in arrays.items()}
        out = nc.dram_tensor("out_x", (1, T, D), F32, kind="ExternalOutput").ap()
        build(nc, dram, out, steps)
        return nc

    counts = Steps()
    program(counts)
    nc = program(Steps(counts))
    r = run(nc, [{f"in_{k}": v for k, v in arrays.items()}], core_ids=[0])
    return r.results[0]["out_x"]
```

```python
from collections import defaultdict
from contextlib import ExitStack, contextmanager

import numpy as np

import concourse.bass as bass
from concourse import mybir

ALU = mybir.AluOpType
ACT = mybir.ActivationFunctionType
AX = mybir.AxisListType
F32 = mybir.dt.float32
F32R = mybir.dt.float32r
U32 = mybir.dt.uint32

P = 128
T = 256
D = 1024
TT = T // P
KD = D // P
DEPTH = 2
EPS = 1e-6
NEG = -1e30
BIG = 3e38

HEAD = 64
HG_HEADS, AT_HEADS, SS_HEADS = 4, 6, 6
HG_W, AT_W, SS_W = HG_HEADS * HEAD, AT_HEADS * HEAD, SS_HEADS * HEAD
GROUPS = 2
CONV_CH = SS_W + 2 * GROUPS * 128
CONV_TILES = CONV_CH // P
IN1 = 4 * HG_W + 3 * AT_W + SS_W + CONV_CH + SS_HEADS
BUCKETS, MAX_DISTANCE = 32, 2048
REL = T + P - 1
NKEYS, TOPK, PEER_HEADS = 128, 16, 8
HC = PEER_HEADS * 2
VGROUP = 4
SCANS = HG_W // (2 * VGROUP)
BLOCKS = NKEYS // 2
GROUP = 8
GATES = T * NKEYS // 2
IN2 = 3 * 256 + 2 * 256 + 2 * 512 + 512 + 3 * D
RET_HEADS, RET_V = 4, 128
D_FF = 2816
KF = D_FF // P

HYBRID_BLOCKS = [
    ("w_in", 0, KD, 0, 512), ("w_in", 0, KD, 512, 256), ("w_in", 0, KD, 768, 512), ("w_in", 0, KD, 1280, 512),
    ("w_in", 0, KD, 1792, 512), ("w_in", 0, KD, 2304, 256), ("w_in", 0, KD, 2560, 512), ("w_in", 0, KD, 3072, 390),
    ("w_out", 0, KD, 0, 512), ("w_out", 0, KD, 512, 512),
    ("peer_w_query", 0, KD, 0, 512), ("peer_w_query", 0, KD, 512, 512),
]
SECOND_BLOCKS = (
    [("xa_k_2", 0, KD, 0, 512), ("xa_k_2", 0, KD, 512, 512), ("xa_v_2", 0, KD, 0, 512), ("xa_v_2", 0, KD, 512, 512)]
    + [("w_in_2", 0, KD, 0, 512), ("w_in_2", 0, KD, 512, 256)]
    + [("w_in_2", 0, KD, 768 + 512 * n, 512) for n in range(10)]
    + [("w_a_out_2", 0, 2, 0, D), ("w_b_out_2", 0, 4, 0, D), ("w_c_out_2", 0, 2, 0, D)]
    + [("w_o_2", 0, KD, 0, 512), ("w_o_2", 0, KD, 512, 512)]
    + [("xa_q_2", 0, KD, 0, 512), ("xa_q_2", 0, KD, 512, 512), ("xa_o_2", 0, KD, 0, 512), ("xa_o_2", 0, KD, 512, 512)]
    + [("w1w3", 0, KD, 256 * n, 256) for n in range(D_FF // 256)]
    + [("w2_2", 4 * n, min(4, KF - 4 * n), 0, D) for n in range(-(-KF // 4))]
)
BLOCK_AT = {5: 4, 9: 5, 13: 6, 15: 7, 19: 8, 23: 9}
COLUMNS = {"w_in": IN1, "w_out": D, "peer_w_query": D, "w_in_2": IN2, "w_a_out_2": D, "w_b_out_2": D, "w_c_out_2": D,
           "w_o_2": D, "xa_q_2": D, "xa_k_2": D, "xa_v_2": D, "xa_o_2": D, "w1_2": D_FF, "w3_2": D_FF, "w2_2": D}
ROWS = {"w_a_out_2": 256, "w_b_out_2": 512, "w_c_out_2": 256, "w2_2": D_FF}

HYBRID_PARAMS = {}
for _name, _n in [("attn_norm", KD), ("ffn_norm", KD), ("mix_norm", KD), ("q_norm", 1), ("k_norm", 1),
                  ("conv_w", 4 * CONV_TILES), ("conv_b", CONV_TILES), ("dt_bias", 1), ("a_log", 1), ("d_skip", SS_HEADS)]:
    HYBRID_PARAMS[_name] = (sum(n for _, n in HYBRID_PARAMS.values()), _n)
N_HYBRID = sum(n for _, n in HYBRID_PARAMS.values())
SECOND_PARAMS = {}
for _name, _n in [("norm_mix", KD), ("norm_xa", KD), ("norm_mem", KD), ("norm_ffn", KD), ("ret_gn", 4),
                  ("conv_w", 6), ("sg_b", 4), ("sg_ln", 256), ("sg_w", 512)]:
    SECOND_PARAMS[_name] = (sum(n for _, n in SECOND_PARAMS.values()), _n)
N_SECOND = sum(n for _, n in SECOND_PARAMS.values())
N_COMMON = 3 * P + 16 + 2
N_HYBRID_CONST = 2 * (T + P) + REL
N_SECOND_CONST = 4 * (T + P) + 2 * TT * 32 + P
N_PHASE_CONST = max(N_HYBRID_CONST, N_SECOND_CONST)


class Steps:

    def __init__(self, before=None):
        self.known = before
        self.marks, self.per, self.turns, self.semaphores = {}, {}, {}, {}


class Program:

    def __init__(self, engine, own_name, steps):
        self.e, self.own_name, self.steps = engine, own_name, steps
        self.path, self.counts = [], defaultdict(int)

    def count(self, name=None, stream=None):
        counted = stream or self.own_name
        self.counts[counted] += 1
        if name:
            assert name not in self.steps.marks, name
            self.steps.marks[name] = (counted, [(loop, base[counted]) for loop, _, base in self.path],
                                      self.counts[counted])
        return self.steps.semaphores[counted], 16 if stream else 1

    @contextmanager
    def loop(self, name, turns):
        base = self.counts
        self.steps.turns[name] = turns
        with self.e.Fori(0, turns) as i:
            self.path.append((name, i, base))
            self.counts = defaultdict(int)
            yield i
        for counted, n in self.counts.items():
            self.steps.per[name, counted] = n
            base[counted] += turns * n
        self.path.pop()
        self.counts = base

    def value(self, counted, loops, value, back=0):
        known = self.steps.known
        semaphore = self.steps.semaphores[counted]
        if known is None:
            return semaphore, 1
        mine = {name: i for name, i, _ in self.path}
        shared = [loop for loop, _ in loops if loop in mine]
        moving = []
        for loop, base in loops:
            per = known.per[loop, counted]
            value += base
            if loop in mine:
                moving.append((mine[loop], per))
            else:
                value += (known.turns[loop] - 1) * per
            if back and loop == shared[-1]:
                value -= back * per
        assert value > 0, (counted, loops, value)
        unit = 16 if counted.startswith("dma") else 1
        total = value * unit
        for i, per in moving:
            total = i * (per * unit) + total
        return semaphore, total

    def at(self, name, back=0):
        if self.steps.known is None:
            return self.steps.semaphores["dma_start"], 1
        return self.value(*self.steps.known.marks[name], back)

    def mine(self, lag=0):
        loops = [(loop, base[self.own_name]) for loop, _, base in self.path]
        return self.value(self.own_name, loops, self.counts[self.own_name] - lag)


def constants():
    p = np.arange(P)[:, None]
    common = np.zeros((P, N_COMMON), np.float32)
    common[:, 0:P] = np.eye(P)
    common[:, P:2 * P] = np.eye(P)[::-1]
    common[:, 2 * P:3 * P] = np.arange(P)[None]
    common[:, 3 * P:3 * P + 16] = np.arange(16)[None]
    common[:, 3 * P + 16] = np.arange(P) < 64
    common[:, 3 * P + 17] = np.arange(P) >= 64

    def times(delta):
        n = (delta <= 128).astype(int) + (delta % 4 == 0) + (delta % 16 == 0)
        n = np.where(delta >= 0, n, 0)
        return np.where(n > 0, np.log(np.maximum(n, 1)), NEG).astype(np.float32)

    hybrid = np.zeros((P, N_HYBRID_CONST), np.float32)
    s = np.arange(T)[None]
    hybrid[:, 0:T] = times(P + p - s)
    hybrid[:, T:T + P] = times(p - s[:, :P])
    hybrid[:, T + P:2 * T + P] = np.where(s >= p, 0, NEG)
    hybrid[:, 2 * T + P:2 * (T + P)] = np.where(s[:, :P] >= p, 0, NEG)
    dist = np.maximum(T - 1 - np.arange(REL), 0)
    exact = BUCKETS // 2
    d = np.maximum(dist, 1).astype(np.float32)
    large = exact + (np.log(d / exact) / np.log(MAX_DISTANCE / exact) * (BUCKETS - exact)).astype(np.int32)
    bucket = np.where(dist < exact, dist, np.minimum(large, BUCKETS - 1))
    hybrid[0:BUCKETS, 2 * (T + P):] = np.arange(BUCKETS)[:, None] == bucket[None]

    second = np.zeros((P, N_SECOND_CONST), np.float32)
    gamma = 1.0 - np.exp2(-5.0 - np.arange(RET_HEADS))
    for h in range(RET_HEADS):
        at = h * (T + P)
        full = np.where(s >= p, np.exp(np.log(gamma[h]) * np.maximum(s - p, 0)), 0) * 64 ** -0.5
        second[:, at:at + T] = full
        second[:, at + T:at + T + P] = full[:, :P]
    at = 4 * (T + P)
    inv = np.float32(10000.0) ** (-np.arange(32, dtype=np.float32) / np.float32(32))
    angle = (np.arange(T, dtype=np.float32)[:, None] * inv[None].astype(np.float32)).reshape(TT, P, 32)
    second[:, at:at + 64] = np.cos(angle).transpose(1, 0, 2).reshape(P, 64)
    second[:, at + 64:at + 128] = np.sin(angle).transpose(1, 0, 2).reshape(P, 64)
    second[:, at + 128:] = s[:, :P] >= p
    return {"common": common, "hybrid_const": hybrid, "second_const": second}


def build(nc, dram, out, steps):
    ctx = ExitStack()
    with ctx:
        def sb(name, shape, dt=F32):
            return ctx.enter_context(nc.sbuf_tensor(name, shape, dt))

        for name in ("vector", "scalar", "tensor", "pool", "dma_w0", "dma_w1", "dma_down0", "dma_down1", "dma_up0",
                     "dma_up1", "dma_start", "dma_const", "dma_params", "dma_bias_out", "dma_bias_in", "dma_hi_out",
                     "dma_hi_in0", "dma_hi_in1", "dma_out"):
            steps.semaphores[name] = ctx.enter_context(nc.semaphore(name))

        X = sb("x_res", [P, TT, D])
        with nc.sbuf_tensor("h_t", [P, KD, T], F32) as HT:
            pass
        HT_LO = sb("h_t_lo", [P, KD, T], F32R)
        RING = sb("ring", [P, 2, 4096])
        COMMON = sb("common_sb", [P, N_COMMON])
        PHASE = sb("phase_sb", [P, N_PHASE_CONST])
        HPAR = sb("hybrid_params", [P, N_HYBRID])
        LB = sb("lower", [P, 16])
        STAT = sb("stat", [P, 128])
        with nc.sbuf_tensor("one_hot", [P, 3072], F32) as ONE:
            pass
        GELU = sb("gelu", [P, 2, 512])
        COEF_HI, COEF_LO = sb("coef_hi", [P, 2, 512], F32R), sb("coef_lo", [P, 2, 512], F32R)
        KEYS = sb("keys", [P, P])
        with nc.sbuf_tensor("arena", [P, 32768], F32) as ARENA:
            pass
        sb("arena_gates", [P, GATES])
        DOWN_HI, DOWN_LO = sb("down_hi", [P, 2, 2 * D], F32R), sb("down_lo", [P, 2, 2 * D], F32R)
        UP_HI, UP_LO = sb("up_hi", [P, 2, 2 * D], F32R), sb("up_lo", [P, 2, 2 * D], F32R)
        with nc.sbuf_tensor("hk_t", [P, 3, T], F32) as HK:
            pass
        HT_HI = sb("h_t_hi", [P, KD, T], F32R)
        PS = ctx.enter_context(nc.psum_tensor("ps", [P, 8, 512], F32))
        IDENT, FLIP = COMMON[:, 0:P], COMMON[:, P:2 * P]
        IOTA, IOTA16 = COMMON[:, 2 * P:3 * P], COMMON[:, 3 * P:3 * P + 16]
        HALVES = COMMON[:, 3 * P + 16:3 * P + 18]
        bias_rows = nc.dram_tensor("bias_rows", [AT_HEADS, REL], F32, kind="Internal").ap()
        hi_rows = nc.dram_tensor("hi_rows", [HG_W, T], F32, kind="Internal").ap()

        def carve(start, *sizes):
            pieces = []
            for n in sizes:
                pieces.append(ARENA[:, start:start + n])
                start += n
            assert start <= 32768, start
            return pieces, start

        def split(ap, pattern, **sizes):
            return ap.rearrange(pattern, **sizes)

        (SCR_,), after_scr = carve(0, TT * D)
        SCR = split(SCR_, "p (t d) -> p t d", t=TT)
        (HQ, FS, HI, KEY, FR_, U, XB, XC), scan_at = carve(
            after_scr, 2 * T, 2 * T, 2 * T, 2 * T, 2 * VGROUP * T, TT * 1792, CONV_TILES * (T + 3), CONV_TILES * T)
        HQ, FS, HI, KEY = (split(a, "p (c t) -> p c t", c=2) for a in (HQ, FS, HI, KEY))
        FR = split(FR_, "p (c v t) -> p c v t", c=2, v=VGROUP)
        QKN = split(FR_[:, 0:TT * 768], "p (t n) -> p t n", t=TT)
        U = split(U, "p (t n) -> p t n", t=TT)
        XB, XC = (split(a, "p (c t) -> p c t", c=CONV_TILES) for a in (XB, XC))
        scan_buffers, mix_at = carve(scan_at, *[2 * VGROUP * T] * 3, 3 * VGROUP * T)
        VB, KV, ST, QS = (split(a, "p (b v t) -> p b v t", v=VGROUP, t=T) for a in scan_buffers)
        (SCORE, PT, XDT, XSK, SZ), end = carve(scan_at, AT_HEADS * (T + P), AT_HEADS * 3 * P, *[TT * SS_W] * 3)
        assert end <= mix_at
        PT = split(PT, "p (h k t) -> p h k t", h=AT_HEADS, k=3)
        XDT, XSK, SZ = (split(a, "p (t n) -> p t n", t=TT) for a in (XDT, XSK, SZ))
        (MIX, BIAS, DT, DC, CD, HANK, QKT), _ = carve(mix_at, TT * D, AT_HEADS * (T + P), 6 * T, T, TT * 64,
                                                      AT_HEADS * T, 6 * T)
        MIX = split(MIX, "p (t d) -> p t d", t=TT)
        DT = split(DT, "p (k t) -> p k t", k=6)
        CD = split(CD, "p (t n) -> p t n", t=TT)
        HANK = split(HANK, "p (h i) -> p h i", h=AT_HEADS)
        QKT = split(QKT, "p (c t) -> p c t", c=6)
        SCORE1, BIAS1 = (split(a[:, 0:AT_HEADS * T], "p (h s) -> p h s", h=AT_HEADS) for a in (SCORE, BIAS))
        SCORE0, BIAS0 = (split(a[:, AT_HEADS * T:], "p (h s) -> p h s", h=AT_HEADS) for a in (SCORE, BIAS))
        DEC = split(SCORE, "p (h s) -> p h s", h=SS_HEADS)
        (PQ, SC, SC2, CAND, EQ, TOPV, TOPI, TOPF, BESTI, KI, KF_, BESTV, OFF), end = carve(
            after_scr, PEER_HEADS * T, TT * HC * P, HC * P, *[PEER_HEADS * 256] * 2, *[HC * TOPK] * 3, P,
            2 * P, 2 * P, TT * P, TT * P)
        assert end <= GATES
        PQ = split(PQ, "p (h t) -> p h t", h=PEER_HEADS)
        SC = split(SC, "p (t c n) -> p t c n", t=TT, c=HC)
        CAND, CAND2 = (split(a, "p (h n) -> p h n", h=PEER_HEADS) for a in (CAND, SC2))
        SC2 = split(SC2, "p (c n) -> p c n", c=HC)
        TOPV, TOPF = (split(a, "p (c k) -> p c k", c=HC) for a in (TOPV, TOPF))
        TOPI = split(TOPI.bitcast(U32), "p (c k) -> p c k", c=HC)
        BESTV, OFF = (split(a, "p (t n) -> p t n", t=TT) for a in (BESTV, OFF))
        BESTI = BESTI.bitcast(U32)
        KI = split(KI.bitcast(U32), "p (c n) -> p c n", c=2)
        KF_ = split(KF_, "p (c n) -> p c n", c=2)
        HKR = ONE[:, 0:TT * 3 * P].rearrange("p (t c n) -> p t c n", t=TT, c=3)
        G = split(ARENA[:, 0:GATES], "p (t n) -> p t n", t=T)
        HOT1 = ONE[:, 0:2048].rearrange("p (b j n) -> p b j n", b=2, j=GROUP)
        HOT2 = ONE[:, 2048:3072].rearrange("p (b j n) -> p b j n", b=2, j=GROUP)
        (SPAR, MEMX, MT, MK, MV, ABC, Z3, YA, QKVG, ZG, GT, MER, QKR, QKT2, DM, R, RT), _ = carve(
            after_scr, N_SECOND + N_SECOND % 2, TT * D, KD * T, KD * T, TT * D, 4 * T, 2 * (T + 2), 2 * T, TT * 1536,
            TT * 512, TT * 3 * D, TT * D, TT * 512, 4 * T, 4 * (T + P), TT * 512, 4 * T)
        WSM, VN, YC, YCT = (ONE[:, n * 512:(n + 1) * 512] for n in range(4))
        MEMX, MV, MER = (split(a, "p (t n) -> p t n", t=TT) for a in (MEMX, MV, MER))
        QX_, SX_, PTX_, FF_, SILU = QKVG[:, 0:KD * T], None, None, GT[:, 0:KF * T], QKVG[:, 2 * D:2 * D + 1024]
        SX_, PTX_ = GT[:, 0:TT * 4 * T], GT[:, TT * 4 * T:2 * TT * 4 * T]
        FINAL = MT[:, 0:D]
        MT, MK = (split(a, "p (k t) -> p k t", k=KD) for a in (MT, MK))
        ABC = split(ABC, "p (c t) -> p c t", c=4)
        Z3 = split(Z3, "p (c t) -> p c t", c=2)
        YA, YCT = (split(a, "p (c t) -> p c t", c=2) for a in (YA, YCT))
        QKVG, ZG, GT, QKR, R, VN, YC = (split(a, "p (t n) -> p t n", t=TT) for a in (QKVG, ZG, GT, QKR, R, VN, YC))
        QKT2, RT = (split(a, "p (c t) -> p c t", c=4) for a in (QKT2, RT))
        DM = split(DM, "p (h s) -> p h s", h=RET_HEADS)
        WSM = split(WSM, "p (g n) -> p g n", g=4)
        QX = split(QX_, "p (k t) -> p k t", k=KD)
        SX = split(SX_, "p (t h m) -> p t h m", t=TT, h=4)
        PTX = split(PTX_, "p (h k t) -> p h k t", h=4, k=TT)
        FF = split(FF_, "p (k t) -> p k t", k=KF)
        SILU = split(SILU, "p (b n) -> p b n", b=2)

        def spar(name, a=0, b=None):
            o, n = SECOND_PARAMS[name]
            return SPAR[:, o + a:o + (n if b is None else b)]

        def hpar(name, a=0, b=None):
            o, n = HYBRID_PARAMS[name]
            return HPAR[:, o + a:o + (n if b is None else b)]

        def ring(j, k, w):
            return RING[:, j % 2, 0:k * w].rearrange("p (k w) -> p k w", k=k)

        block = ctx.enter_context(nc.Block())

        def weight_block(sp, blocks, tag, l, j):
            name, k0, k, c0, w = blocks[j]
            if j >= 2:
                sp.e.wait_ge(*sp.at(f"{tag}{j - 2}_mm"))
            for half in range(2):
                if name == "w1w3":
                    src, kk, first = ("w1_2", "w3_2")[half], KD, 0
                    view = ring(j, 2 * KD, w)[:, half * KD:(half + 1) * KD, :]
                else:
                    src, kk = name, k // 2
                    first = half * kk
                    view = ring(j, k, w)[:, first:first + kk, :]
                cols = COLUMNS[src]
                ap = bass.AP(tensor=dram[src].tensor,
                             offset=l * (ROWS.get(src, D) * cols) + (k0 + first) * P * cols + c0,
                             ap=[[cols, P], [P * cols, kk], [1, w]])
                sp.e.dma_start(view, ap).then_inc(*sp.count(f"{tag}{j}_in" if half else None, f"dma_w{j % 2}"))

        def peer_block(sp, which, b, slot, l, name=None):
            n = 2 * D
            if which == "down":
                ap = bass.AP(tensor=dram["peer_down"].tensor, offset=l * (NKEYS * NKEYS * D) + b * (2 * P * D),
                             ap=[[D, P], [P * D, 2], [1, D]])
                view = RING[:, slot, 0:n].rearrange("p (j n) -> p j n", j=2)
            else:
                ap = bass.AP(tensor=dram["peer_up"].tensor, offset=l * (NKEYS * NKEYS * D) + b * (2 * D),
                             ap=[[NKEYS * D, P], [1, n]])
                view = RING[:, slot, n:2 * n]
            sp.e.dma_start(view, ap).then_inc(*sp.count(name, f"dma_{which}{slot}"))

        def raw(which, slot):
            return RING[:, slot, 0:2 * D] if which == "down" else RING[:, slot, 2 * D:4 * D]

        def norm_scalar(a, tag, src, ready):
            for name in ready:
                a.e.wait_ge(*a.at(name))
            for t in range(TT):
                a.e.activation(SCR[:, t, :], src[:, t, :], ACT.Square, accum_out=STAT[:, 48 + t:49 + t]) \
                    .then_inc(*a.count(f"{tag}_sq{t}"))
            a.e.wait_ge(*a.at(f"{tag}_ms"))
            a.e.activation(STAT[:, 52:54], STAT[:, 50:52], ACT.Sqrt).then_inc(*a.count(f"{tag}_sd"))

        def norm_vector(v, tag, src):
            v.e.wait_ge(*v.at(f"{tag}_sq1"))
            v.e.tensor_scalar(STAT[:, 50:52], STAT[:, 48:50], 1.0 / D, EPS, ALU.mult, ALU.add) \
                .then_inc(*v.count(f"{tag}_ms"))
            v.e.wait_ge(*v.at(f"{tag}_sd"))
            v.e.reciprocal(STAT[:, 54:56], STAT[:, 52:54]).then_inc(*v.count())
            v.e.wait_ge(*v.mine())
            for t in range(TT):
                v.e.tensor_scalar(SCR[:, t, :], src[:, t, :], STAT[:, 54 + t:55 + t], None, ALU.mult) \
                    .then_inc(*v.count(f"{tag}_xn{t}"))

        def turn_tensor(pe, tag, src, nk, ready, free=()):
            for name in free:
                pe.e.wait_ge(*pe.at(name))
            for t in range(TT):
                pe.e.wait_ge(*pe.at(ready[t]))
                for k0 in range(0, nk, 4):
                    kn = min(4, nk - k0)
                    for k in range(k0, k0 + kn):
                        m = pe.e.transpose(PS[:, 4 + 2 * t + k0 // 4, (k - k0) * P:(k - k0 + 1) * P],
                                           src[:, t, k * P:(k + 1) * P], IDENT)
                    m.then_inc(*pe.count(f"{tag}_t{t}{k0 // 4}"))

        def turn_vector(v, tag, dst, nk, weight):
            for t in range(TT):
                for k0 in range(0, nk, 4):
                    kn = min(4, nk - k0)
                    v.e.wait_ge(*v.at(f"{tag}_t{t}{k0 // 4}"))
                    src = PS[:, 4 + 2 * t + k0 // 4, 0:kn * P].rearrange("p (k n) -> p k n", k=kn)
                    to = dst[:, k0:k0 + kn, t * P:(t + 1) * P]
                    name = f"{tag}_done" if t == TT - 1 and k0 + 4 >= nk else None
                    if weight is None:
                        v.e.tensor_copy(to, src).then_inc(*v.count(name))
                    else:
                        w = weight[:, k0:k0 + kn].unsqueeze(2).broadcast_to([P, kn, P])
                        v.e.tensor_tensor(to, src, w, ALU.mult).then_inc(*v.count(name))

        def product(pe, tag, blocks, j, kind, src, bank, free=(), first=True, last=True):
            _, _, k, _, w = blocks[j]
            pe.e.wait_ge(*pe.at(f"{tag}{j}_in"))
            for name in free:
                pe.e.wait_ge(*pe.at(name))
            W = ring(j, k, w)
            if kind == "tokens":
                for t in range(TT):
                    for c0 in range(0, w, 512):
                        cw = min(512, w - c0)
                        b = bank + (t if w <= 512 else 2 * t + c0 // 512)
                        for kc in range(k):
                            m = pe.e.matmul(PS[:, b, 0:cw], src[:, kc, t * P:(t + 1) * P], W[:, kc, c0:c0 + cw],
                                            start=first and kc == 0, stop=last and kc == k - 1)
            else:
                for c in range(-(-w // P)):
                    cw = min(P, w - c * P)
                    for kc in range(k):
                        m = pe.e.matmul(PS[0:cw, bank + c // 2, (c % 2) * T:(c % 2 + 1) * T],
                                        W[:, kc, c * P:c * P + cw], src[:, kc, :], start=kc == 0, stop=kc == k - 1)
            m.then_inc(*pe.count(f"{tag}{j}_mm"))

        def block_pieces(block):
            _, _, _, c0, w = block
            n = TT * w // 256 if c0 < 2560 else -(-w // P)
            return [(i, i == n - 1) for i in range(n)]

        def product_piece(pe, blocks, j, kind, n):
            _, _, k, _, w = blocks[j]
            W, bank = ring(j, k, w), 2 * (j % 2)
            for kc in range(k):
                if kind == "tokens":
                    t, c = divmod(n, w // 256)
                    m = pe.e.matmul(PS[:, bank + t, c * 256:(c + 1) * 256], HT[:, kc, t * P:(t + 1) * P],
                                    W[:, kc, c * 256:(c + 1) * 256], start=kc == 0, stop=kc == k - 1)
                else:
                    cw = min(P, w - n * P)
                    m = pe.e.matmul(PS[0:cw, bank + n // 2, (n % 2) * T:(n % 2 + 1) * T], W[:, kc, n * P:n * P + cw],
                                    HT[:, kc, :], start=kc == 0, stop=kc == k - 1)
            return m

        def hybrid_pool(p):
            with p.loop("hybrid", DEPTH) as l:
                p.e.wait_ge(*p.at("hybrid_start"))
                p.e.wait_ge(*p.mine())
                p.e.tensor_tensor(LB[:, 15:16], COMMON[:, 0:1], COMMON[:, 0:1], ALU.add).then_inc(*p.count())
                p.e.dma_start(HPAR[:, :], bass.AP(tensor=dram["hybrid_par"].tensor, offset=l * (P * N_HYBRID),
                                                  ap=[[N_HYBRID, P], [1, N_HYBRID]])) \
                    .then_inc(*p.count(None, "dma_params"))
                p.e.dma_start(KEYS[:, :], bass.AP(tensor=dram["sub_keys"].tensor, offset=l * (P * P),
                                                  ap=[[P, P], [1, P]])).then_inc(*p.count("params_in", "dma_params"))
                p.e.wait_ge(*p.at("bias_out"))
                p.e.dma_start(HANK, bass.AP(tensor=bias_rows.tensor, offset=0,
                                            ap=[[1, P], [REL, AT_HEADS], [1, T]])) \
                    .then_inc(*p.count("hank_in", "dma_bias_in"))
                p.e.memset(DC, 0.0).then_inc(*p.count())
                p.e.memset(DT[:, 5, :], 1.0).then_inc(*p.count("dt_clear"))
                p.e.wait_ge(*p.at("h1_ev"))
                p.e.wait_ge(*p.mine())
                p.e.tensor_tensor(LB[:, 15:16], COMMON[:, 0:1], COMMON[:, 0:1], ALU.add).then_inc(*p.count())
                p.e.dma_start(hi_rows.rearrange("(c p) t -> p c t", p=P), HI) \
                    .then_inc(*p.count("hi_out", "dma_hi_out"))
                p.e.wait_ge(*p.at("gates"))
                for g in range(SCANS):
                    p.e.wait_ge(*p.at(f"hi_in{g}"))
                    if g >= 2:
                        p.e.wait_ge(*p.at(f"state{g - 2}"))
                    p.e.tensor_tensor(KV[:, g % 2, :, :], VB[:, g % 2, :, :],
                                      KEY[:, g // (SCANS // 2), :].unsqueeze(1).broadcast_to([P, VGROUP, T]),
                                      ALU.mult).then_inc(*p.count(f"kv{g}"))

        def hybrid_scalar(a, l):
            norm_scalar(a, "n1", X, ["hybrid_start"])
            a.e.wait_ge(*a.at("h0_mm"))
            a.e.activation(HQ.rearrange("p c t -> p (c t)"), PS[:, 0, :], ACT.Copy, scale=HEAD ** -0.5) \
                .then_inc(*a.count())
            a.e.activation(FS.rearrange("p c t -> p (c t)"), PS[:, 1, :], ACT.Sigmoid).then_inc(*a.count("h0_ev"))
            a.e.wait_ge(*a.at("h1_mm"))
            a.e.activation(HI.rearrange("p c t -> p (c t)"), PS[:, 2, :], ACT.Copy).then_inc(*a.count("h1_ev"))
            for j in range(2, 6):
                _, _, _, c0, w = HYBRID_BLOCKS[j]
                a.e.wait_ge(*a.at(f"h{j}_mm"))
                for t in range(TT):
                    a.e.activation(U[:, t, c0 - 768:c0 - 768 + w], PS[:, 2 * (j % 2) + t, 0:w], ACT.Copy) \
                        .then_inc(*a.count(f"h{j}_ev" if t else None))
            for j in range(6, 8):
                a.e.wait_ge(*a.at(f"h{j}_mm"))
                for b in range(2):
                    c = 4 * (j - 6) + 2 * b
                    n = min(2, CONV_TILES - c)
                    a.e.activation(XB[:, c:c + n, 3:T + 3],
                                   PS[:, 2 * (j % 2) + b, 0:n * T].rearrange("p (c t) -> p c t", c=n), ACT.Copy) \
                        .then_inc(*a.count("h6_ev" if j == 6 and b else None))
            a.e.wait_ge(*a.at("dt_clear"))
            a.e.activation(DT[0:SS_HEADS, 0, :], PS[0:SS_HEADS, 3, T:2 * T], ACT.Copy).then_inc(*a.count("h7_ev"))
            a.e.wait_ge(*a.at("gates"))
            a.e.activation(FS.rearrange("p c t -> p (c t)").rearrange("p (t n) -> p t n", t=TT),
                           U[:, :, 0:HG_W], ACT.Silu).then_inc(*a.count("g_silu"))
            a.e.wait_ge(*a.at("hg_ms"))
            a.e.activation(STAT[:, 24:32], STAT[:, 16:24], ACT.Sqrt).then_inc(*a.count("hg_sd"))
            a.e.wait_ge(*a.at("qk_ms"))
            a.e.activation(STAT[:, 88:112], STAT[:, 64:88], ACT.Sqrt).then_inc(*a.count("qk_sd"))
            a.e.wait_ge(*a.at("at_max"))
            for h in range(AT_HEADS):
                for t, s in ((0, SCORE0), (1, SCORE1)):
                    c = t * AT_HEADS + h
                    a.e.activation(s[:, h, :], s[:, h, :], ACT.Exp, bias=STAT[:, c:c + 1],
                                   accum_out=STAT[:, 12 + c:13 + c]) \
                        .then_inc(*a.count("at_exp" if h == 5 and t == 1 else None))
            for n in range(5):
                a.e.wait_ge(*a.at(f"pt{n}"))
                w = min(4, 18 - 4 * n) * P
                a.e.activation(PT.rearrange("p h k t -> p (h k t)")[:, n * 512:n * 512 + w], PS[:, n, 0:w],
                               ACT.Copy).then_inc(*a.count(f"pt{n}_ev"))
            a.e.wait_ge(*a.at("dt_neg"))
            a.e.activation(DT[0:SS_HEADS, 3, :], DT[0:SS_HEADS, 2, :], ACT.Exp).then_inc(*a.count())
            a.e.wait_ge(*a.mine())
            a.e.activation(DT[0:SS_HEADS, 3, :], DT[0:SS_HEADS, 3, :], ACT.Ln, bias=1.0).then_inc(*a.count())
            a.e.activation(STAT[0:SS_HEADS, 56:57], hpar("a_log")[0:SS_HEADS], ACT.Exp).then_inc(*a.count("dt_log"))
            a.e.wait_ge(*a.at("conv"))
            for c in range(CONV_TILES):
                a.e.activation(XC[:, c, :], XC[:, c, :], ACT.Silu, bias=hpar("conv_b", c, c + 1)) \
                    .then_inc(*a.count(f"xc{c}"))
            a.e.activation(SZ, U[:, :, 1408:1792], ACT.Silu).then_inc(*a.count("z_silu"))
            a.e.wait_ge(*a.at("dec"))
            a.e.activation(SCORE, SCORE, ACT.Exp).then_inc(*a.count("dec_exp"))
            a.e.wait_ge(*a.at("ss_ms"))
            a.e.activation(STAT[:, 24:28], STAT[:, 16:20], ACT.Sqrt).then_inc(*a.count("ss_sd"))
            norm_scalar(a, "n2", X, ["h9_ev"])
            for j in (10, 11):
                a.e.wait_ge(*a.at(f"h{j}_mm"))
                for b in range(2):
                    h = 4 * (j - 10) + 2 * b
                    a.e.activation(PQ[:, h:h + 2, :].rearrange("p h t -> p (h t)"), PS[:, 2 * (j % 2) + b, :],
                                   ACT.Copy).then_inc(*a.count(f"h{j}_ev" if b else None))
            for t in range(TT):
                a.e.wait_ge(*a.at(f"key_mm{t}"))
                for b in range(4):
                    to = SC[:, t, :, :].rearrange("p (h c) n -> p h c n", c=2)[:, 4 * (b % 2):4 * (b % 2) + 4, b // 2, :]
                    a.e.activation(to, PS[:, 4 * t + b, :].rearrange("p (h n) -> p h n", h=4), ACT.Copy) \
                        .then_inc(*a.count(f"key_ev{t}" if b == 3 else None))
            with a.loop("lead", BLOCKS // 8) as i:
                for b in range(2):
                    a.e.wait_ge(*a.at(f"lead_mm{b}"))
                    a.e.activation(ARENA[:, bass.ds(i * 1024 + (GATES + 512 * b), 512)], PS[:, 4 + b, :],
                                   ACT.Gelu_apprx_tanh).then_inc(*a.count(f"lead_act{b}"))
            a.e.wait_ge(*a.at("best_off"))
            a.e.activation(BESTV, OFF, ACT.Exp).then_inc(*a.count("best_exp"))

            def gates_out(name, i, k):
                a.e.wait_ge(*a.at(f"{name}_gate{k}"))
                a.e.activation(ARENA[:, bass.ds(i * (4 * 512) + k * 512, 512)], PS[:, 6 + k % 2, :], ACT.Copy) \
                    .then_inc(*a.count(f"{name}_gate_out{k}"))

            with a.loop("gate", BLOCKS // 8) as i:
                for b in range(2):
                    a.e.wait_ge(*a.at(f"gate_mm{b}"))
                    a.e.activation(ARENA[:, bass.ds(i * 1024 + (GATES + 512 * (16 + b)), 512)], PS[:, 4 + b, :],
                                   ACT.Gelu_apprx_tanh).then_inc(*a.count(f"gate_act{b}"))
                    gates_out("gate", i, 2 * b)
                    gates_out("gate", i, 2 * b + 1)
            def high(which, slot, name):
                to = DOWN_HI if which == "down" else UP_HI
                a.e.activation(to[:, slot, :], raw(which, slot), ACT.Copy).then_inc(*a.count(name))

            a.e.wait_ge(*a.at("outa_mm1"))
            for b in range(2):
                a.e.wait_ge(*a.at(f"gate_in{b}"))
                high("down", b, f"down_hi_first{b}")
            with a.loop("outb", BLOCKS // 8) as i:
                for k in range(4):
                    gates_out("outb", i, k)
            a.e.wait_ge(*a.at("outb_hot3"))
            a.e.activation(HT_HI[:, :, :], HT[:, :, :], ACT.Copy).then_inc(*a.count("ht_hi"))
            a.e.wait_ge(*a.at("outb_in0"))
            a.e.wait_ge(*a.at("outb_mm1"))
            high("up", 0, "up_hi_first")

            def gelu(b, name):
                a.e.activation(GELU[:, b, :], PS[:, 4 + b, :], ACT.Gelu_apprx_tanh).then_inc(*a.count(name))

            def coef_high(b, name):
                a.e.activation(COEF_HI[:, b, :], GELU[:, b, :], ACT.Copy).then_inc(*a.count(name))

            a.e.wait_ge(*a.at("act_in_first"))
            a.e.wait_ge(*a.at("outb_gate3"))
            with a.loop("peer", BLOCKS // 4 - 1):
                a.e.wait_ge(*a.at("act_in0", back=1))
                a.e.wait_ge(*a.at("coef_lo0", back=1))
                gelu(0, "gelu0")
                a.e.wait_ge(*a.at("down0"))
                high("down", 0, "down_hi0")
                a.e.wait_ge(*a.at("coef0"))
                a.e.wait_ge(*a.at("out0", back=1))
                coef_high(0, "coef_hi0")
                a.e.wait_ge(*a.at("up1", back=1))
                a.e.wait_ge(*a.at("out1", back=1))
                high("up", 1, "up_hi1")
                a.e.wait_ge(*a.at("act_in1"))
                a.e.wait_ge(*a.at("coef_lo1", back=1))
                gelu(1, "gelu1")
                a.e.wait_ge(*a.at("down1"))
                high("down", 1, "down_hi1")
                a.e.wait_ge(*a.at("coef1"))
                a.e.wait_ge(*a.at("out1", back=1))
                coef_high(1, "coef_hi1")
                a.e.wait_ge(*a.at("up0"))
                a.e.wait_ge(*a.at("out0"))
                high("up", 0, "up_hi0")
            a.e.wait_ge(*a.at("act_in0"))
            a.e.wait_ge(*a.at("coef_lo0"))
            gelu(0, "gelu_last0")
            a.e.wait_ge(*a.at("coef_last0"))
            a.e.wait_ge(*a.at("out0"))
            coef_high(0, "coef_hi_last0")
            a.e.wait_ge(*a.at("up1"))
            a.e.wait_ge(*a.at("out1"))
            high("up", 1, "up_hi_last")
            a.e.wait_ge(*a.at("act_in_last"))
            a.e.wait_ge(*a.at("coef_lo1"))
            gelu(1, "gelu_last1")
            a.e.wait_ge(*a.at("coef_last1"))
            coef_high(1, "coef_hi_last1")
            for b in range(4):
                a.e.wait_ge(*a.at("out_last1"))
                a.e.activation(HT[:, 2 * b:2 * b + 2, :].rearrange("p k t -> p (k t)"), PS[:, b, :], ACT.Copy) \
                    .then_inc(*a.count(f"peer_sum{b}"))

        def hybrid_tensor(pe, l):
            turn_tensor(pe, "n1", SCR, KD, ["n1_xn0", "n1_xn1"], ["hybrid_start"])
            pe.e.wait_ge(*pe.at("n1_done"))
            for j in range(2):
                product(pe, "h", HYBRID_BLOCKS, j, "channels", HT, 2 * j)
            OB = PS[:, 7, :].rearrange("p (t h v) -> p t h v", t=TT, h=HG_HEADS)
            pieces = [(j, n, last) for j in range(2, 8) for n, last in block_pieces(HYBRID_BLOCKS[j])]
            for g in range(SCANS):
                if g < len(pieces):
                    j, n, last = pieces[g]
                    kind = "tokens" if j < 6 else "channels"
                    if n == 0:
                        pe.e.wait_ge(*pe.at(f"h{j}_in"))
                        pe.e.wait_ge(*pe.at(f"h{j - 2}_ev"))
                    m = product_piece(pe, HYBRID_BLOCKS, j, kind, n)
                    if last:
                        m.then_inc(*pe.count(f"h{j}_mm"))
                pe.e.wait_ge(*pe.at(f"qs{g}"))
                pair, v0 = g // (SCANS // 2), g % (SCANS // 2) * VGROUP
                for v in range(VGROUP):
                    for t in range(TT):
                        m = pe.e.matmul(OB[:, t, 2 * pair:2 * pair + 2, v0 + v:v0 + v + 1],
                                        QS[:, g % 3, v, t * P:(t + 1) * P], HALVES, start=True, stop=True)
                m.then_inc(*pe.count(f"hg{g}"))
            assert len(pieces) <= SCANS
            pe.e.wait_ge(*pe.at("hank_in"))
            for h in range(AT_HEADS):
                m = pe.e.matmul(PS[:, 4 + h // 2, (h % 2) * T:(h % 2 + 1) * T], FLIP, HANK[:, h, :], start=True,
                                stop=True)
            m.then_inc(*pe.count("flip"))
            pe.e.wait_ge(*pe.at("qkn"))
            pe.e.wait_ge(*pe.at("bias_ev"))
            for c in range(6):
                for t in range(TT):
                    m = pe.e.transpose(PS[:, 4 + c // 2, (c % 2) * T + t * P:(c % 2) * T + (t + 1) * P],
                                       QKN[:, t, c * P:(c + 1) * P], IDENT)
            m.then_inc(*pe.count("qk_t"))
            pe.e.wait_ge(*pe.at("qkt"))
            pe.e.wait_ge(*pe.at("h6_ev"))
            pe.e.wait_ge(*pe.at("h7_ev"))
            for h in range(AT_HEADS):
                r = 64 * (h % 2)
                q, k = QKT[r:r + 64, h // 2, :], QKT[r:r + 64, 3 + h // 2, :]
                pe.e.matmul(PS[:, 2 * (h % 2) + h // 4, (h // 2 % 2) * T:(h // 2 % 2 + 1) * T], q[:, P:T], k,
                            start=True, stop=True)
                m = pe.e.matmul(PS[:, 4 + h % 2, (h // 2) * P:(h // 2 + 1) * P], q[:, 0:P], k[:, 0:P], start=True,
                                stop=True)
            m.then_inc(*pe.count("at_scores"))
            pe.e.wait_ge(*pe.at("at_exp"))
            for n in range(18):
                h, k = divmod(n, 3)
                src = SCORE0[:, h, :] if k == 0 else SCORE1[:, h, (k - 1) * P:k * P]
                m = pe.e.transpose(PS[:, n // 4, (n % 4) * P:(n % 4 + 1) * P], src, IDENT)
                if n % 4 == 3 or n == 17:
                    m.then_inc(*pe.count(f"pt{n // 4}"))
            pe.e.wait_ge(*pe.at("pt4_ev"))
            for h in range(AT_HEADS):
                v = [U[:, t, 1024 + HEAD * h:1024 + HEAD * (h + 1)] for t in range(TT)]
                o = slice(h * HEAD, (h + 1) * HEAD)
                pe.e.matmul(PS[:, 5, o], PT[:, h, 0, :], v[0], start=True, stop=True)
                pe.e.matmul(PS[:, 6, o], PT[:, h, 1, :], v[0], start=True, stop=False)
                m = pe.e.matmul(PS[:, 6, o], PT[:, h, 2, :], v[1], start=False, stop=True)
            m.then_inc(*pe.count("at_out"))
            pe.e.wait_ge(*pe.at("dc"))
            pe.e.wait_ge(*pe.at("hg_read"))
            for t in range(TT):
                m = pe.e.transpose(PS[:, 7, t * P:(t + 1) * P], DC[:, t * P:(t + 1) * P], IDENT)
            m.then_inc(*pe.count("cd_t"))
            for h in range(SS_HEADS):
                m = pe.e.matmul(PS[:, h // 2, (h % 2) * T:(h % 2 + 1) * T],
                                IDENT[0:SS_HEADS, h:h + 1].broadcast_to([SS_HEADS, P]), DT[0:SS_HEADS, 4, :],
                                start=True, stop=True)
            m.then_inc(*pe.count("cum_rows"))
            pe.e.wait_ge(*pe.at("xc6"))
            for g in range(GROUPS):
                pe.e.matmul(PS[:, 3 + g, 0:T], XC[:, 3 + g, 0:P], XC[:, 5 + g, :], start=True, stop=True)
                m = pe.e.matmul(PS[:, 3 + g, T:T + P], XC[:, 3 + g, P:T], XC[:, 5 + g, P:T], start=True, stop=True)
            m.then_inc(*pe.count("bc"))
            pe.e.wait_ge(*pe.at("at_mix"))
            for t in range(TT):
                for c in range(3):
                    m = pe.e.transpose(PS[:, 5 + t, c * P:(c + 1) * P], XC[:, c, t * P:(t + 1) * P], IDENT)
            m.then_inc(*pe.count("xs_t"))
            pe.e.wait_ge(*pe.at("dec_bc"))
            pe.e.wait_ge(*pe.at("xdt"))
            for h in range(SS_HEADS):
                o = slice(h * HEAD, (h + 1) * HEAD)
                pe.e.matmul(PS[:, 0, o], DEC[:, h, 0:P], XDT[:, 0, o], start=True, stop=True)
                pe.e.matmul(PS[:, 1, o], DEC[:, h, P:T], XDT[:, 0, o], start=True, stop=False)
                m = pe.e.matmul(PS[:, 1, o], DEC[:, h, T:T + P], XDT[:, 1, o], start=False, stop=True)
            m.then_inc(*pe.count("ss_out"))
            turn_tensor(pe, "mx", MIX, KD, ["mix", "mix"])
            pe.e.wait_ge(*pe.at("mx_done"))
            for j in (8, 9):
                product(pe, "h", HYBRID_BLOCKS, j, "tokens", HT, 2 * (j % 2), ["ss_read"])
            turn_tensor(pe, "n2", SCR, KD, ["n2_xn0", "n2_xn1"])
            pe.e.wait_ge(*pe.at("n2_done"))
            for j in (10, 11):
                product(pe, "h", HYBRID_BLOCKS, j, "channels", HT, 2 * (j % 2), [f"h{j - 2}_ev"])
            pe.e.wait_ge(*pe.at("h11_ev"))
            pe.e.wait_ge(*pe.at("params_in"))
            for t in range(TT):
                for h in range(PEER_HEADS):
                    for c in range(2):
                        r = 64 * c
                        m = pe.e.matmul(PS[:, 4 * t + 2 * c + h // 4, (h % 4) * P:(h % 4 + 1) * P],
                                        PQ[r:r + 64, h, t * P:(t + 1) * P], KEYS[r:r + 64, :], start=True, stop=True)
                m.then_inc(*pe.count(f"key_mm{t}"))

            def act_in(b, bank):
                for j in range(2):
                    for kc in range(KD):
                        m = pe.e.matmul(PS[:, bank, j * T:(j + 1) * T],
                                        RING[:, b, j * D + kc * P:j * D + (kc + 1) * P], HT[:, kc, :],
                                        start=kc == 0, stop=kc == KD - 1)
                return m

            def out_of(b, coefficients, last=False):
                for j in range(2):
                    for k in range(KD):
                        at = 2 * D + j * D + k * P
                        m = pe.e.matmul(PS[:, k // 2, (k % 2) * T:(k % 2 + 1) * T], RING[:, b, at:at + P],
                                        coefficients(j), start=False, stop=last and j == 1, skip_group_check=True)
                return m

            def stored(i, block):
                return lambda j: ARENA[:, bass.ds(i * 1024 + (GATES + 512 * block + j * T), T)]

            def gates(name, k):
                pe.e.wait_ge(*pe.at(f"{name}_hot{k}"))
                if k < 2:
                    pe.e.wait_ge(*pe.at(f"{name}_gate_out{k + 2}", back=1))
                else:
                    pe.e.wait_ge(*pe.at(f"{name}_gate_out{k - 2}"))
                for j in range(GROUP):
                    m = pe.e.matmul(PS[:, 6 + k % 2, j * 64:(j + 1) * 64], HOT1[:, k % 2, j, :], HOT2[:, k % 2, j, :],
                                    start=True, stop=True)
                m.then_inc(*pe.count(f"{name}_gate{k}"))

            with pe.loop("lead", BLOCKS // 8):
                pe.e.wait_ge(*pe.at("key_ev1"))
                for b in range(2):
                    pe.e.wait_ge(*pe.at(f"lead_in{b}", back=1))
                    pe.e.wait_ge(*pe.at(f"lead_act{b}", back=1))
                    act_in(b, 4 + b).then_inc(*pe.count(f"lead_mm{b}"))
            pe.e.wait_ge(*pe.at("hkr"))
            for t in range(TT):
                for c in range(3):
                    m = pe.e.transpose(PS[:, t, c * P:(c + 1) * P], HKR[:, t, c, :], IDENT)
                m.then_inc(*pe.count(f"hk_t{t}"))
            with pe.loop("gate", BLOCKS // 8):
                for b in range(2):
                    pe.e.wait_ge(*pe.at(f"gate_in{b}", back=1))
                    pe.e.wait_ge(*pe.at(f"gate_act{b}", back=1))
                    act_in(b, 4 + b).then_inc(*pe.count(f"gate_mm{b}"))
                    gates("gate", 2 * b)
                    gates("gate", 2 * b + 1)
            pe.e.wait_ge(*pe.at("zero"))
            pe.e.wait_ge(*pe.at("hk_read"))
            for b in range(4):
                m = pe.e.matmul(PS[:, b, :], KEYS[:, :], PHASE[:, 0:512], start=True, stop=False,
                                skip_group_check=True)
            with pe.loop("outa", BLOCKS // 8) as i:
                pe.e.wait_ge(*pe.at("fold"))
                for b in range(2):
                    pe.e.wait_ge(*pe.at(f"outa_in{b}", back=1))
                    out_of(b, stored(i, b)).then_inc(*pe.count(f"outa_mm{b}"))
            with pe.loop("outb", BLOCKS // 8) as i:
                for b in range(2):
                    pe.e.wait_ge(*pe.at(f"outb_in{b}", back=1))
                    out_of(b, stored(i, 16 + b)).then_inc(*pe.count(f"outb_mm{b}"))
                    gates("outb", 2 * b)
                    gates("outb", 2 * b + 1)
            def act_in_parts(b):
                for j in range(2):
                    for kc in range(KD):
                        o = slice(j * D + kc * P, j * D + (kc + 1) * P)
                        passes = ((DOWN_HI, HT_HI), (DOWN_HI, HT_LO), (DOWN_LO, HT_HI))
                        for n, (w, x) in enumerate(passes):
                            m = pe.e.matmul(PS[:, 4 + b, j * T:(j + 1) * T], w[:, b, o], x[:, kc, :],
                                            start=kc == 0 and n == 0, stop=kc == KD - 1 and n == 2)
                return m

            def out_of_parts(b, last=False):
                for j in range(2):
                    for k in range(KD):
                        o = slice(j * D + k * P, j * D + (k + 1) * P)
                        passes = ((UP_HI, COEF_HI), (UP_HI, COEF_LO), (UP_LO, COEF_HI))
                        for n, (w, x) in enumerate(passes):
                            m = pe.e.matmul(PS[:, k // 2, (k % 2) * T:(k % 2 + 1) * T], w[:, b, o],
                                            x[:, b, j * T:(j + 1) * T], start=False,
                                            stop=last and j == 1 and n == 2, skip_group_check=True)
                return m

            pe.e.wait_ge(*pe.at("down_lo_first1"))
            pe.e.wait_ge(*pe.at("ht_lo"))
            act_in_parts(0).then_inc(*pe.count("act_in_first"))
            with pe.loop("peer", BLOCKS // 4 - 1):
                pe.e.wait_ge(*pe.at("up_lo_first"))
                pe.e.wait_ge(*pe.at("down_lo1", back=1))
                pe.e.wait_ge(*pe.at("gelu1", back=1))
                act_in_parts(1).then_inc(*pe.count("act_in1"))
                pe.e.wait_ge(*pe.at("up_lo0", back=1))
                pe.e.wait_ge(*pe.at("coef_lo0"))
                out_of_parts(0).then_inc(*pe.count("out0"))
                pe.e.wait_ge(*pe.at("down_lo0"))
                pe.e.wait_ge(*pe.at("gelu0"))
                act_in_parts(0).then_inc(*pe.count("act_in0"))
                pe.e.wait_ge(*pe.at("up_lo1"))
                pe.e.wait_ge(*pe.at("coef_lo1"))
                out_of_parts(1).then_inc(*pe.count("out1"))
            pe.e.wait_ge(*pe.at("down_lo1"))
            pe.e.wait_ge(*pe.at("gelu1"))
            act_in_parts(1).then_inc(*pe.count("act_in_last"))
            pe.e.wait_ge(*pe.at("up_lo0"))
            pe.e.wait_ge(*pe.at("coef_lo_last0"))
            out_of_parts(0).then_inc(*pe.count("out_last0"))
            pe.e.wait_ge(*pe.at("up_lo_last"))
            pe.e.wait_ge(*pe.at("coef_lo_last1"))
            out_of_parts(1, last=True).then_inc(*pe.count("out_last1"))
            pe.e.wait_ge(*pe.at("gelu_last1"))
            for b in range(4):
                pe.e.wait_ge(*pe.at(f"peer_sum{b}"))
                for k in (2 * b, 2 * b + 1):
                    for t in range(TT):
                        m = pe.e.transpose(PS[:, 4 + 2 * t + k // 4, (k % 4) * P:(k % 4 + 1) * P],
                                           HT[:, k, t * P:(t + 1) * P], IDENT)
            m.then_inc(*pe.count("peer_t"))

        def hybrid_vector(v, l):
            def bc(ap, n):
                return ap.unsqueeze(2).broadcast_to([P, ap.shape[1], n])

            def rstd(tag, n, width, src, dst):
                v.e.wait_ge(*v.mine())
                v.e.tensor_scalar(STAT[:, src:src + n], STAT[:, src:src + n], 1.0 / width, EPS, ALU.mult,
                                  ALU.add).then_inc(*v.count(f"{tag}_ms"))
                v.e.wait_ge(*v.at(f"{tag}_sd"))
                v.e.reciprocal(STAT[:, dst:dst + n], STAT[:, dst:dst + n]).then_inc(*v.count())
                v.e.wait_ge(*v.mine())

            v.e.wait_ge(*v.mine())
            v.e.memset(XB[:, :, 0:3], 0.0).then_inc(*v.count("hybrid_start"))
            norm_vector(v, "n1", X)
            v.e.wait_ge(*v.at("params_in"))
            turn_vector(v, "n1", HT, KD, hpar("attn_norm"))
            v.e.tensor_copy(STAT[:, 0:2], LB[:, bass.ds(l * 2 + 10, 2)]).then_inc(*v.count())
            v.e.wait_ge(*v.mine())
            v.e.tensor_scalar(STAT[:, 2:4], STAT[:, 0:2], -1.0, 1.0, ALU.mult, ALU.add).then_inc(*v.count())
            v.e.wait_ge(*v.mine())
            v.e.wait_ge(*v.at("h0_ev"))
            for c in range(2):
                v.e.tensor_scalar(FS[:, c, :], FS[:, c, :], STAT[:, 2 + c:3 + c], STAT[:, c:c + 1], ALU.mult,
                                  ALU.add).then_inc(*v.count())
            v.e.wait_ge(*v.mine())
            v.e.tensor_scalar(KEY, FS, -1.0, 1.0, ALU.mult, ALU.add).then_inc(*v.count())
            for c in range(2):
                v.e.tensor_copy(FR[:, c, :, :], FS[:, c, :].unsqueeze(1).broadcast_to([P, VGROUP, T])) \
                    .then_inc(*v.count())
            v.e.wait_ge(*v.mine())
            v.e.memset(FR[:, :, :, 0:1], 0.0).then_inc(*v.count("gates"))
            v.e.wait_ge(*v.mine())
            v.e.tensor_copy(LB[:, 14:15], COMMON[:, 0:1]).then_inc(*v.count())
            for g in range(SCANS):
                v.e.wait_ge(*v.at(f"kv{g}"))
                v.e.tensor_tensor_scan(
                    ST[:, g % 2, :, :].rearrange("p v t -> p (v t)"),
                    FR[:, g // (SCANS // 2), :, :].rearrange("p v t -> p (v t)"),
                    KV[:, g % 2, :, :].rearrange("p v t -> p (v t)"), 0.0, ALU.mult, ALU.add) \
                    .then_inc(*v.count(f"state{g}"))
                v.e.wait_ge(*v.mine())
                if g >= 3:
                    v.e.wait_ge(*v.at(f"hg{g - 3}"))
                v.e.tensor_tensor(QS[:, g % 3, :, :], ST[:, g % 2, :, :],
                                  HQ[:, g // (SCANS // 2), :].unsqueeze(1).broadcast_to([P, VGROUP, T]), ALU.mult) \
                    .then_inc(*v.count(f"qs{g}"))
            v.e.wait_ge(*v.at("flip"))
            for b in range(3):
                v.e.tensor_tensor(BIAS1[:, 2 * b:2 * b + 2, :],
                                  PS[:, 4 + b, :].rearrange("p (h s) -> p h s", h=2),
                                  PHASE[:, 0:T].unsqueeze(1).broadcast_to([P, 2, T]), ALU.add).then_inc(*v.count())
                v.e.tensor_tensor(BIAS0[:, 2 * b:2 * b + 2, :],
                                  PS[:, 4 + b, :].rearrange("p (h s) -> p h s", h=2)[:, :, P:T],
                                  PHASE[:, T:T + P].unsqueeze(1).broadcast_to([P, 2, P]), ALU.add) \
                    .then_inc(*v.count("bias_ev" if b == 2 else None))
            v.e.wait_ge(*v.at(f"hg{SCANS - 1}"))
            o, sq = SCORE[:, 0:512], SCORE[:, 512:1024]
            v.e.tensor_copy(o, PS[:, 7, :]).then_inc(*v.count("hg_read"))
            v.e.wait_ge(*v.mine())
            v.e.tensor_tensor(sq, o, o, ALU.mult).then_inc(*v.count())
            v.e.wait_ge(*v.mine())
            v.e.tensor_reduce(STAT[:, 16:24], sq.rearrange("p (n v) -> p n v", v=HEAD), AX.X, ALU.add) \
                .then_inc(*v.count())
            rstd("hg", 8, HEAD, 16, 24)
            v.e.tensor_tensor(o.rearrange("p (n v) -> p n v", v=HEAD), o.rearrange("p (n v) -> p n v", v=HEAD),
                              bc(STAT[:, 24:32], HEAD), ALU.mult).then_inc(*v.count())
            v.e.wait_ge(*v.mine())
            v.e.wait_ge(*v.at("g_silu"))
            v.e.tensor_tensor(MIX[:, :, 0:HG_W], o.rearrange("p (t n) -> p t n", t=TT),
                              FS.rearrange("p c t -> p (c t)").rearrange("p (t n) -> p t n", t=TT), ALU.mult) \
                .then_inc(*v.count())
            v.e.wait_ge(*v.mine())
            sq = SCORE[:, 0:1536].rearrange("p (t n) -> p t n", t=TT)
            v.e.tensor_tensor(sq, U[:, :, 256:1024], U[:, :, 256:1024], ALU.mult).then_inc(*v.count())
            v.e.wait_ge(*v.mine())
            v.e.tensor_reduce(STAT[:, 64:88], SCORE[:, 0:1536].rearrange("p (n d) -> p n d", d=HEAD), AX.X,
                              ALU.add).then_inc(*v.count())
            rstd("qk", 24, HEAD, 64, 88)
            for t in range(TT):
                v.e.tensor_tensor(QKN[:, t, :].rearrange("p (n d) -> p n d", d=HEAD),
                                  U[:, t, 256:1024].rearrange("p (n d) -> p n d", d=HEAD),
                                  bc(STAT[:, 88 + 12 * t:100 + 12 * t], HEAD), ALU.mult) \
                    .then_inc(*v.count("qkn" if t else None))
            v.e.wait_ge(*v.at("qk_t"))
            for c0, c1, w in ((0, 2, "q_norm"), (2, 3, "q_norm"), (3, 4, "k_norm"), (4, 6, "k_norm")):
                v.e.tensor_scalar(QKT[:, c0:c1, :].rearrange("p c t -> p (c t)"),
                                  PS[:, 4 + c0 // 2, (c0 % 2) * T:(c0 % 2) * T + (c1 - c0) * T],
                                  hpar(w), HEAD ** -0.5 if w == "q_norm" else 1.0, ALU.mult, ALU.mult) \
                    .then_inc(*v.count("qkt" if c1 == 6 else None))
            v.e.wait_ge(*v.at("at_scores"))
            v.e.wait_ge(*v.mine())
            for odd in range(2):
                v.e.tensor_tensor(SCORE1[:, odd:4:2, :],
                                  PS[:, 2 * odd, :].rearrange("p (h s) -> p h s", h=2),
                                  BIAS1[:, odd:4:2, :], ALU.add).then_inc(*v.count())
                v.e.tensor_tensor(SCORE1[:, 4 + odd, :], PS[:, 2 * odd + 1, 0:T], BIAS1[:, 4 + odd, :],
                                  ALU.add).then_inc(*v.count())
                v.e.tensor_tensor(SCORE0[:, odd:6:2, :],
                                  PS[:, 4 + odd, 0:3 * P].rearrange("p (h s) -> p h s", h=3),
                                  BIAS0[:, odd:6:2, :], ALU.add).then_inc(*v.count())
            v.e.wait_ge(*v.mine())
            v.e.tensor_reduce(STAT[:, 0:6], SCORE0, AX.X, ALU.max, negate=True).then_inc(*v.count())
            v.e.tensor_reduce(STAT[:, 6:12], SCORE1, AX.X, ALU.max, negate=True).then_inc(*v.count("at_max"))
            v.e.wait_ge(*v.at("h7_ev"))
            z, neg, soft, cum = (DT[0:SS_HEADS, k, :] for k in (1, 2, 3, 4))
            v.e.tensor_scalar(z, DT[0:SS_HEADS, 0, :], hpar("dt_bias")[0:SS_HEADS], None, ALU.add) \
                .then_inc(*v.count())
            v.e.wait_ge(*v.mine())
            v.e.scalar_tensor_tensor(neg, z, -1.0, z, ALU.mult, ALU.min).then_inc(*v.count("dt_neg"))
            for k in range(4):
                for c in range(CONV_TILES):
                    w = hpar("conv_w", k * CONV_TILES + c, k * CONV_TILES + c + 1)
                    if k == 0:
                        i = v.e.tensor_scalar(XC[:, c, :], XB[:, c, 0:T], w, None, ALU.mult)
                    else:
                        v.e.wait_ge(*v.mine(CONV_TILES - 1))
                        i = v.e.scalar_tensor_tensor(XC[:, c, :], XB[:, c, k:k + T], w, XC[:, c, :], ALU.mult, ALU.add)
                    i.then_inc(*v.count("conv" if k == 3 and c == CONV_TILES - 1 else None))
            v.e.wait_ge(*v.at("at_exp"))
            v.e.reciprocal(STAT[:, 32:44], STAT[:, 12:24]).then_inc(*v.count())
            v.e.wait_ge(*v.mine())
            v.e.wait_ge(*v.at("at_out"))
            for t in range(TT):
                v.e.tensor_tensor(MIX[:, t, HG_W:HG_W + AT_W].rearrange("p (h d) -> p h d", d=HEAD),
                                  PS[:, 5 + t, 0:AT_W].rearrange("p (h d) -> p h d", d=HEAD),
                                  bc(STAT[:, 32 + 6 * t:38 + 6 * t], HEAD), ALU.mult) \
                    .then_inc(*v.count("at_mix" if t else None))
            v.e.wait_ge(*v.at("dt_log"))
            v.e.scalar_tensor_tensor(neg, z, 0.0, soft, ALU.max, ALU.add).then_inc(*v.count())
            v.e.wait_ge(*v.mine())
            v.e.tensor_scalar(soft, neg, STAT[0:SS_HEADS, 56:57], -1.0, ALU.mult, ALU.mult).then_inc(*v.count())
            v.e.wait_ge(*v.mine())
            v.e.tensor_tensor_scan(cum, DT[0:SS_HEADS, 5, :], soft, 0.0, ALU.mult, ALU.add).then_inc(*v.count())
            v.e.wait_ge(*v.mine())
            v.e.tensor_copy(DC[0:SS_HEADS, :], cum).then_inc(*v.count())
            v.e.tensor_copy(DC[32:32 + SS_HEADS, :], neg).then_inc(*v.count("dc"))
            v.e.wait_ge(*v.at("cd_t"))
            v.e.tensor_copy(CD, PS[:, 7, 0:T].rearrange("p (t n) -> p t n", t=TT)[:, :, 0:64]).then_inc(*v.count())
            v.e.wait_ge(*v.mine())
            v.e.wait_ge(*v.at("cum_rows"))
            mask = PHASE[:, T + P:2 * (T + P)]
            for h in range(SS_HEADS):
                row = PS[:, h // 2, (h % 2) * T:(h % 2 + 1) * T]
                v.e.scalar_tensor_tensor(DEC[:, h, 0:T], row, CD[:, 0, h:h + 1], mask[:, 0:T], ALU.subtract,
                                         ALU.add).then_inc(*v.count())
                v.e.scalar_tensor_tensor(DEC[:, h, T:T + P], row[:, P:T], CD[:, 1, h:h + 1], mask[:, T:T + P],
                                         ALU.subtract, ALU.add) \
                    .then_inc(*v.count("dec" if h == SS_HEADS - 1 else None))
            v.e.wait_ge(*v.at("xs_t"))
            for t in range(TT):
                x = PS[:, 5 + t, 0:SS_W].rearrange("p (h d) -> p h d", d=HEAD)
                v.e.tensor_tensor(XDT[:, t, :].rearrange("p (h d) -> p h d", d=HEAD), x,
                                  bc(CD[:, t, 32:32 + SS_HEADS], HEAD), ALU.mult).then_inc(*v.count())
                v.e.tensor_tensor(XSK[:, t, :].rearrange("p (h d) -> p h d", d=HEAD), x,
                                  bc(hpar("d_skip"), HEAD), ALU.mult).then_inc(*v.count("xdt" if t else None))
            v.e.wait_ge(*v.at("dec_exp"))
            v.e.wait_ge(*v.at("bc"))
            for g in range(GROUPS):
                d = DEC[:, 3 * g:3 * g + 3, :]
                v.e.tensor_tensor(d, d, PS[:, 3 + g, 0:T + P].unsqueeze(1).broadcast_to([P, 3, T + P]),
                                  ALU.mult).then_inc(*v.count("dec_bc" if g else None))
            v.e.wait_ge(*v.at("ss_out"))
            for t in range(TT):
                v.e.tensor_tensor(XSK[:, t, :], PS[:, t, 0:SS_W], XSK[:, t, :], ALU.add) \
                    .then_inc(*v.count("ss_read" if t else None))
            v.e.wait_ge(*v.mine())
            v.e.wait_ge(*v.at("z_silu"))
            v.e.tensor_tensor(XSK, XSK, SZ, ALU.mult).then_inc(*v.count())
            v.e.wait_ge(*v.mine())
            v.e.tensor_tensor(XDT, XSK, XSK, ALU.mult).then_inc(*v.count())
            v.e.wait_ge(*v.mine())
            v.e.tensor_reduce(STAT[:, 16:20], XDT.rearrange("p t (g n) -> p (t g) n", g=GROUPS), AX.X, ALU.add) \
                .then_inc(*v.count())
            rstd("ss", 4, SS_W // GROUPS, 16, 24)
            for t in range(TT):
                v.e.tensor_tensor(MIX[:, t, HG_W + AT_W:D].rearrange("p (g n) -> p g n", g=GROUPS),
                                  XSK[:, t, :].rearrange("p (g n) -> p g n", g=GROUPS),
                                  bc(STAT[:, 24 + 2 * t:26 + 2 * t], SS_W // GROUPS), ALU.mult) \
                    .then_inc(*v.count("mix" if t else None))
            turn_vector(v, "mx", HT, KD, hpar("mix_norm"))
            add_to_x(v, "h", HYBRID_BLOCKS, (8, 9))
            v.e.wait_ge(*v.mine())
            norm_vector(v, "n2", X)
            turn_vector(v, "n2", HT, KD, hpar("ffn_norm"))
            for t in range(TT):
                top_keys(v, t)
            choice_gates(v)
            v.e.wait_ge(*v.at("key_mm1"))
            v.e.memset(KEYS[:, :], 0.0).then_inc(*v.count("zero"))
            v.e.wait_ge(*v.mine())
            v.e.tensor_copy(LB[:, 14:15], COMMON[:, 0:1]).then_inc(*v.count())

            def hot(name, i, k, half):
                if k < 2:
                    v.e.wait_ge(*v.at(f"{name}_gate{k + 2}", back=1))
                else:
                    v.e.wait_ge(*v.at(f"{name}_gate{k - 2}"))
                for j in range(GROUP):
                    at = i * (4 * GROUP) + (GROUP * k + j)
                    v.e.tensor_scalar(HOT1[:, k % 2, j, :], IOTA, HK[:, 0, bass.ds(at, 1)], None, ALU.is_equal) \
                        .then_inc(*v.count())
                    v.e.tensor_scalar(HOT2[:, k % 2, j, :], IOTA[:, half * 64:(half + 1) * 64],
                                      HK[:, 1, bass.ds(at, 1)], HK[:, 2, bass.ds(at, 1)], ALU.is_equal, ALU.mult) \
                        .then_inc(*v.count(f"{name}_hot{k}" if j == GROUP - 1 else None))

            with v.loop("gate", BLOCKS // 8) as i:
                for k in range(4):
                    hot("gate", i, k, 0)
            v.e.wait_ge(*v.at("gate_gate_out3"))
            v.e.tensor_copy(LB[:, 14:15], COMMON[:, 0:1]).then_inc(*v.count())
            with v.loop("outa", BLOCKS // 8) as i:
                for b in range(4):
                    act = ARENA[:, bass.ds(i * 2048 + (GATES + 512 * b), 512)].rearrange("p (j t) -> p j t", j=2)
                    v.e.tensor_tensor(act, act, G[:, :, bass.ds(i * 8 + 2 * b, 2)].rearrange("p t j -> p j t"),
                                      ALU.mult).then_inc(*v.count("fold" if b == 3 else None))
            def low(which, slot, name):
                hi, lo = (DOWN_HI, DOWN_LO) if which == "down" else (UP_HI, UP_LO)
                v.e.tensor_tensor(lo[:, slot, :], raw(which, slot), hi[:, slot, :].bitcast(F32), ALU.subtract) \
                    .then_inc(*v.count(name))

            for b in range(2):
                v.e.wait_ge(*v.at(f"down_hi_first{b}"))
                low("down", b, f"down_lo_first{b}")
            with v.loop("outb", BLOCKS // 8) as i:
                for k in range(4):
                    hot("outb", i, k, 1)
            v.e.wait_ge(*v.at("ht_hi"))
            v.e.tensor_tensor(HT_LO[:, :, :], HT[:, :, :], HT_HI[:, :, :].bitcast(F32), ALU.subtract).then_inc(*v.count("ht_lo"))
            v.e.wait_ge(*v.at("up_hi_first"))
            low("up", 0, "up_lo_first")

            def coef(b, n2, name):
                act = GELU[:, b, :].rearrange("p (j t) -> p j t", j=2)
                v.e.tensor_tensor(act, act, G[:, :, bass.ds(n2, 2)].rearrange("p t j -> p j t"), ALU.mult) \
                    .then_inc(*v.count(name))

            def coef_low(b, name):
                v.e.tensor_tensor(COEF_LO[:, b, :], GELU[:, b, :], COEF_HI[:, b, :].bitcast(F32), ALU.subtract) \
                    .then_inc(*v.count(name))

            with v.loop("peer", BLOCKS // 4 - 1) as i:
                for b in range(2):
                    v.e.wait_ge(*v.at(f"gelu{b}"))
                    coef(b, i * 4 + 2 * b, f"coef{b}")
                    v.e.wait_ge(*v.at(f"coef_hi{b}"))
                    coef_low(b, f"coef_lo{b}")
                    v.e.wait_ge(*v.at(f"down_hi{b}"))
                    low("down", b, f"down_lo{b}")
                    v.e.wait_ge(*v.at(f"up_hi{1 - b}"))
                    low("up", 1 - b, f"up_lo{1 - b}")
            for b in range(2):
                v.e.wait_ge(*v.at(f"gelu_last{b}"))
                coef(b, NKEYS // 2 - 4 + 2 * b, f"coef_last{b}")
                v.e.wait_ge(*v.at(f"coef_hi_last{b}"))
                coef_low(b, f"coef_lo_last{b}")
                if b == 0:
                    v.e.wait_ge(*v.at("up_hi_last"))
                    low("up", 1, "up_lo_last")
            v.e.wait_ge(*v.at("peer_t"))
            for t in range(TT):
                for half in range(2):
                    x = X[:, t, half * 512:(half + 1) * 512]
                    v.e.tensor_tensor(x, PS[:, 4 + 2 * t + half, :], x, ALU.add) \
                        .then_inc(*v.count("hybrid_end" if t == 1 and half else None))

        def add_to_x(v, tag, blocks, js):
            for j in js:
                c0 = blocks[j][3]
                v.e.wait_ge(*v.at(f"{tag}{j}_mm"))
                for t in range(TT):
                    x = X[:, t, c0:c0 + 512]
                    v.e.tensor_tensor(x, PS[:, 2 * (j % 2) + t, :], x, ALU.add) \
                        .then_inc(*v.count(f"{tag}{j}_ev" if t else None))

        def top_keys(v, t):
            S = SC[:, t, :, :]
            v.e.wait_ge(*v.at(f"key_ev{t}"))

            def best(scores, spare, values, index, n):
                v.e.wait_ge(*v.mine())
                v.e.tensor_copy(LB[:, 14:15], COMMON[:, 0:1]).then_inc(*v.count())
                for c in range(n):
                    v.e.max(values(c)[:, 0:8], scores(c)).then_inc(*v.count())
                v.e.wait_ge(*v.mine())
                v.e.tensor_copy(LB[:, 14:15], COMMON[:, 0:1]).then_inc(*v.count())
                for c in range(n):
                    v.e.max_index(index(c)[:, 0:8], values(c)[:, 0:8], scores(c)).then_inc(*v.count())
                for c in range(n):
                    v.e.match_replace(spare(c), values(c)[:, 0:8], scores(c), -BIG).then_inc(*v.count())
                v.e.wait_ge(*v.mine())
                v.e.tensor_copy(LB[:, 14:15], COMMON[:, 0:1]).then_inc(*v.count())
                for c in range(n):
                    v.e.max(values(c)[:, 8:16], spare(c)).then_inc(*v.count())
                v.e.wait_ge(*v.mine())
                v.e.tensor_copy(LB[:, 14:15], COMMON[:, 0:1]).then_inc(*v.count())
                for c in range(n):
                    v.e.max_index(index(c)[:, 8:16], values(c)[:, 8:16], spare(c)).then_inc(*v.count())
                v.e.wait_ge(*v.mine())

            best(lambda c: S[:, c, :], lambda c: SC2[:, c, :], lambda c: TOPV[:, c, :], lambda c: TOPI[:, c, :], HC)
            v.e.tensor_copy(TOPF, TOPI).then_inc(*v.count())
            pair = TOPV.rearrange("p (h c) k -> p h c k", c=2)
            v.e.tensor_tensor(CAND.rearrange("p h (a b) -> p h a b", a=TOPK),
                              pair[:, :, 0, :].unsqueeze(3).broadcast_to([P, PEER_HEADS, TOPK, TOPK]),
                              pair[:, :, 1, :].unsqueeze(2).broadcast_to([P, PEER_HEADS, TOPK, TOPK]), ALU.add) \
                .then_inc(*v.count())
            BV, BI = (a.rearrange("p (h k) -> p h k", h=PEER_HEADS) for a in (BESTV[:, t, :], BESTI))
            best(lambda c: CAND[:, c, :], lambda c: CAND2[:, c, :], lambda c: BV[:, c, :], lambda c: BI[:, c, :],
                 PEER_HEADS)
            v.e.tensor_scalar(KI[:, 0, :], BESTI, 4, None, ALU.logical_shift_right).then_inc(*v.count())
            v.e.tensor_scalar(KI[:, 1, :], BESTI, 15, None, ALU.bitwise_and).then_inc(*v.count())
            v.e.tensor_tensor(OFF[:, t, :].rearrange("p (h k) -> p h k", h=PEER_HEADS), BV,
                              BV[:, :, 0:1].broadcast_to([P, PEER_HEADS, TOPK]), ALU.subtract) \
                .then_inc(*v.count("best_off" if t else None))
            v.e.wait_ge(*v.mine())
            v.e.tensor_copy(KF_, KI).then_inc(*v.count())
            topf = TOPF.rearrange("p (h c) k -> p h c k", c=2)
            E4 = EQ.rearrange("p (h k i) -> p h k i", h=PEER_HEADS, k=TOPK)
            E3 = EQ.rearrange("p (n i) -> p n i", i=TOPK)
            for c in range(2):
                v.e.wait_ge(*v.mine())
                v.e.tensor_tensor(E3, bc16(KF_[:, c, :]), IOTA16.unsqueeze(1).broadcast_to([P, P, TOPK]),
                                  ALU.is_equal).then_inc(*v.count())
                v.e.wait_ge(*v.mine())
                v.e.tensor_tensor(E4, E4, topf[:, :, c, :].unsqueeze(2).broadcast_to(
                    [P, PEER_HEADS, TOPK, TOPK]), ALU.mult).then_inc(*v.count())
                v.e.wait_ge(*v.mine())
                v.e.tensor_reduce(HKR[:, t, c, :], E3, AX.X, ALU.add).then_inc(*v.count())

        def choice_gates(v):
            v.e.wait_ge(*v.at("best_exp"))
            v.e.wait_ge(*v.mine())
            v.e.tensor_reduce(STAT[:, 0:16], BESTV.rearrange("p t (h k) -> p (t h) k", h=PEER_HEADS), AX.X, ALU.add) \
                .then_inc(*v.count())
            v.e.wait_ge(*v.mine())
            v.e.reciprocal(STAT[:, 16:32], STAT[:, 0:16]).then_inc(*v.count())
            v.e.wait_ge(*v.mine())
            for t in range(TT):
                v.e.tensor_tensor(HKR[:, t, 2, :].rearrange("p (h k) -> p h k", h=PEER_HEADS),
                                  BESTV[:, t, :].rearrange("p (h k) -> p h k", h=PEER_HEADS),
                                  STAT[:, 16 + 8 * t:24 + 8 * t].unsqueeze(2).broadcast_to([P, PEER_HEADS, TOPK]),
                                  ALU.mult).then_inc(*v.count("hkr" if t else None))
            for t in range(TT):
                v.e.wait_ge(*v.at(f"hk_t{t}"))
                v.e.tensor_copy(HK[:, :, t * P:(t + 1) * P], PS[:, t, 0:3 * P].rearrange("p (c n) -> p c n", c=3)) \
                    .then_inc(*v.count("hk_read" if t else None))

        def bc16(ap):
            return ap.unsqueeze(2).broadcast_to([P, ap.shape[1], TOPK])

        def second_loads(sp):
            sp.e.dma_start(MEMX, dram["mem_2"].rearrange("b (t p) d -> p (b t) d", p=P)) \
                .then_inc(*sp.count("mem_in", "dma_start"))
            with sp.loop("second", DEPTH) as l:
                sp.e.wait_ge(*sp.at("second_start"))
                for j in range(len(SECOND_BLOCKS)):
                    weight_block(sp, SECOND_BLOCKS, "s", l, j)

        def second_pool(p):
            with p.loop("second", DEPTH) as l:
                p.e.wait_ge(*p.at("second_start"))
                p.e.wait_ge(*p.mine())
                p.e.tensor_tensor(LB[:, 15:16], COMMON[:, 0:1], COMMON[:, 0:1], ALU.add).then_inc(*p.count())
                p.e.dma_start(SPAR[:, 0:N_SECOND],
                              bass.AP(tensor=dram["second_par"].tensor, offset=l * (P * N_SECOND),
                                      ap=[[N_SECOND, P], [1, N_SECOND]])) \
                    .then_inc(*p.count("second_params_in", "dma_params"))
            p.e.wait_ge(*p.at("second_end"))
            p.e.dma_start(FINAL, bass.AP(tensor=dram["final_norm_2"].tensor, offset=0, ap=[[0, P], [1, D]])) \
                .then_inc(*p.count("final_in", "dma_params"))

        def second_scalar(a, l):
            norm_scalar(a, "nm", MEMX, ["second_start", "mem_in"])
            for j in (0, 1):
                a.e.wait_ge(*a.at(f"s{j}_mm"))
                for b in range(2):
                    k = 4 * j + 2 * b
                    a.e.activation(MK[:, k:k + 2, :].rearrange("p k t -> p (k t)"),
                                   PS[:, 2 * (j % 2) + b, :], ACT.Copy).then_inc(*a.count(f"s{j}_ev" if b else None))
            for j in (2, 3):
                a.e.wait_ge(*a.at(f"s{j}_mm"))
                for t in range(TT):
                    a.e.activation(MV[:, t, (j - 2) * 512:(j - 1) * 512], PS[:, 2 * (j % 2) + t, :], ACT.Copy) \
                        .then_inc(*a.count(f"s{j}_ev" if t else None))
            norm_scalar(a, "nx", X, ["nm_done"])
            a.e.wait_ge(*a.at("s4_mm"))
            a.e.activation(ABC[:, 0:2, :].rearrange("p c t -> p (c t)"), PS[:, 0, :], ACT.Copy) \
                .then_inc(*a.count("ax_ev"))
            a.e.wait_ge(*a.at("s5_mm"))
            a.e.activation(ABC[:, 2:4, :].rearrange("p c t -> p (c t)"), PS[:, 2, :], ACT.Copy) \
                .then_inc(*a.count("s5_ev"))
            for j in range(6, 16):
                to, c0, func = ((QKVG, 0, ACT.Copy) if j == 6 else (QKVG, 512, ACT.Copy) if j == 7 else
                                (QKVG, 1024, ACT.Silu) if j == 8 else (ZG, 0, ACT.Gelu_apprx_tanh) if j == 9 else
                                (GT, (j - 10) * 512, ACT.Sigmoid))
                a.e.wait_ge(*a.at(f"s{j}_mm"))
                for t in range(TT):
                    a.e.activation(to[:, t, c0:c0 + 512], PS[:, 2 * (j % 2) + t, :], func) \
                        .then_inc(*a.count(f"s{j}_ev" if t else None))
            a.e.wait_ge(*a.at("ln_var"))
            a.e.activation(STAT[:, 100:102], STAT[:, 98:100], ACT.Sqrt).then_inc(*a.count("ln_sd"))
            a.e.wait_ge(*a.at("gn_var"))
            a.e.activation(STAT[:, 80:88], STAT[:, 72:80], ACT.Sqrt).then_inc(*a.count("gn_sd"))
            norm_scalar(a, "nq", X, ["s20_ev"])
            for j in (21, 22):
                a.e.wait_ge(*a.at(f"s{j}_mm"))
                for b in range(2):
                    k = 4 * (j - 21) + 2 * b
                    a.e.activation(QX[:, k:k + 2, :].rearrange("p k t -> p (k t)"),
                                   PS[:, 2 * (j % 2) + b, :], ACT.Copy).then_inc(*a.count(f"s{j}_ev" if b else None))
            a.e.wait_ge(*a.at("xa_max"))
            for t in range(TT):
                for h in range(4):
                    c = 4 * t + h
                    a.e.activation(SX[:, t, h, :], PS[:, 4 + 2 * t + h // 2, (h % 2) * T:(h % 2 + 1) * T],
                                   ACT.Exp, bias=STAT[:, 8 + c:9 + c], scale=1.0 / 16,
                                   accum_out=STAT[:, 16 + c:17 + c]).then_inc(*a.count("xa_exp" if c == 7 else None))
            for h in range(4):
                a.e.wait_ge(*a.at(f"ptx{h}"))
                a.e.activation(PTX[:, h, :, :].rearrange("p k t -> p (k t)"), PS[:, h, :], ACT.Copy) \
                    .then_inc(*a.count(f"ptx{h}_ev"))
            norm_scalar(a, "nf", X, ["s24_ev"])
            for n in range(D_FF // 256):
                j = 25 + n
                a.e.wait_ge(*a.at(f"s{j}_mm"))
                if n >= 2:
                    a.e.wait_ge(*a.at(f"s{j - 2}_ev"))
                a.e.activation(SILU[:, j % 2, :], PS[:, 2 * (j % 2), :], ACT.Silu).then_inc(*a.count(f"ff_silu{n}"))

        def second_tensor(pe, l):
            turn_tensor(pe, "nm", SCR, KD, ["nm_xn0", "nm_xn1"])
            pe.e.wait_ge(*pe.at("nm_done"))
            B = SECOND_BLOCKS
            for j in range(4):
                product(pe, "s", B, j, "channels" if j < 2 else "tokens", MT, 2 * (j % 2),
                        [f"s{j - 2}_ev"] if j >= 2 else [])
            turn_tensor(pe, "nx", SCR, KD, ["nx_xn0", "nx_xn1"])
            pe.e.wait_ge(*pe.at("nx_done"))
            for j in range(4, 16):
                product(pe, "s", B, j, "channels" if j < 6 else "tokens", HT, 2 * (j % 2), [f"s{j - 2}_ev"])
            turn_tensor(pe, "rq", QKR, 4, ["rot", "rot"])
            pe.e.wait_ge(*pe.at("rq_done"))
            for h in range(RET_HEADS):
                r = 64 * (h % 2)
                q, k = QKT2[r:r + 64, h // 2, :], QKT2[r:r + 64, 2 + h // 2, :]
                pe.e.matmul(PS[:, 4 + h, 0:T], k[:, 0:P], q, start=True, stop=True)
                m = pe.e.matmul(PS[:, 4 + h, T:T + P], k[:, P:T], q[:, P:T], start=True, stop=True)
            m.then_inc(*pe.count("ret_scores"))
            pe.e.wait_ge(*pe.at("ret_dec"))
            for h in range(RET_HEADS):
                o = slice(h * RET_V, (h + 1) * RET_V)
                v = [QKVG[:, t, 512 + h * RET_V:512 + (h + 1) * RET_V] for t in range(TT)]
                pe.e.matmul(PS[:, 4, o], DM[:, h, 0:P], v[0], start=True, stop=True)
                pe.e.matmul(PS[:, 5, o], DM[:, h, P:T], v[0], start=True, stop=False)
                m = pe.e.matmul(PS[:, 5, o], DM[:, h, T:T + P], v[1], start=False, stop=True)
            m.then_inc(*pe.count("ret_out"))
            pe.e.wait_ge(*pe.at("sg_norm"))
            for t in range(TT):
                for g in range(4):
                    m = pe.e.matmul(PS[:, 6, t * 256 + g * 64:t * 256 + (g + 1) * 64], WSM[:, g, :],
                                    VN[:, t, g * 64:(g + 1) * 64], start=True, stop=True)
            m.then_inc(*pe.count("sg_mm"))
            turn_tensor(pe, "rr", R, 4, ["ret_norm", "ret_norm"], ["sg_out"])
            turn_tensor(pe, "yc", YC, 2, ["sg_out", "sg_out"], ["rr_done"])
            product(pe, "s", B, 16, "tokens", YA, 0, ["conv_out", "s14_ev", "s15_ev"])
            product(pe, "s", B, 17, "tokens", RT, 4, ["yc_done"])
            product(pe, "s", B, 18, "tokens", YCT, 0, ["s16_ev"])
            turn_tensor(pe, "mg", MER, KD, ["merged", "merged"])
            pe.e.wait_ge(*pe.at("mg_done"))
            for j in (19, 20):
                product(pe, "s", B, j, "tokens", HT, 2 * (j % 2), [f"s{18}_ev"])
            turn_tensor(pe, "nq", SCR, KD, ["nq_xn0", "nq_xn1"])
            pe.e.wait_ge(*pe.at("nq_done"))
            for j in (21, 22):
                product(pe, "s", B, j, "channels", HT, 2 * (j % 2), [f"s{j - 2}_ev"])
            pe.e.wait_ge(*pe.at("s21_ev"))
            pe.e.wait_ge(*pe.at("s22_ev"))
            for t in range(TT):
                for h in range(4):
                    for c in range(2):
                        m = pe.e.matmul(PS[:, 4 + 2 * t + h // 2, (h % 2) * T:(h % 2 + 1) * T],
                                        QX[:, 2 * h + c, t * P:(t + 1) * P], MK[:, 2 * h + c, :], start=c == 0,
                                        stop=c == 1)
            m.then_inc(*pe.count("xa_scores"))
            pe.e.wait_ge(*pe.at("xa_probs"))
            for h in range(4):
                for k in range(TT):
                    for t in range(TT):
                        m = pe.e.transpose(PS[:, h, k * T + t * P:k * T + (t + 1) * P],
                                           SX[:, t, h, k * P:(k + 1) * P], IDENT)
                m.then_inc(*pe.count(f"ptx{h}"))
            for h in range(4):
                pe.e.wait_ge(*pe.at(f"ptx{h}_ev"))
                for c in range(2):
                    for k in range(TT):
                        m = pe.e.matmul(PS[:, 4 + h, c * T:(c + 1) * T],
                                        MV[:, k, h * 256 + c * P:h * 256 + (c + 1) * P], PTX[:, h, k, :],
                                        start=k == 0, stop=k == TT - 1)
                m.then_inc(*pe.count(f"xa_out{h}"))
            pe.e.wait_ge(*pe.at("xa_done"))
            for j in (23, 24):
                product(pe, "s", B, j, "tokens", HT, 2 * (j % 2))
            turn_tensor(pe, "nf", SCR, KD, ["nf_xn0", "nf_xn1"])
            pe.e.wait_ge(*pe.at("nf_done"))
            for n in range(D_FF // 256):
                j = 25 + n
                pe.e.wait_ge(*pe.at(f"s{j}_in"))
                pe.e.wait_ge(*pe.at(f"s{j - 2}_ev"))
                W = RING[:, j % 2, :].rearrange("p (k w) -> p k w", w=256)
                for half in range(2):
                    for c in range(2):
                        for kc in range(KD):
                            m = pe.e.matmul(PS[:, 2 * (j % 2) + half, c * T:(c + 1) * T],
                                            W[:, half * KD + kc, c * P:(c + 1) * P], HT[:, kc, :], start=kc == 0,
                                            stop=kc == KD - 1)
                m.then_inc(*pe.count(f"s{j}_mm"))
            for n in range(-(-KF // 4)):
                j = 36 + n
                product(pe, "s", B, j, "tokens", FF[:, 4 * n:, :], 4, ["s35_ev"], n == 0, 4 * n + 4 >= KF)

        def second_vector(v, l):
            cos = PHASE[:, 4 * (T + P):4 * (T + P) + 64].rearrange("p (t n) -> p t n", t=TT)
            sin = PHASE[:, 4 * (T + P) + 64:4 * (T + P) + 128].rearrange("p (t n) -> p t n", t=TT)
            tri = PHASE[:, 4 * (T + P) + 128:4 * (T + P) + 128 + P]
            v.e.wait_ge(*v.mine())
            v.e.memset(Z3[:, :, 0:2], 0.0).then_inc(*v.count("second_start"))
            norm_vector(v, "nm", MEMX)
            v.e.wait_ge(*v.at("second_params_in"))
            turn_vector(v, "nm", MT, KD, spar("norm_mem"))
            norm_vector(v, "nx", X)
            turn_vector(v, "nx", HT, KD, spar("norm_mix"))
            v.e.wait_ge(*v.at("ax_ev"))
            v.e.wait_ge(*v.at("s4_mm"))
            v.e.tensor_tensor(Z3[:, :, 2:T + 2], PS[:, 1, :].rearrange("p (c t) -> p c t", c=2),
                              ABC[:, 0:2, :], ALU.mult).then_inc(*v.count("s4_ev"))
            v.e.wait_ge(*v.mine())
            for k in range(3):
                for c in range(2):
                    w = spar("conv_w", 2 * k + c, 2 * k + c + 1)
                    if k == 0:
                        v.e.tensor_scalar(YA[:, c, :], Z3[:, c, 0:T], w, None, ALU.mult).then_inc(*v.count())
                    else:
                        v.e.wait_ge(*v.mine(1))
                        v.e.scalar_tensor_tensor(YA[:, c, :], Z3[:, c, k:k + T], w, YA[:, c, :], ALU.mult,
                                                 ALU.add).then_inc(*v.count())
            v.e.wait_ge(*v.mine())
            v.e.wait_ge(*v.at("s5_ev"))
            v.e.tensor_tensor(YA, YA, ABC[:, 2:4, :], ALU.mult).then_inc(*v.count("conv_out"))
            v.e.tensor_tensor(WSM, spar("sg_w").rearrange("p (g n) -> p g n", g=4),
                              tri.unsqueeze(1).broadcast_to([P, 4, P]), ALU.mult).then_inc(*v.count())
            v.e.wait_ge(*v.at("s6_ev"))
            parts = MER.rearrange("p t (m g n) -> p (t m) g n", m=4, n=32)
            C, S = ([w[:, t, :].unsqueeze(1).broadcast_to([P, 8, 32]) for t in range(TT)] for w in (cos, sin))
            for t in range(TT):
                x = QKVG[:, t, 0:512].rearrange("p (g c n) -> p g c n", g=8, c=2)
                for n, (c, w) in enumerate(((0, C), (1, S), (0, S), (1, C))):
                    v.e.tensor_tensor(parts[:, 4 * t + n, :, :], x[:, :, c, :], w[t], ALU.mult).then_inc(*v.count())
            v.e.wait_ge(*v.mine())
            for t in range(TT):
                to = QKR[:, t, :].rearrange("p (g c n) -> p g c n", g=8, c=2)
                for c, op in ((0, ALU.subtract), (1, ALU.add)):
                    v.e.tensor_tensor(to[:, :, c, :], parts[:, 4 * t + 2 * c, :, :],
                                      parts[:, 4 * t + 2 * c + 1, :, :], op) \
                        .then_inc(*v.count("rot" if t and c else None))
            turn_vector(v, "rq", QKT2, 4, None)
            v.e.wait_ge(*v.at("ret_scores"))
            for h in range(RET_HEADS):
                v.e.tensor_tensor(DM[:, h, :], PS[:, 4 + h, 0:T + P],
                                  PHASE[:, h * (T + P):(h + 1) * (T + P)], ALU.mult) \
                    .then_inc(*v.count("ret_dec" if h == 3 else None))

            def center(tag, src, dst, n, at):
                for i in range(n):
                    v.e.bn_stats(MER[:, 0, 512 + 8 * i:518 + 8 * i], src(i)).then_inc(*v.count())
                v.e.wait_ge(*v.mine())
                v.e.tensor_copy(LB[:, 14:15], COMMON[:, 0:1]).then_inc(*v.count())
                for i in range(n):
                    v.e.bn_aggr(MER[:, 0, 640 + 2 * i:642 + 2 * i], MER[:, 0, 512 + 8 * i:518 + 8 * i]) \
                        .then_inc(*v.count())
                v.e.wait_ge(*v.mine())
                v.e.tensor_scalar(STAT[:, at:at + n],
                                  MER[:, 0, 640:640 + 2 * n].rearrange("p (i c) -> p i c", c=2)[:, :, 1],
                                  EPS, None, ALU.add).then_inc(*v.count(f"{tag}_var"))
                v.e.wait_ge(*v.at(f"{tag}_sd"))
                sd = at + (n if n > 2 else 2)
                v.e.reciprocal(STAT[:, sd:sd + n], STAT[:, sd:sd + n]).then_inc(*v.count())
                v.e.wait_ge(*v.mine())
                for i in range(n):
                    v.e.tensor_scalar(dst(i), src(i), MER[:, 0, 640 + 2 * i:641 + 2 * i],
                                      STAT[:, sd + i:sd + i + 1], ALU.subtract, ALU.mult).then_inc(*v.count())
                v.e.wait_ge(*v.mine())

            v.e.wait_ge(*v.at("s9_ev"))
            center("ln", lambda t: ZG[:, t, 256:512], lambda t: VN[:, t, :], TT, 98)
            v.e.tensor_tensor(VN, VN, spar("sg_ln").unsqueeze(1).broadcast_to([P, TT, 256]), ALU.mult) \
                .then_inc(*v.count("sg_norm"))
            v.e.wait_ge(*v.at("ret_out"))
            v.e.wait_ge(*v.mine())
            center("gn", lambda i: PS[:, 4 + i // 4, (i % 4) * P:(i % 4 + 1) * P],
                   lambda i: R[:, i // 4, (i % 4) * P:(i % 4 + 1) * P], 8, 72)
            v.e.wait_ge(*v.at("s8_ev"))
            v.e.tensor_tensor(R, R, QKVG[:, :, 1024:1536], ALU.mult).then_inc(*v.count("ret_norm"))
            v.e.wait_ge(*v.at("sg_mm"))
            for g in range(4):
                o = slice(g * 64, (g + 1) * 64)
                v.e.scalar_tensor_tensor(YC[:, :, o], PS[:, 6, :].rearrange("p (t n) -> p t n", t=TT)[:, :, o],
                                         spar("sg_b", g, g + 1), ZG[:, :, o], ALU.add, ALU.mult) \
                    .then_inc(*v.count("sg_out" if g == 3 else None))
            turn_vector(v, "rr", RT, 4, spar("ret_gn"))
            turn_vector(v, "yc", YCT, 2, None)
            v.e.wait_ge(*v.at("s15_ev"))
            for n, (j, bank) in enumerate(((16, 0), (17, 4), (18, 0))):
                v.e.wait_ge(*v.at(f"s{j}_mm"))
                v.e.wait_ge(*v.mine())
                for t in range(TT):
                    for half in range(2):
                        o = slice(half * 512, (half + 1) * 512)
                        to = (MER if n == 0 else SCR)[:, t, o]
                        v.e.tensor_tensor(to, PS[:, bank + 2 * t + half, :],
                                          GT[:, t, n * D + half * 512:n * D + (half + 1) * 512], ALU.mult) \
                            .then_inc(*v.count(f"s{j}_ev" if t and half else None))
                if n:
                    v.e.wait_ge(*v.mine())
                    v.e.tensor_tensor(MER, MER, SCR, ALU.add).then_inc(*v.count("merged" if n == 2 else None))
            turn_vector(v, "mg", HT, KD, None)
            add_to_x(v, "s", SECOND_BLOCKS, (19, 20))
            v.e.wait_ge(*v.mine())
            norm_vector(v, "nq", X)
            turn_vector(v, "nq", HT, KD, spar("norm_xa"))
            v.e.wait_ge(*v.at("xa_scores"))
            for b in range(4):
                v.e.tensor_reduce(STAT[:, 2 * b:2 * b + 2], PS[:, 4 + b, :].rearrange("p (h m) -> p h m", h=2),
                                  AX.X, ALU.max, negate=True).then_inc(*v.count())
            v.e.wait_ge(*v.mine())
            v.e.tensor_scalar(STAT[:, 8:16], STAT[:, 0:8], 1.0 / 16, None, ALU.mult).then_inc(*v.count("xa_max"))
            v.e.wait_ge(*v.at("xa_exp"))
            v.e.reciprocal(STAT[:, 24:32], STAT[:, 16:24]).then_inc(*v.count())
            v.e.wait_ge(*v.mine())
            flat = SX.rearrange("p t h m -> p (t h) m")
            v.e.tensor_tensor(flat, flat, STAT[:, 24:32].unsqueeze(2).broadcast_to([P, 8, T]), ALU.mult) \
                .then_inc(*v.count("xa_probs"))
            for h in range(4):
                v.e.wait_ge(*v.at(f"xa_out{h}"))
                v.e.tensor_copy(HT[:, 2 * h:2 * h + 2, :].rearrange("p k t -> p (k t)"), PS[:, 4 + h, :]) \
                    .then_inc(*v.count("xa_done" if h == 3 else None))
            add_to_x(v, "s", SECOND_BLOCKS, (23, 24))
            v.e.wait_ge(*v.mine())
            norm_vector(v, "nf", X)
            turn_vector(v, "nf", HT, KD, spar("norm_ffn"))
            for n in range(D_FF // 256):
                j = 25 + n
                v.e.wait_ge(*v.at(f"ff_silu{n}"))
                v.e.tensor_tensor(FF[:, 2 * n:2 * n + 2, :].rearrange("p k t -> p (k t)"),
                                  PS[:, 2 * (j % 2) + 1, :], SILU[:, j % 2, :], ALU.mult) \
                    .then_inc(*v.count(f"s{j}_ev"))
            v.e.wait_ge(*v.at("s41_mm"))
            for t in range(TT):
                for half in range(2):
                    x = X[:, t, half * 512:(half + 1) * 512]
                    v.e.tensor_tensor(x, PS[:, 4 + 2 * t + half, :], x, ALU.add) \
                        .then_inc(*v.count("second_end" if t and half else None))

        @block.sync
        def _(eng):
            sp = Program(eng, "sync", steps)
            eng.dma_start(X[:, :, :], dram["x"].rearrange("b (t p) d -> p (b t) d", p=P)) \
                .then_inc(*sp.count(None, "dma_start"))
            eng.dma_start(COMMON[:, :], dram["common"]).then_inc(*sp.count(None, "dma_start"))
            eng.dma_start(PHASE[:, 0:N_HYBRID_CONST], dram["hybrid_const"]).then_inc(*sp.count(None, "dma_start"))
            eng.dma_start(STAT[0:BUCKETS, 0:AT_HEADS], dram["rel_bias"]).then_inc(*sp.count(None, "dma_start"))
            eng.dma_start(LB[:, 0:4], dram["lower_bounds"]).then_inc(*sp.count("start_in", "dma_start"))
            with sp.loop("hybrid", DEPTH) as l:
                sp.e.wait_ge(*sp.at("hybrid_start"))
                for j in range(4):
                    weight_block(sp, HYBRID_BLOCKS, "h", l, j)
                sp.e.wait_ge(*sp.at("hi_out"))
                for g in range(SCANS):
                    if g >= 2:
                        sp.e.wait_ge(*sp.at(f"kv{g - 2}"))
                    row = g // (SCANS // 2) * 2 * HEAD + g % (SCANS // 2) * VGROUP
                    for h in range(2):
                        src = bass.AP(tensor=hi_rows.tensor, offset=(row + h * HEAD) * T,
                                      ap=[[0, HEAD], [T, VGROUP], [1, T]])
                        sp.e.dma_start(VB[h * HEAD:(h + 1) * HEAD, g % 2, :, :], src) \
                            .then_inc(*sp.count(f"hi_in{g}" if h else None, f"dma_hi_in{g % 2}"))
                    if g in BLOCK_AT:
                        weight_block(sp, HYBRID_BLOCKS, "h", l, BLOCK_AT[g])
                for j in range(10, 12):
                    weight_block(sp, HYBRID_BLOCKS, "h", l, j)
                n = len(HYBRID_BLOCKS)
                for b in range(2):
                    sp.e.wait_ge(*sp.at(f"h{n - 2 + b}_mm"))
                    peer_block(sp, "down", b, b, l)
                    peer_block(sp, "up", b, b, l)
                for which, loops in (("down", ("lead", "gate")), ("up", ("outa", "outb"))):
                    for k, name in enumerate(loops):
                        with sp.loop(name, BLOCKS // 8) as i:
                            for b in range(2):
                                sp.e.wait_ge(*sp.at(f"{name}_mm{b}"))
                                peer_block(sp, which, i * 2 + (16 * k + 2 + b), b, l, f"{name}_in{b}")
                with sp.loop("peer", BLOCKS // 4 - 1) as i:
                    for b in range(2):
                        sp.e.wait_ge(*sp.at(f"down_lo{b}", back=1))
                        peer_block(sp, "down", i * 2 + (BLOCKS // 2 + 2 + b), b, l, f"down{b}")
                    sp.e.wait_ge(*sp.at("up_lo0", back=1))
                    peer_block(sp, "up", i * 2 + (BLOCKS // 2 + 2), 0, l, "up0")
                    sp.e.wait_ge(*sp.at("up_lo1"))
                    peer_block(sp, "up", i * 2 + (BLOCKS // 2 + 3), 1, l, "up1")
            sp.e.wait_ge(*sp.at("hybrid_end"))
            eng.dma_start(PHASE[:, 0:N_SECOND_CONST], dram["second_const"]) \
                .then_inc(*sp.count("second_const_in", "dma_const"))
            second_loads(sp)
            sp.e.wait_ge(*sp.at("result"))
            eng.dma_start(out.rearrange("b (t p) d -> p (b t) d", p=P), SCR) \
                .then_inc(*sp.count("out_done", "dma_out"))
            sp.e.wait_ge(*sp.at("out_done"))

        @block.gpsimd
        def _(eng):
            p = Program(eng, "pool", steps)
            p.e.wait_ge(*p.at("start_in"))
            p.e.tensor_tensor(LB[:, 15:16], COMMON[:, 0:1], COMMON[:, 0:1], ALU.add).then_inc(*p.count())
            p.e.wait_ge(*p.at("bias_sb"))
            eng.dma_start(bias_rows, SCR[0:AT_HEADS, 0, 0:REL]).then_inc(*p.count("bias_out", "dma_bias_out"))
            hybrid_pool(p)
            second_pool(p)

        @block.scalar
        def _(eng):
            a = Program(eng, "scalar", steps)
            a.e.wait_ge(*a.at("lower_off"))
            eng.activation(LB[:, 6:10], LB[:, 6:10], ACT.Exp).then_inc(*a.count("lower_exp"))
            a.e.wait_ge(*a.at("bias_mm"))
            eng.activation(SCR[0:AT_HEADS, 0, 0:REL], PS[0:AT_HEADS, 6, 0:REL], ACT.Copy) \
                .then_inc(*a.count("bias_sb"))
            a.e.wait_ge(*a.at("bias_out"))
            with a.loop("hybrid", DEPTH) as l:
                hybrid_scalar(a, l)
            a.e.wait_ge(*a.at("hybrid_end"))
            with a.loop("second", DEPTH) as l:
                second_scalar(a, l)
            norm_scalar(a, "end", X, ["second_end"])

        @block.tensor
        def _(eng):
            pe = Program(eng, "tensor", steps)
            pe.e.wait_ge(*pe.at("start_in"))
            eng.matmul(PS[0:AT_HEADS, 6, 0:REL], STAT[0:BUCKETS, 0:AT_HEADS],
                       PHASE[0:BUCKETS, 2 * (T + P):2 * (T + P) + REL], start=True, stop=True) \
                .then_inc(*pe.count("bias_mm"))
            with pe.loop("hybrid", DEPTH) as l:
                hybrid_tensor(pe, l)
            pe.e.wait_ge(*pe.at("second_const_in"))
            with pe.loop("second", DEPTH) as l:
                second_tensor(pe, l)

        @block.vector
        def _(eng):
            v = Program(eng, "vector", steps)
            v.e.wait_ge(*v.at("start_in"))
            raw = LB[:, 0:4].rearrange("p (l c) -> p l c", l=DEPTH)
            off = LB[:, 6:10].rearrange("p (l c) -> p l c", l=DEPTH)
            eng.tensor_tensor(LB[:, 4:6], LB[:, 0:2], LB[:, 2:4], ALU.max).then_inc(*v.count())
            v.e.wait_ge(*v.mine())
            eng.tensor_tensor(off, raw, LB[:, 4:6].unsqueeze(1).broadcast_to([P, DEPTH, 2]), ALU.subtract) \
                .then_inc(*v.count("lower_off"))
            v.e.wait_ge(*v.at("lower_exp"))
            eng.tensor_tensor(LB[:, 4:6], LB[:, 6:8], LB[:, 8:10], ALU.add).then_inc(*v.count())
            v.e.wait_ge(*v.mine())
            eng.reciprocal(LB[:, 4:6], LB[:, 4:6]).then_inc(*v.count())
            v.e.wait_ge(*v.mine())
            eng.tensor_tensor(off, off, LB[:, 4:6].unsqueeze(1).broadcast_to([P, DEPTH, 2]), ALU.mult) \
                .then_inc(*v.count())
            v.e.wait_ge(*v.mine())
            eng.tensor_tensor(LB[:, 10:12], LB[:, 6:8], LB[:, 6:8], ALU.subtract).then_inc(*v.count())
            eng.tensor_tensor(LB[:, 12:14], LB[:, 6:8], LB[:, 8:10], ALU.add).then_inc(*v.count())
            v.e.wait_ge(*v.mine())
            eng.tensor_tensor(LB[:, 12:14], LB[:, 12:14], LB[:, 6:8], ALU.subtract).then_inc(*v.count())
            v.e.wait_ge(*v.at("bias_mm"))
            with v.loop("hybrid", DEPTH) as l:
                hybrid_vector(v, l)
            v.e.wait_ge(*v.at("second_const_in"))
            v.e.wait_ge(*v.at("mem_in"))
            with v.loop("second", DEPTH) as l:
                second_vector(v, l)
            norm_vector(v, "end", X)
            v.e.wait_ge(*v.mine())
            v.e.wait_ge(*v.at("final_in"))
            eng.tensor_tensor(SCR, SCR, FINAL.unsqueeze(1).broadcast_to([P, TT, D]), ALU.mult) \
                .then_inc(*v.count("result"))


def columns(rows):
    return np.ascontiguousarray(rows.reshape(DEPTH, -1, P).transpose(0, 2, 1))


def layouts(i):
    i = {k: np.asarray(v) for k, v in i.items()}
    a = {k: i[k] for k in ("x", "w_in", "w_out", "peer_w_query", "peer_up", "rel_bias", "mem_2", "w_in_2", "w_a_out_2",
                           "w_b_out_2", "w_c_out_2", "w_o_2", "xa_q_2", "xa_k_2", "xa_v_2", "xa_o_2", "w1_2", "w3_2",
                           "w2_2", "final_norm_2")}
    a["peer_down"] = i["peer_down"].reshape(DEPTH, NKEYS, NKEYS, KD, P).transpose(0, 2, 4, 3, 1)
    a["sub_keys"] = i["peer_sub_keys"].transpose(0, 1, 3, 2).reshape(DEPTH, P, NKEYS)
    a["lower_bounds"] = i["hgrn_lower_bounds"].reshape(DEPTH * 2, P).T

    def rows(name, n):
        out = np.zeros((DEPTH, P, 1), np.float32)
        out[:, 0:n, 0] = i[name]
        return out

    parts = {
        "attn_norm": columns(i["attn_norm_w"]), "ffn_norm": columns(i["ffn_norm_w"]),
        "mix_norm": columns(np.concatenate([np.tile(i["hgrn_norm_w"], (1, HG_HEADS)),
                                            np.ones((DEPTH, AT_W), np.float32), i["ssm_norm_w"]], axis=1)),
        "q_norm": columns(np.tile(i["q_norm_w"], (1, 2))), "k_norm": columns(np.tile(i["k_norm_w"], (1, 2))),
        "conv_w": columns(i["ssm_conv_w"].reshape(DEPTH, -1)), "conv_b": columns(i["ssm_conv_b"]),
        "dt_bias": rows("ssm_dt_bias", SS_HEADS), "a_log": rows("ssm_a_log", SS_HEADS),
        "d_skip": np.repeat(i["ssm_d"][:, None, :], P, axis=1),
    }
    a["hybrid_par"] = np.concatenate([parts[k] for k in HYBRID_PARAMS], axis=2)
    parts = {
        "norm_mix": columns(i["norm_mix_2"]), "norm_xa": columns(i["norm_xa_2"]), "norm_mem": columns(i["norm_mem_2"]),
        "norm_ffn": columns(i["norm_ffn_2"]), "ret_gn": columns(i["ret_gn_2"]),
        "conv_w": columns(i["conv_w_2"].reshape(DEPTH, -1)), "sg_b": i["sg_b_2"].transpose(0, 2, 1),
        "sg_ln": np.repeat(i["sg_ln_2"][:, None, :], P, axis=1),
        "sg_w": i["sg_w_2"].transpose(0, 3, 1, 2).reshape(DEPTH, P, 512),
    }
    a["second_par"] = np.concatenate([parts[k] for k in SECOND_PARAMS], axis=2)
    a.update(constants())
    return {k: np.ascontiguousarray(v) for k, v in a.items()}


def kernel(**inputs):
    import concourse.bacc as bacc
    from concourse.bass_utils import run_bass_kernel_spmd as run

    arrays = layouts(inputs)

    def program(steps):
        nc = bacc.Bacc("TRN2", target_bir_lowering=False, num_devices=1)
        dram = {k: nc.dram_tensor(f"in_{k}", v.shape, F32, kind="ExternalInput").ap() for k, v in arrays.items()}
        out = nc.dram_tensor("out_x", (1, T, D), F32, kind="ExternalOutput").ap()
        build(nc, dram, out, steps)
        return nc

    counts = Steps()
    program(counts)
    nc = program(Steps(counts))
    r = run(nc, [{f"in_{k}": v for k, v in arrays.items()}], core_ids=[0])
    return r.results[0]["out_x"]
```
